# Optimizing a Trainium2 kernel written in Bass

```python
import jax, jax.numpy as jnp
from jax import lax
import numpy as np

D_MODEL = 1024
BATCH = 1
SEQ = 512
DEPTH = 2

CONV_WIDTH = 3
CONV_CHANNELS = D_MODEL // 2
HGRN_HEAD_DIM = 128
HGRN_HEADS = (D_MODEL // 2) // HGRN_HEAD_DIM
HGRN_WIDTH = HGRN_HEADS * HGRN_HEAD_DIM
HGRN_CHUNK = 64
ATTN_HEAD_DIM = 64
ATTN_HEADS = D_MODEL // ATTN_HEAD_DIM
DILATED_BRANCHES = ((128, 1), (512, 4), (2048, 16))
ATTN_BLOCK = 128
ROPE_THETA = 10000.0
D_FF = -(-8 * D_MODEL // (3 * 256)) * 256
RMS_EPS = 1e-6
N_EVEN = (DEPTH + 1) // 2
N_ODD = DEPTH // 2
REC_IN_WIDTH = 3 * CONV_CHANNELS + 4 * HGRN_WIDTH

kernel_name = "hybrid_conv_hgrn2_dilated_attn_block"

def rmsnorm(x, g):
    xf = x.astype(jnp.float32)
    y = xf * lax.rsqrt(jnp.mean(xf * xf, axis=-1, keepdims=True) + RMS_EPS)
    return (y * g.astype(jnp.float32)).astype(x.dtype)

def short_conv_mixer(b_gate, c_gate, v, conv_w):
    u = c_gate * v
    S = u.shape[1]
    up = jnp.pad(u, ((0, 0), (CONV_WIDTH - 1, 0), (0, 0)))
    y = conv_w[0] * up[:, 0:S]
    for j in range(1, CONV_WIDTH):
        y = y + conv_w[j] * up[:, j:j + S]
    return b_gate * y

def hgrn2_mixer(q, f_logit, i_in, g, lb, norm_g):
    B, S, _ = q.shape
    H, Dh, C = HGRN_HEADS, HGRN_HEAD_DIM, HGRN_CHUNK
    nc = S // C

    def heads(t):
        return t.reshape(B, S, H, Dh).transpose(0, 2, 1, 3).astype(jnp.float32)

    z = heads(f_logit)
    lbh = lb.reshape(H, 1, Dh)
    log_f = jnp.logaddexp(jnp.log(lbh), jnp.log1p(-lbh) + jax.nn.log_sigmoid(z))
    k = (1.0 - lbh) * jax.nn.sigmoid(-z)
    qh = heads(q)
    vh = heads(jax.nn.silu(i_in))

    def chunks(t):
        return t.reshape(B, H, nc, C, Dh).transpose(2, 0, 1, 3, 4)

    causal = jnp.tril(jnp.ones((C, C), dtype=bool))

    def step(state, inp):
        qc, kc, vc, lfc = inp
        G = jnp.cumsum(lfc, axis=2)
        o_inter = jnp.einsum('bhtk,bhkv->bhtv', qc * jnp.exp(G), state)
        rel = G[:, :, :, None, :] - G[:, :, None, :, :]
        decay = jnp.exp(jnp.where(causal[:, :, None], rel, -jnp.inf))
        scores = jnp.einsum('bhtk,bhtsk,bhsk->bhts', qc, decay, kc)
        o = o_inter + jnp.einsum('bhts,bhsv->bhtv', scores, vc)
        G_last = G[:, :, -1:, :]
        new_state = (jnp.exp(G_last[:, :, 0, :])[..., None] * state
                     + jnp.einsum('bhsk,bhsv->bhkv', kc * jnp.exp(G_last - G), vc))
        return new_state, o

    state0 = jnp.zeros((B, H, Dh, Dh), jnp.float32)
    _, o = lax.scan(step, state0, (chunks(qh), chunks(k), chunks(vh), chunks(log_f)))
    o = o.transpose(1, 2, 0, 3, 4).reshape(B, H, S, Dh)
    o = rmsnorm(o, norm_g)
    o = o.transpose(0, 2, 1, 3).reshape(B, S, HGRN_WIDTH)
    return (o * jax.nn.silu(g.astype(jnp.float32))).astype(q.dtype)

def rope(t, positions):
    hd = t.shape[-1]
    half = hd // 2
    freqs = ROPE_THETA ** (-jnp.arange(half, dtype=jnp.float32) / half)
    ang = positions.astype(jnp.float32)[:, None] * freqs[None, :]
    cos, sin = jnp.cos(ang), jnp.sin(ang)
    tf = t.astype(jnp.float32)
    t1, t2 = tf[..., :half], tf[..., half:]
    return jnp.concatenate([t1 * cos - t2 * sin, t1 * sin + t2 * cos], axis=-1)

def dilated_branch(q, k, v, dilation, span):
    B, H, S, hd = q.shape
    L = S // dilation
    nb = -(-L // ATTN_BLOCK)
    Lp = nb * ATTN_BLOCK

    def strided(t):
        t = t.reshape(B, H, L, dilation, hd).transpose(0, 1, 3, 2, 4)
        t = jnp.pad(t, ((0, 0), (0, 0), (0, 0), (0, Lp - L), (0, 0)))
        return t.reshape(B, H, dilation, nb, ATTN_BLOCK, hd)

    def with_prev(t):
        prev = jnp.pad(t, ((0, 0), (0, 0), (0, 0), (1, 0), (0, 0), (0, 0)))[:, :, :, :-1]
        return jnp.concatenate([prev, t], axis=4)

    qb = strided(q)
    kk = with_prev(strided(k))
    vv = with_prev(strided(v))
    s = jnp.einsum('bhrnqd,bhrnkd->bhrnqk', qb, kk).astype(jnp.float32)
    qi = jnp.arange(ATTN_BLOCK)[:, None]
    kj = jnp.arange(2 * ATTN_BLOCK)[None, :]
    rel = ATTN_BLOCK + qi - kj
    band = (rel >= 0) & (rel <= span)
    has_prev = (jnp.arange(nb)[:, None, None] > 0) | (kj >= ATTN_BLOCK)[None]
    mask = band[None] & has_prev
    s = jnp.where(mask, s, -jnp.inf)
    m = jnp.max(s, axis=-1, keepdims=True)
    p = jnp.exp(s - m)
    denom = jnp.sum(p, axis=-1, keepdims=True)
    o = jnp.einsum('bhrnqk,bhrnkd->bhrnqd', (p / denom).astype(vv.dtype), vv)
    lse = (m + jnp.log(denom))[..., 0]
    o = o.reshape(B, H, dilation, Lp, hd)[:, :, :, :L].transpose(0, 1, 3, 2, 4).reshape(B, H, S, hd)
    lse = lse.reshape(B, H, dilation, Lp)[..., :L].transpose(0, 1, 3, 2).reshape(B, H, S)
    return o, lse

def dilated_attention(q, k, v):
    outs, lses = [], []
    for window, dilation in DILATED_BRANCHES:
        o, lse = dilated_branch(q, k, v, dilation, window // dilation)
        outs.append(o.astype(jnp.float32))
        lses.append(lse)
    w = jax.nn.softmax(jnp.stack(lses, axis=0), axis=0)
    return jnp.einsum('nbhs,nbhsd->bhsd', w, jnp.stack(outs, axis=0))

def swiglu(h, w_in, w_out):
    gate, up = jnp.split(h @ w_in, 2, axis=-1)
    return (jax.nn.silu(gate) * up) @ w_out

def setup_inputs(seed: int = 0) -> dict:
    key = jax.random.key(seed)
    ks = jax.random.split(key, 13)
    D = D_MODEL
    f32 = jnp.float32

    def nrm(k, shape, scale):
        return jax.random.normal(k, shape, f32) * scale

    return {
        "x": nrm(ks[0], (BATCH, SEQ, D), 1.0),
        "mix_norm": 1.0 + nrm(ks[1], (DEPTH, D), 0.02),
        "ffn_norm": 1.0 + nrm(ks[2], (DEPTH, D), 0.02),
        "w_in_rec": nrm(ks[3], (N_EVEN, D, REC_IN_WIDTH), D ** -0.5),
        "conv_w": nrm(ks[4], (N_EVEN, CONV_WIDTH, CONV_CHANNELS), CONV_WIDTH ** -0.5),
        "hgrn_lb": nrm(ks[5], (DEPTH + 1, HGRN_WIDTH), 0.5),
        "hgrn_norm": 1.0 + nrm(ks[6], (N_EVEN, HGRN_HEAD_DIM), 0.02),
        "w_out_rec": nrm(ks[7], (N_EVEN, CONV_CHANNELS + HGRN_WIDTH, D), (CONV_CHANNELS + HGRN_WIDTH) ** -0.5),
        "w_qkv_attn": nrm(ks[8], (N_ODD, D, 3 * ATTN_HEADS * ATTN_HEAD_DIM), D ** -0.5),
        "w_o_attn": nrm(ks[9], (N_ODD, ATTN_HEADS * ATTN_HEAD_DIM, D), (ATTN_HEADS * ATTN_HEAD_DIM) ** -0.5),
        "w_ffn_in": nrm(ks[10], (DEPTH, D, 2 * D_FF), D ** -0.5),
        "w_ffn_out": nrm(ks[11], (DEPTH, D_FF, D), D_FF ** -0.5),
        "final_norm": 1.0 + nrm(ks[12], (D,), 0.02),
    }

def reference(x, mix_norm, ffn_norm, w_in_rec, conv_w, hgrn_lb, hgrn_norm, w_out_rec,
              w_qkv_attn, w_o_attn, w_ffn_in, w_ffn_out, final_norm):
    B, S, D = x.shape
    positions = jnp.arange(S, dtype=jnp.int32)
    lb_cum = jnp.cumsum(jax.nn.softmax(hgrn_lb.astype(jnp.float32), axis=0), axis=0)
    splits = [CONV_CHANNELS, 2 * CONV_CHANNELS, 3 * CONV_CHANNELS,
              3 * CONV_CHANNELS + HGRN_WIDTH, 3 * CONV_CHANNELS + 2 * HGRN_WIDTH,
              3 * CONV_CHANNELS + 3 * HGRN_WIDTH]
    for layer in range(DEPTH):
        h = rmsnorm(x, mix_norm[layer])
        if layer % 2 == 0:
            e = layer // 2
            proj = h @ w_in_rec[e]
            b_g, c_g, v_c, q_r, f_r, i_r, g_r = jnp.split(proj, splits, axis=-1)
            a_out = short_conv_mixer(b_g, c_g, v_c, conv_w[e])
            lb = lb_cum[layer + 1] - lb_cum[0]
            b_out = hgrn2_mixer(q_r, f_r, i_r, g_r, lb, hgrn_norm[e])
            mix = jnp.concatenate([a_out.astype(x.dtype), b_out.astype(x.dtype)], axis=-1) @ w_out_rec[e]
        else:
            o_idx = layer // 2
            qkv = (h @ w_qkv_attn[o_idx]).reshape(B, S, 3, ATTN_HEADS, ATTN_HEAD_DIM)
            qkv = qkv.transpose(2, 0, 3, 1, 4)
            q = rope(qkv[0], positions) * (ATTN_HEAD_DIM ** -0.5)
            k = rope(qkv[1], positions)
            v = qkv[2]
            o = dilated_attention(q, k, v)
            o = o.transpose(0, 2, 1, 3).reshape(B, S, ATTN_HEADS * ATTN_HEAD_DIM).astype(x.dtype)
            mix = o @ w_o_attn[o_idx]
        x = x + mix.astype(x.dtype)
        h = rmsnorm(x, ffn_norm[layer])
        x = x + swiglu(h, w_ffn_in[layer], w_ffn_out[layer]).astype(x.dtype)
    return rmsnorm(x, final_norm)


_drawn_inputs = setup_inputs


def setup_inputs(seed=0):
    import zlib

    import numpy as np

    out = dict(_drawn_inputs(seed))
    spreads = {}
    factors = {'ffn_norm': 3.197, 'hgrn_norm': 6.664, 'final_norm': 2.888}
    for name, (base, spread) in spreads.items():
        noise = np.random.default_rng([zlib.crc32(name.encode()), seed]).standard_normal(out[name].shape)
        drawn = base * np.exp(spread * noise) if base else spread * noise
        out[name] = __import__('jax').numpy.asarray(drawn.astype(out[name].dtype))
    for name, factor in factors.items():
        out[name] = (out[name] * factor).astype(out[name].dtype)
    return out
```

```python
from contextlib import ExitStack

import numpy as np

import concourse.bass as bass
from concourse import mybir
from concourse.bass import ds

ALU = mybir.AluOpType
ACT = mybir.ActivationFunctionType
F32 = mybir.dt.float32
F32R = mybir.dt.float32r
U8 = mybir.dt.uint8

P = 128
S = 512
D = 1024
KT = D // P
TT = S // P
HG = 4
HEADS, HD = 16, 64
PAIRS = HEADS // 2
FF = 2816
FT = FF // P
EPS = 1e-6
CONV_W = 3
LEVELS = 7
QSCALE = -(HD ** -0.5)

RING, AHEAD = 4, 3
UNIT = 1024
FO_TILES = (6, 6, 5, 5)
assert sum(FO_TILES) == FT

U_REC = 0
U_WOR = U_REC + 28
U_FI = [U_WOR + 8, 0]
U_FO = [U_FI[0] + 2 * FT, 0]
U_QKV = U_FO[0] + 4 * KT
U_WOA = U_QKV + 24
U_FI[1] = U_WOA + 8
U_FO[1] = U_FI[1] + 2 * FT
U_END = U_FO[1] + 4 * KT
assert all(u % RING == 0 for u in (U_WOR, *U_FI, *U_FO, U_QKV, U_WOA, U_END))

E_REC = 0
E_WOR = E_REC + 24
E_FI = [E_WOR + 16, 0]
E_FO = [E_FI[0] + 2 * FT, 0]
E_QKV = E_FO[0] + KT
E_WOA = E_QKV + 2 * PAIRS
E_FI[1] = E_WOA + KT
E_FO[1] = E_FI[1] + 2 * FT

C_MIX, C_FFN, C_FIN, C_CONV, C_LB, C_HN = 0, 16, 32, 40, 52, 64
N_PARAMS = 65

DIAG_STEP = 12
LEVEL_STEP = [13, 13, 14, 14, 15, 15, 16, 17, 18, 19, 20, 21, 22, 23]
TAIL = 24

class Positions:
    def __init__(self, qk, bias, exp, norm, turn, probs, pv):
        self.qk = qk
        self.bias = [q + bias for q in qk]
        self.exp = [q + exp for q in qk]
        self.norm = [q + norm for q in qk]
        self.turn = [q + turn for q in qk]
        self.probs = [q + probs for q in qk]
        self.values, self.pv, self.out = 3, pv, pv + 1


ATT = Positions([6, 8, 9, 11, 12, 14, 15, 17], 1, 2, 4, 5, 6, 25)
LAST_ATT = Positions([6 + n for n in range(8)], 1, 2, 3, 4, 5, 19)
SWAP, ROPE = 0, 4
WOA_BANK = (0, 3, 1)
WOA_SLOTS = ([(k, n) for k in range(3) for n in range(2)] + [(k, 2) for k in range(3)]
             + [(k, n) for k in range(3, KT) for n in range(3)])


def unit_cols(u):
    for base in U_FO:
        if base <= u < base + 4 * KT:
            return FO_TILES[u % 4] * P
    return UNIT


class Chain:

    def __init__(self, eng, sem):
        self.eng, self.sem, self.n, self.shift = eng, sem, 0, 0

    def mark(self, ins):
        ins.then_inc(self.sem, 1)
        self.n += 1

    def fence(self):
        self.eng.wait_ge(self.sem, self.shift + self.n)

    def loop(self, i, first, per_round):
        self.shift, self.start, self.per = (i - first) * per_round, self.n, per_round

    def done(self, rounds):
        assert self.n - self.start == self.per, (self.n - self.start, self.per)
        self.shift, self.n = 0, self.start + rounds * self.per


def wait(eng, sem, value):
    if not isinstance(value, int) or value > 0:
        eng.wait_ge(sem, value)


def trunk(nc, x_in, params_in, ident_in, bias_in, masks_in, trig_in, w_rec, w_or, w_fi, w_fo, w_qkv,
          w_oa, out):
    with ExitStack() as ctx:
        def sem(name):
            return ctx.enter_context(nc.semaphore(name))

        base, sbuf_end = {"at": -(-nc.sbuf_base // 32) * 32}, nc.sbuf_top
        ctx.enter_context(nc.sbuf_tensor("arena", [P, (nc.sbuf_top - base["at"]) // 4], F32))

        def sb(name, cols, dt=F32, at=None):
            size = cols * (1 if dt == U8 else 4)
            if at is None:
                at = base["at"]
                base["at"] += -(-size // 32) * 32
            return nc.alloc_sbuf_tensor_at(name, [P, cols], dt, offset=at), at

        x, _ = sb("x", KT * S)
        w_raw, _ = sb("w_raw", RING * UNIT)
        w_hi, _ = sb("w_hi", RING * UNIT, F32R)
        w_lo, _ = sb("w_lo", RING * UNIT, F32R)
        y_hi, at_y = sb("y_hi", KT * S, F32R)
        y_lo, _ = sb("y_lo", KT * S, F32R)
        act_hi, at_b = sb("act_hi", FT * S, F32R)
        act_lo, _ = sb("act_lo", FT * S, F32R)
        rstd, _ = sb("rstd", S)
        sq, _ = sb("sq", S)
        sq_sum, _ = sb("sq_sum", S)
        ident, _ = sb("ident", P)
        ones_d, _ = sb("ones_d", P)
        ones_h, _ = sb("ones_h", P)
        masks, _ = sb("masks", (LEVELS + 1) * P, U8)
        params, _ = sb("params", N_PARAMS)
        lb_e, _ = sb("lb_e", 12)
        lb_s, _ = sb("lb_s", 4)
        lb, _ = sb("lb", 4)
        one_lb, _ = sb("one_lb", 4)
        rstd_tok, _ = sb("rstd_tok", TT)
        neg_max, _ = sb("neg_max", 8)
        denom, _ = sb("denom", 8)
        recip, _ = sb("recip", 8)
        wait_carrier, _ = sb("wait_carrier", 8)
        at_t = base["at"]
        t_slot = [at_t + n * 2080 for n in range(6)]
        gate_t = [sb(f"gate_t{n}", S, at=t_slot[n])[0] for n in range(2)]
        silu_t = [sb(f"silu_t{n}", S, at=t_slot[2 + n])[0] for n in range(2)]
        up_t = [sb(f"up_t{n}", S, at=t_slot[4 + n])[0] for n in range(2)]
        conv_u, _ = sb("conv_u", S + CONV_W - 1, at=t_slot[0])
        conv_c, _ = sb("conv_c", S, at=t_slot[1])
        conv_y, _ = sb("conv_y", S, at=t_slot[2])
        conv_b, _ = sb("conv_b", S, at=t_slot[3])
        cos_k, _ = sb("cos_k", S, at=t_slot[0])
        sin_k, _ = sb("sin_k", S, at=t_slot[1])
        cos_q, _ = sb("cos_q", S, at=t_slot[2])
        sin_q, _ = sb("sin_q", S, at=t_slot[3])
        bias, _ = sb("bias", S, at=t_slot[4])
        swapped, _ = sb("swapped", S, at=t_slot[5])
        assert t_slot[5] + 2080 <= sbuf_end, (t_slot, sbuf_end)

        big = HG * S
        hq, hp, hk, hsg, hv, hat, hsc = (sb(n, big, at=at_b + m * big * 4)[0] for m, n in enumerate(
            ("hg_q", "hg_logf", "hg_k", "hg_gate", "hg_v", "hg_hat", "hg_scores")))
        masks_f, _ = sb("masks_f", (LEVELS + 1) * P, at=at_b + 6 * big * 4)
        mix_hi, _ = sb("mix_hi", KT * S, F32R, at=at_b + 7 * big * 4)
        mix_lo, _ = sb("mix_lo", KT * S, F32R, at=at_b + 9 * big * 4)
        state, _ = sb("hg_state", 3 * S, at=at_b + 2 * big * 4)
        khat_t, _ = sb("hg_khat_t", 3 * S, at=at_b + 5 * big * 4)
        ho, ho_sq, ho_rstd = (sb(n, big, at=at_y + m * big * 4)[0] for m, n in enumerate(
            ("hg_o", "hg_o_sq", "hg_o_rstd")))
        o_hi, _ = sb("o_hi", KT * S, F32R, at=at_b)
        o_lo, _ = sb("o_lo", KT * S, F32R, at=at_b + 16384)
        v_tok, _ = sb("v_tok", TT * D, at=at_b + 32768)
        pt = [sb(f"probs_t{e}", TT * S, at=at_b + 49152 + e * 8192)[0] for e in range(2)]
        q_t = [sb(f"q_t{n}", S, at=at_b + 65536 + n * 2048)[0] for n in range(2)]
        k_t = [sb(f"k_t{n}", S, at=at_b + 69632 + n * 2048)[0] for n in range(2)]
        v_pair = [sb(f"v_pair{n}", TT * P, at=at_b + 73728 + n * 2048)[0] for n in range(2)]
        s_sb = [sb(f"scores{n}", S, at=at_b + 77824 + n * 2048)[0] for n in range(2)]
        prob = [sb(f"probs{n}", S, at=at_b + 81920 + n * 2048)[0] for n in range(4)]
        y_fin, _ = sb("y_fin", KT * S, at=at_y)

        G = [ctx.enter_context(nc.psum_tensor(f"gemm{n}", [P, S], F32)) for n in range(4)]
        aux = ctx.enter_context(nc.psum_tensor("aux", [P, 4 * S], F32))

        def A(bank, c0=0, n=S):
            return aux[:, bank * S + c0:bank * S + c0 + n]


        w_loaded = [sem(f"w_loaded{n}") for n in range(RING)]
        hi_ready = sem("hi_ready")
        lo_ready = sem("lo_ready")
        unit_done = sem("unit_done")
        evacuated = sem("evacuated")
        x_loaded = [sem(f"x_loaded{n}") for n in range(KT // 2)]
        params_loaded, consts_loaded, trig_loaded = sem("params_loaded"), sem("consts_loaded"), sem("trig_loaded")
        ones_set = sem("ones_set")
        masks_ready = sem("masks_ready")
        yh_ready, y_ready = sem("yh_ready"), sem("y_ready")
        sq_ready, sq_added = sem("sq_ready"), sem("sq_added")
        ms_ready = sem("ms_ready")
        inv_ready = sem("inv_ready")
        rstd_ready = sem("rstd_ready")
        v_ready = sem("v_ready")
        dve_chain = sem("dve_chain")
        lb_shifted, lb_exp, lb_ready = sem("lb_shifted"), sem("lb_exp"), sem("lb_ready")
        sig_ready = sem("sig_ready")
        f_ready = sem("f_ready")
        hk_ready = sem("hk_ready")
        logf_ready = sem("logf_ready")
        diff_ready, exp_ready = sem("diff_ready"), sem("exp_ready")
        hat_ready = sem("hat_ready")
        raw_scored, merged = sem("raw_scored"), sem("merged")
        conv_ready, mixh_ready, mix_ready = sem("conv_ready"), sem("mixh_ready"), sem("mix_ready")
        tail_diff, tail_exp, khat_ready, qhat_ready = (
            sem("tail_diff"), sem("tail_exp"), sem("khat_ready"), sem("qhat_ready"))
        khat_turned, khat_copied = sem("khat_turned"), sem("khat_copied")
        kv_ready, state_ready, o_ready, o_taken = sem("kv_ready"), sem("state_ready"), sem("o_ready"), sem("o_taken")
        silu_g_ready = sem("silu_g_ready")
        oms_ready, oinv_ready, orstd_ready, onorm_ready = (
            sem("oms_ready"), sem("oinv_ready"), sem("orstd_ready"), sem("onorm_ready"))
        silu_ready, prod_ready = sem("silu_ready"), sem("prod_ready")
        acth_ready, act_ready = sem("acth_ready"), sem("act_ready")
        swap_ready = sem("swap_ready")
        vp_ready = sem("vp_ready")
        scored, biased, expd = sem("scored"), sem("biased"), sem("expd")
        normed, turned, pt_ready = sem("normed"), sem("turned"), sem("pt_ready")
        pv_done, oh_ready, o_split = sem("pv_done"), sem("oh_ready"), sem("o_split")
        out_ready, out_stored = sem("out_ready"), sem("out_stored")

        block = ctx.enter_context(nc.Block())

        def wslot(t, u, c0=0, n=None):
            s0 = (u % RING) * UNIT + c0
            return t[:, s0:s0 + (unit_cols(u) if n is None else n)]

        @block.sync
        def _(sp):
            def load(src, unit, slot, cols):
                sp.dma_start(w_raw[:, slot * UNIT:slot * UNIT + cols], src[unit, :, 0:cols]).then_inc(w_loaded[slot], 16)

            def loads(src, base_u, count):
                first = RING if base_u == 0 else 0
                for u in range(first):
                    load(src, u, u % RING, unit_cols(base_u + u))
                with sp.Fori(first // RING, count // RING) as i:
                    for s in range(RING):
                        sp.wait_ge(lo_ready, i * RING + (base_u + s + 1 - RING))
                        cols = unit_cols(base_u + s)
                        sp.dma_start(w_raw[:, s * UNIT:s * UNIT + cols],
                                     src[ds(i * RING + s, 1), :, 0:cols].rearrange("o p c -> (o p) c")
                                     ).then_inc(w_loaded[s], 16)

            loads(w_rec, U_REC, 28)
            loads(w_or, U_WOR, 8)
            loads(w_fi[0], U_FI[0], 2 * FT)
            loads(w_fo[0], U_FO[0], 4 * KT)
            loads(w_qkv, U_QKV, 24)
            loads(w_oa, U_WOA, 8)
            loads(w_fi[1], U_FI[1], 2 * FT)
            loads(w_fo[1], U_FO[1], 4 * KT)
            for n in range(KT):
                sp.wait_ge(out_ready, n + 1)
                sp.dma_start(out[n], y_fin[:, n * S:(n + 1) * S]).then_inc(out_stored, 16)
            sp.wait_ge(out_stored, 16 * KT)

        @block.gpsimd
        def _(pool):
            nc.gpsimd.memset(ones_d[:], 1.0 / D).then_inc(ones_set, 1)
            nc.gpsimd.memset(ones_h[:], 1.0 / P).then_inc(ones_set, 1)
            pool.wait_ge(consts_loaded, 32)
            nc.gpsimd.tensor_copy(masks[:], masks_f[:]).then_inc(masks_ready, 1)

            def add_squares(m, first, n):
                pool.wait_ge(sq_ready, 8 * m + n + 1)
                if first:
                    wait(pool, ms_ready, m)
                    nc.gpsimd.tensor_copy(sq_sum[:], sq[:]).then_inc(sq_added, 1)
                else:
                    pool.wait_ge(sq_added, 8 * m + n)
                    nc.gpsimd.tensor_tensor(sq_sum[:], sq_sum[:], sq[:], ALU.add).then_inc(sq_added, 1)

            for m in range(5):
                add_squares(m, True, 0)
                with pool.Fori(1, KT) as n:
                    add_squares(m, False, n)

        def halves(t, a, L):
            h = 1 << L
            v = t[:, a * 2 * S:(a + 1) * 2 * S].rearrange("p (n two h) -> p n two h", two=2, h=h)
            return v[:, :, 0, :], v[:, :, 1, :]

        def events(step):
            return ([0, 1] if step == DIAG_STEP else []) + [
                2 + e for e in range(2 * LEVELS) if LEVEL_STEP[e] == step]


        @block.scalar
        def _(act):
            def split_hi(u, shift=0):
                s = u % RING
                cols = unit_cols(u)
                act.wait_ge(w_loaded[s], shift * (16 // RING) + 16 * (u // RING + 1))
                wait(act, unit_done, shift + (u + 1 - RING))
                nc.scalar.copy(wslot(w_hi, u, 0, cols), wslot(w_raw, u, 0, cols)).then_inc(hi_ready, 1)

            def norm_tile(m, gain, n, out_t):
                wait(act, sq_added, 8 * m + n)
                xn = x[:, ds(n * S, S)]
                nc.scalar.mul(out_t[:, ds(n * S, S)], xn, params[:, ds(n + gain, 1)]).then_inc(yh_ready, 1)
                nc.scalar.activation(sq[:], xn, ACT.Square).then_inc(sq_ready, 1)

            def rstd_root(m, tok=False):
                act.wait_ge(inv_ready, m + 1)
                if tok:
                    nc.scalar.activation(rstd_tok[:], rstd_tok[:], ACT.Sqrt)
                nc.scalar.activation(rstd[:], rstd[:], ACT.Sqrt).then_inc(rstd_ready, 1)

            def prologue():
                act.dma_start(params[:], params_in).then_inc(params_loaded, 16)
                for c in range(KT // 2):
                    act.dma_start(x[:, c * 2 * S:(c + 1) * 2 * S].rearrange("p (t s) -> p t s", t=2),
                                  x_in[:, 2 * c:2 * c + 2, :]).then_inc(x_loaded[c], 16)
                act.dma_start(ident[:], ident_in).then_inc(consts_loaded, 16)
                act.dma_start(masks_f[:], masks_in).then_inc(consts_loaded, 16)
                act.wait_ge(params_loaded, 16)
                split_hi(0)
                for n in range(KT):
                    act.wait_ge(x_loaded[n // 2], 16)
                    norm_tile(0, C_MIX, n, y_hi)
                    if n in (1, 3):
                        split_hi(n // 2 + 1)
                act.wait_ge(lb_shifted, 3)
                nc.scalar.activation(lb_e[:], lb_e[:], ACT.Exp).then_inc(lb_exp, 1)

            def level_exps(e):
                L, a = divmod(e, 2)
                lo, hi = halves(hat, a, L)
                act.wait_ge(diff_ready, e + 1)
                if L:
                    nc.scalar.activation(lo, lo, ACT.Exp)
                nc.scalar.activation(hi, halves(hp, a, L)[1], ACT.Exp).then_inc(exp_ready, 1)

            def conv_hi(j):
                act.wait_ge(conv_ready, j + 1)
                nc.scalar.copy(mix_hi[:, j * S:(j + 1) * S], conv_y[:]).then_inc(mixh_ready, 1)

            def mixer():
                for step in range(0, 36 + 1):
                    split_hi(step + AHEAD)
                    if step == 1:
                        rstd_root(0, tok=True)
                    if step == 4:
                        act.wait_ge(unit_done, 4)
                        act.wait_ge(rstd_ready, 1)
                        for t in range(TT):
                            nc.scalar.activation(hv[:, t * S:(t + 1) * S], A(t), ACT.Silu,
                                                 scale=rstd_tok[:, t:t + 1]).then_inc(v_ready, 1)
                    if step == 8:
                        act.wait_ge(evacuated, E_REC + HG)
                        nc.scalar.activation(hp[:], hk[:], ACT.Sigmoid).then_inc(sig_ready, 1)
                        nc.scalar.activation(hk[:], hk[:], ACT.Sigmoid, scale=-1.0).then_inc(sig_ready, 1)
                    if step == 9:
                        act.wait_ge(f_ready, HG)
                        nc.scalar.activation(hp[:], hp[:], ACT.Ln).then_inc(logf_ready, 1)
                    for x_ in events(step):
                        if x_ >= 2:
                            level_exps(x_ - 2)
                    if step == TAIL:
                        act.wait_ge(tail_diff, 1)
                        nc.scalar.activation(hat[:], hat[:], ACT.Exp).then_inc(tail_exp, 1)
                        nc.scalar.activation(hp[:], hp[:], ACT.Exp).then_inc(tail_exp, 1)
                    if step == TAIL + 2:
                        act.wait_ge(khat_turned, 1)
                        for c in range(3):
                            nc.scalar.copy(khat_t[:, c * S:(c + 1) * S], A(c)).then_inc(khat_copied, 1)
                    for j in range(HG):
                        if step == 19 + 3 * j:
                            conv_hi(j)
                    if step == TAIL + 4:
                        for h in range(HG):
                            act.wait_ge(o_ready, h + 1)
                            nc.scalar.copy(ho[:, h * S:(h + 1) * S], A(h)).then_inc(o_taken, 1)
                            nc.scalar.activation(ho_sq[:, h * S:(h + 1) * S], A(h), ACT.Square).then_inc(o_taken, 1)
                    if step == TAIL + 5:
                        act.wait_ge(evacuated, E_REC + 3 * HG)
                        nc.scalar.activation(hsg[:], hsg[:], ACT.Silu).then_inc(silu_g_ready, 1)
                        act.wait_ge(oinv_ready, 1)
                        nc.scalar.activation(ho_rstd[:], ho_rstd[:], ACT.Sqrt).then_inc(orstd_ready, 1)
                    if step == TAIL + 6:
                        for h in range(HG):
                            act.wait_ge(onorm_ready, h + 1)
                            nc.scalar.copy(mix_hi[:, (HG + h) * S:(HG + h + 1) * S], ho[:, h * S:(h + 1) * S]
                                           ).then_inc(mixh_ready, 1)
                    if step > U_WOR + 4:
                        for n in (2 * (step - U_WOR - 5), 2 * (step - U_WOR - 5) + 1):
                            act.wait_ge(evacuated, E_WOR + 8 + n + 1)
                            norm_tile(1, C_FFN, n, y_hi)

            def ffn_in(l):
                rstd_root(1 + 2 * l)

                def body(i, last):
                    for s in range(1, 5):
                        u = U_FI[l] + s + AHEAD
                        split_hi(u + 4 * i if last else u, 0 if last else 4 * i)
                        j, k = (s - 1) // 2, FT * l + 2 * i + (s - 1) // 2
                        if s % 2:
                            act.wait_ge(evacuated, E_FI[l] + 4 * i + s)
                            nc.scalar.activation(silu_t[j][:], gate_t[j][:], ACT.Silu).then_inc(silu_ready, 1)
                        else:
                            act.wait_ge(prod_ready, k + 1)
                            nc.scalar.copy(act_hi[:, ds((2 * i + j) * S, S)], up_t[j][:]).then_inc(acth_ready, 1)

                with act.Fori(0, FT // 2 - 1) as i:
                    body(i, False)
                body(FT // 2 - 1, True)

            def ffn_out(l):
                m, gain, out_t = ((2, C_MIX + KT, y_hi), (4, C_FIN, y_fin))[l]

                def body(i, last):
                    for s in range(1, 9):
                        u = U_FO[l] + s + AHEAD
                        if not last:
                            split_hi(u, 8 * i)
                        elif u + 8 * i < U_END:
                            split_hi(u + 8 * i)
                        if s % 4 == 0:
                            n = 2 * i + (s // 4 - 1)
                            act.wait_ge(evacuated, E_FO[l] + n + 1)
                            norm_tile(m, gain, n, out_t)

                with act.Fori(0, KT // 2 - 1) as i:
                    body(i, False)
                body(KT // 2 - 1, True)

            def swap(k, bank, g):
                if g == 0:
                    act.wait_ge(unit_done, k + (U_QKV + 8 + 1))
                    wait(act, evacuated, k + E_QKV)
                nc.scalar.copy(swapped[32 * (g ^ 1):32 * (g ^ 1) + 32, :], G[bank][32 * g:32 * g + 32, :]
                               ).then_inc(swap_ready, 1)

            def attend(q, par, pos, tab):
                if pos == tab.values:
                    wait(act, pv_done, q - 1)
                    src = v_tok[:].rearrange("s (j c) -> s j c", j=TT)[:, :, ds(q * P, P)]
                    nc.scalar.copy(v_pair[par][:].rearrange("s (j c) -> s j c", j=TT), src).then_inc(vp_ready, 1)
                for n in range(8):
                    t = n % 4
                    w = (t + 1) * P
                    if pos == tab.probs[n]:
                        act.wait_ge(turned, 8 * q + n + 1)
                        if t == 0:
                            wait(act, pv_done, q)
                        dst = pt[n // 4][:].rearrange("s (j t) -> s j t", j=TT)[:, 0:t + 1, t * P:w]
                        nc.scalar.copy(dst, A(2 + n % 2, 0, w).rearrange("s (j t) -> s j t", j=t + 1)
                                       ).then_inc(pt_ready, 1)
                for n in range(8):
                    t = n % 4
                    w = (t + 1) * P
                    if pos == tab.exp[n]:
                        act.wait_ge(biased, 8 * q + n + 1)
                        wait(act, turned, 8 * q + n - 3)
                        nc.scalar.activation(prob[t][:, 0:w], s_sb[n % 2][:, 0:w], ACT.Exp,
                                             bias=neg_max[:, n:n + 1], scale=-1.0,
                                             accum_out=denom[:, n:n + 1]).then_inc(expd, 1)
                if pos == tab.out:
                    act.wait_ge(pv_done, q + 1)
                    nc.scalar.copy(o_hi[:, ds(q * S, S)], G[2][:]).then_inc(oh_ready, 1)

            def values(half):
                for t in range(TT):
                    src = A(t) if half == 0 else G[t][:]
                    nc.scalar.activation(v_tok[:, t * D + half * S:t * D + half * S + S], src, ACT.Copy,
                                         scale=rstd_tok[:, t:t + 1]).then_inc(v_ready, 1)

            def pair(p, ps, shift=0):
                for s in range(16):
                    if s % 8 == 0:
                        split_hi(U_QKV + 8 + ps * 2 + s // 8 + AHEAD, shift)
                    if s == 0 and ps == 0:
                        act.wait_ge(unit_done, U_QKV + 8)
                        values(1)
                    if SWAP <= s < SWAP + 4 and ps > 0:
                        swap(2 * p - 1, 1, s - SWAP)
                    if 8 + SWAP <= s < 8 + SWAP + 4:
                        swap(2 * p, 0, s - 8 - SWAP)
                    if ps > 1:
                        attend(p - 2, ps % 2, s + 16, ATT)
                    if ps > 0:
                        attend(p - 1, (ps + 1) % 2, s, ATT)

            def attention():
                act.wait_ge(act_ready, FT)
                act.dma_start(cos_k[:], trig_in[0]).then_inc(trig_loaded, 16)
                act.dma_start(sin_k[:], trig_in[1]).then_inc(trig_loaded, 16)
                act.dma_start(bias[:], bias_in).then_inc(trig_loaded, 16)
                rstd_root(2, tok=True)
                for s in range(1, 8):
                    split_hi(U_QKV + s + AHEAD)
                    if s == 4:
                        act.wait_ge(unit_done, U_QKV + 4)
                        act.wait_ge(rstd_ready, 3)
                        values(0)
                pair(0, 0)
                pair(1, 1)
                with act.Fori(1, PAIRS // 2) as i:
                    for r in range(2):
                        pair(2 * i + r, 2 + r, 4 * (i - 1))
                split_hi(U_WOA + AHEAD)
                for s in range(24):
                    if SWAP <= s < SWAP + 4:
                        swap(2 * PAIRS - 1, 1, s - SWAP)
                    attend(PAIRS - 2, 0, s + 16, ATT)
                    attend(PAIRS - 1, 1, s, LAST_ATT)
                for s in range(1, 9):
                    split_hi(U_WOA + s + AHEAD)
                    act.wait_ge(evacuated, E_WOA + s)
                    norm_tile(3, C_FFN + KT, s - 1, y_hi)

            prologue()
            mixer()
            ffn_in(0)
            ffn_out(0)
            attention()
            ffn_in(1)
            ffn_out(1)
            rstd_root(4)

        @block.vector
        def _(dve):
            V = nc.vector
            chain = Chain(dve, dve_chain)

            def split_lo(u, shift=0):
                cols = unit_cols(u)
                dve.wait_ge(hi_ready, shift + (u + 1))
                V.tensor_tensor(wslot(w_lo, u, 0, cols), wslot(w_raw, u, 0, cols),
                                wslot(w_hi, u, 0, cols).bitcast(F32), ALU.subtract).then_inc(lo_ready, 1)

            def norm_tile(m, gain, n):
                dve.wait_ge(yh_ready, 8 * m + n + 1)
                V.scalar_tensor_tensor(out=y_lo[:, ds(n * S, S)], in0=x[:, ds(n * S, S)],
                                       scalar=params[:, ds(n + gain, 1)],
                                       in1=y_hi[:, ds(n * S, S)].bitcast(F32),
                                       op0=ALU.mult, op1=ALU.subtract).then_inc(y_ready, 1)

            def residual(n, unit, bank):
                dve.wait_ge(unit_done, unit + 1)
                xn = x[:, ds(n * S, S)]
                V.tensor_tensor(xn, xn, bank, ALU.add).then_inc(evacuated, 1)

            def inverse(m, bank, tok_bank=None):
                dve.wait_ge(ms_ready, m + 1)
                if tok_bank is not None:
                    chain.mark(V.tensor_scalar(rstd_tok[:], tok_bank[:, 0:TT], EPS, None, ALU.add))
                    chain.fence()
                    chain.mark(V.reciprocal(rstd_tok[:], rstd_tok[:]))
                chain.mark(V.tensor_scalar(rstd[:], bank, EPS, None, ALU.add))
                chain.fence()
                V.reciprocal(rstd[:], rstd[:]).then_inc(inv_ready, 1)

            def prologue():
                dve.wait_ge(params_loaded, 16)
                row = [params[:, C_LB + 4 * r:C_LB + 4 * r + 4] for r in range(3)]
                chain.mark(V.tensor_tensor(lb_s[:], row[0], row[1], ALU.max))
                chain.fence()
                chain.mark(V.tensor_tensor(lb_s[:], lb_s[:], row[2], ALU.max))
                chain.fence()
                for r in range(3):
                    V.tensor_tensor(lb_e[:, 4 * r:4 * r + 4], row[r], lb_s[:], ALU.subtract
                                    ).then_inc(lb_shifted, 1)
                split_lo(0)
                for n in range(KT):
                    if n % 2 == 0:
                        dve.wait_ge(x_loaded[n // 2], 16)
                    norm_tile(0, C_MIX, n)
                    if n in (1, 3):
                        split_lo(n // 2 + 1)
                dve.wait_ge(lb_exp, 1)
                chain.mark(V.tensor_tensor(one_lb[:], lb_e[:, 0:4], lb_e[:, 8:12], ALU.add))
                chain.fence()
                chain.mark(V.tensor_tensor(lb_s[:], one_lb[:], lb_e[:, 4:8], ALU.add))
                chain.fence()
                chain.mark(V.reciprocal(lb_s[:], lb_s[:]))
                chain.fence()
                V.tensor_tensor(lb[:], lb_e[:, 4:8], lb_s[:], ALU.mult).then_inc(lb_ready, 1)
                V.tensor_tensor(one_lb[:], one_lb[:], lb_s[:], ALU.mult).then_inc(lb_ready, 1)
                chain.mark(V.memset(conv_u[:, 0:CONV_W - 1], 0.0))

            def take(u, dst):
                dve.wait_ge(unit_done, u + 1)
                V.tensor_tensor(dst, G[u % 4][:], rstd[:], ALU.mult).then_inc(evacuated, 1)

            def level_diff(e):
                L, a = divmod(e, 2)
                h = 1 << L
                lo = halves(hat, a, L)[0]
                plo = halves(hp, a, L)[0]
                if L:
                    dve.wait_ge(raw_scored, 2 + e - 2 + 1)
                    chain.fence()
                    V.tensor_tensor(lo, plo[:, :, h - 1:h].broadcast_to(plo.shape), plo, ALU.subtract
                                    ).then_inc(diff_ready, 1)
                else:
                    V.tensor_copy(lo, halves(hk, a, L)[0]).then_inc(diff_ready, 1)

            def level_hat(e):
                L, a = divmod(e, 2)
                h = 1 << L
                lo, hi = halves(hat, a, L)
                plo, phi = halves(hp, a, L)
                dve.wait_ge(exp_ready, e + 1)
                if L:
                    V.tensor_tensor(lo, lo, halves(hk, a, L)[0], ALU.mult).then_inc(hat_ready, 1)
                V.tensor_tensor(hi, hi, halves(hq, a, L)[1], ALU.mult).then_inc(hat_ready, 1)
                chain.mark(V.tensor_tensor(phi, phi, plo[:, :, h - 1:h].broadcast_to(phi.shape), ALU.add))

            def merge(ev):
                dve.wait_ge(raw_scored, ev + 1)
                if ev < 2:
                    dst = hsc[:, ev * 2 * S:(ev + 1) * 2 * S].rearrange("p (m t) -> p m t", t=P)
                    src = aux[:, ev * 2 * S:(ev + 1) * 2 * S].rearrange("p (m t) -> p m t", t=P)
                    mask = masks[:, LEVELS * P:]
                    mask = mask.unsqueeze(1).broadcast_to(dst.shape)
                else:
                    L, a = divmod(ev - 2, 2)
                    dst = halves(hsc, a, L)[1].rearrange("p (m n) h -> p m n h", m=8)
                    src = halves(aux, a, L)[1].rearrange("p (m n) h -> p m n h", m=8)
                    mask = masks[:, L * P:(L + 1) * P].rearrange("p (n two h) -> p n two h", two=2, h=1 << L)
                    mask = mask[:, :, 1, :].unsqueeze(1).broadcast_to(dst.shape)
                    dve.wait_ge(merged, ev - 1)
                V.copy_predicated(dst, mask, src).then_inc(merged, 1)

            def conv(j, part, u):
                if part == 0:
                    take(u, conv_c[:])
                elif part == 1:
                    take(u, conv_u[:, 2:])
                    dve.wait_ge(evacuated, E_REC + 12 + 3 * j + 2)
                    chain.mark(V.tensor_tensor(conv_u[:, 2:], conv_u[:, 2:], conv_c[:], ALU.mult))
                    wait(dve, mixh_ready, j)
                    chain.fence()
                    for tap in range(CONV_W - 1, -1, -1):
                        w = params[:, C_CONV + 4 * tap + j:C_CONV + 4 * tap + j + 1]
                        src = conv_u[:, tap:tap + S]
                        if tap == CONV_W - 1:
                            chain.mark(V.tensor_scalar(conv_y[:], src, w, None, ALU.mult))
                        else:
                            chain.mark(V.scalar_tensor_tensor(out=conv_y[:], in0=src, scalar=w, in1=conv_y[:],
                                                              op0=ALU.mult, op1=ALU.add))
                        chain.fence()
                else:
                    take(u, conv_b[:])
                    dve.wait_ge(evacuated, E_REC + 12 + 3 * j + 3)
                    V.tensor_tensor(conv_y[:], conv_y[:], conv_b[:], ALU.mult).then_inc(conv_ready, 1)

            def mix_split(k, src):
                dve.wait_ge(mixh_ready, k + 1)
                V.tensor_tensor(mix_lo[:, k * S:(k + 1) * S], src, mix_hi[:, k * S:(k + 1) * S].bitcast(F32),
                                ALU.subtract).then_inc(mix_ready, 1)

            def mixer():
                for step in range(0, 36 + 1):
                    split_lo(step + AHEAD)
                    pu = step - 1
                    if step == 1:
                        inverse(0, G[3][:], G[2])
                    if step == DIAG_STEP:
                        dve.wait_ge(masks_ready, 1)
                        chain.mark(V.memset(hsc[:], 0.0))
                        dve.wait_ge(logf_ready, 1)
                        chain.fence()
                    for ev in events(step - 1):
                        merge(ev)
                    for ev in events(step):
                        if ev >= 2:
                            level_diff(ev - 2)
                    if 4 <= pu < 8:
                        h = pu - 4
                        take(pu, hk[:, h * S:(h + 1) * S])
                    elif 8 <= pu < 12:
                        h = pu - 8
                        take(pu, hq[:, h * S:(h + 1) * S])
                    elif 12 <= pu < 16:
                        h = pu - 12
                        take(pu, hsg[:, h * S:(h + 1) * S])
                    elif 16 <= pu < 28:
                        conv((pu - 16) // 3, (pu - 16) % 3, pu)
                    if step == 9:
                        dve.wait_ge(sig_ready, 2)
                        dve.wait_ge(lb_ready, 2)
                        for h in range(HG):
                            blk = slice(h * S, (h + 1) * S)
                            V.tensor_scalar(hp[:, blk], hp[:, blk], one_lb[:, h:h + 1], lb[:, h:h + 1],
                                            ALU.mult, ALU.add).then_inc(f_ready, 1)
                        for h in range(HG):
                            blk = slice(h * S, (h + 1) * S)
                            V.tensor_scalar(hk[:, blk], hk[:, blk], one_lb[:, h:h + 1], None, ALU.mult
                                            ).then_inc(hk_ready, 1)
                    for ev in events(step):
                        if ev >= 2:
                            level_hat(ev - 2)
                    for j in range(HG):
                        if step == (20 + 3 * j if j < HG - 1 else 28):
                            mix_split(j, conv_y[:])
                    tail(step)
                    if step > U_WOR:
                        for n in (2 * (pu - U_WOR), 2 * (pu - U_WOR) + 1):
                            residual(n % KT, pu, G[n % 4][:])
                            if n >= KT:
                                norm_tile(1, C_FFN, n - KT)

            def tail(step):
                if step == TAIL:
                    dve.wait_ge(raw_scored, 2 + 2 * LEVELS)
                    chain.fence()
                    pv = hp[:].rearrange("p (m t) -> p m t", t=P)
                    V.tensor_tensor(hat[:].rearrange("p (m t) -> p m t", t=P),
                                    pv[:, :, P - 1:P].broadcast_to(pv.shape), pv, ALU.subtract
                                    ).then_inc(tail_diff, 1)
                if step == TAIL + 1:
                    dve.wait_ge(tail_exp, 2)
                    V.tensor_tensor(hat[:], hat[:], hk[:], ALU.mult).then_inc(khat_ready, 1)
                    V.tensor_tensor(hq[:], hq[:], hp[:], ALU.mult).then_inc(qhat_ready, 1)
                if step == TAIL + 3:
                    dve.wait_ge(kv_ready, 3)
                    chain.mark(V.tensor_copy(state[:, 0:S], A(3)))
                    for c in (1, 2):
                        prev, cur = state[:, (c - 1) * S:c * S], state[:, c * S:(c + 1) * S]
                        decay = hp[:].rearrange("p (h t) -> p h t", h=HG)[:, :, c * P + P - 1:c * P + P]
                        chain.fence()
                        chain.mark(V.tensor_tensor(cur.rearrange("p (h v) -> p h v", h=HG),
                                                   prev.rearrange("p (h v) -> p h v", h=HG),
                                                   decay.broadcast_to([P, HG, P]), ALU.mult))
                        chain.fence()
                        ins = V.tensor_tensor(cur, cur, A(c - 1), ALU.add)
                        if c == 1:
                            chain.mark(ins)
                        else:
                            ins.then_inc(state_ready, 1)
                if step == TAIL + 5:
                    dve.wait_ge(oms_ready, 1)
                    chain.mark(V.tensor_scalar(ho_rstd[:], aux[:], EPS, None, ALU.add))
                    chain.fence()
                    V.reciprocal(ho_rstd[:], ho_rstd[:]).then_inc(oinv_ready, 1)
                if step == TAIL + 6:
                    dve.wait_ge(orstd_ready, 1)
                    dve.wait_ge(silu_g_ready, 1)
                    for h in range(HG):
                        blk = slice(h * S, (h + 1) * S)
                        chain.mark(V.tensor_tensor(ho[:, blk], ho[:, blk], ho_rstd[:, blk], ALU.mult))
                    chain.fence()
                    for h in range(HG):
                        blk = slice(h * S, (h + 1) * S)
                        V.scalar_tensor_tensor(out=ho[:, blk], in0=ho[:, blk], scalar=params[:, C_HN:C_HN + 1],
                                               in1=hsg[:, blk], op0=ALU.mult, op1=ALU.mult
                                               ).then_inc(onorm_ready, 1)
                    for h in range(HG):
                        mix_split(HG + h, ho[:, h * S:(h + 1) * S])

            def ffn_in(l):
                inverse(1 + 2 * l, A(3))
                dve.wait_ge(rstd_ready, 2 + 2 * l)

                def body(i, last):
                    for s in range(1, 5):
                        u = U_FI[l] + s + AHEAD
                        split_lo(u + 4 * i if last else u, 0 if last else 4 * i)
                        j, k = (s - 1) // 2, FT * l + 2 * i + (s - 1) // 2
                        dve.wait_ge(unit_done, U_FI[l] + 4 * i + s)
                        dst = (gate_t if s % 2 else up_t)[j]
                        V.tensor_tensor(dst[:], G[s - 1][:], rstd[:], ALU.mult).then_inc(evacuated, 1)
                        if s % 2 == 0:
                            dve.wait_ge(evacuated, E_FI[l] + 4 * i + s)
                            dve.wait_ge(silu_ready, k + 1)
                            V.tensor_tensor(dst[:], dst[:], silu_t[j][:], ALU.mult).then_inc(prod_ready, 1)
                            dve.wait_ge(acth_ready, k + 1)
                            tile = ds((2 * i + j) * S, S)
                            V.tensor_tensor(act_lo[:, tile], dst[:], act_hi[:, tile].bitcast(F32), ALU.subtract
                                            ).then_inc(act_ready, 1)

                with dve.Fori(0, FT // 2 - 1) as i:
                    body(i, False)
                body(FT // 2 - 1, True)

            def ffn_out(l):
                def body(i, last):
                    for s in range(1, 9):
                        u = U_FO[l] + s + AHEAD
                        if not last:
                            split_lo(u, 8 * i)
                        elif u + 8 * i < U_END:
                            split_lo(u + 8 * i)
                        if s % 4 == 0:
                            n = 2 * i + (s // 4 - 1)
                            residual(n, U_FO[l] + 8 * i + s - 1, G[s // 4 - 1][:])
                            if l == 0:
                                norm_tile(2, C_MIX + KT, n)

                with dve.Fori(0, KT // 2 - 1) as i:
                    body(i, False)
                body(KT // 2 - 1, True)

            def rope(k, bank, dst, cos, sin, free):
                wait(dve, scored, free)
                dve.wait_ge(swap_ready, 4 * (k + 1))
                chain.mark(V.tensor_tensor(dst[:], G[bank][:], cos[:], ALU.mult))
                chain.mark(V.tensor_tensor(swapped[:], swapped[:], sin[:], ALU.mult))
                chain.fence()
                V.tensor_tensor(dst[:], dst[:], swapped[:], ALU.add).then_inc(evacuated, 1)

            def attend(q, par, pos, tab):
                for n in range(8):
                    t = n % 4
                    w = (t + 1) * P
                    if pos == tab.norm[n]:
                        dve.wait_ge(expd, 8 * q + n + 1)
                        chain.mark(V.reciprocal(recip[:, n:n + 1], denom[:, n:n + 1]))
                        chain.fence()
                        V.tensor_scalar(prob[t][:, 0:w], prob[t][:, 0:w], recip[:, n:n + 1], None, ALU.mult
                                        ).then_inc(normed, 1)
                for n in range(8):
                    t = n % 4
                    w = (t + 1) * P
                    if pos == tab.bias[n]:
                        dve.wait_ge(scored, 8 * q + n + 1)
                        V.memset(wait_carrier[:, n:n + 1], 0.0)
                        V.tensor_tensor_reduce(out=s_sb[n % 2][:, 0:w], in0=A(n % 2, 0, w),
                                               in1=bias[:, (TT - 1 - t) * P:], scale=1.0, scalar=3e38,
                                               op0=ALU.add, op1=ALU.min, accum_out=neg_max[:, n:n + 1]
                                               ).then_inc(biased, 1)
                if pos == tab.out:
                    dve.wait_ge(oh_ready, q + 1)
                    V.tensor_tensor(o_lo[:, ds(q * S, S)], G[2][:], o_hi[:, ds(q * S, S)].bitcast(F32),
                                    ALU.subtract).then_inc(o_split, 1)

            def pair(p, ps, shift=0):
                for s in range(16):
                    if s % 8 == 0:
                        split_lo(U_QKV + 8 + ps * 2 + s // 8 + AHEAD, shift)
                    if s == ROPE and ps > 0:
                        rope(2 * p - 1, 1, k_t[(ps + 1) % 2], cos_k, sin_k, 8 * (p - 2))
                    if s == 8 + ROPE:
                        rope(2 * p, 0, q_t[ps % 2], cos_q, sin_q, 8 * (p - 1))
                    if ps > 1:
                        attend(p - 2, ps % 2, s + 16, ATT)
                    if ps > 0:
                        attend(p - 1, (ps + 1) % 2, s, ATT)

            def attention():
                inverse(2, G[3][:], G[2])
                for s in range(1, 8):
                    split_lo(U_QKV + s + AHEAD)
                    if s == 3:
                        dve.wait_ge(trig_loaded, 48)
                        dve.wait_ge(rstd_ready, 3)
                        for tab in (cos_k, sin_k):
                            chain.mark(V.tensor_tensor(tab[:], tab[:], rstd[:], ALU.mult))
                        chain.fence()
                        for tab, src in ((cos_q, cos_k), (sin_q, sin_k)):
                            chain.mark(V.tensor_scalar(tab[:], src[:], QSCALE, None, ALU.mult))
                        chain.fence()
                pair(0, 0)
                pair(1, 1)
                with dve.Fori(1, PAIRS // 2) as i:
                    chain.loop(i, 1, 24)
                    for r in range(2):
                        pair(2 * i + r, 2 + r, 4 * (i - 1))
                chain.done(PAIRS // 2 - 1)
                split_lo(U_WOA + AHEAD)
                for s in range(24):
                    if s == ROPE:
                        rope(2 * PAIRS - 1, 1, k_t[1], cos_k, sin_k, 8 * (PAIRS - 2))
                    attend(PAIRS - 2, 0, s + 16, ATT)
                    attend(PAIRS - 1, 1, s, LAST_ATT)
                for s in range(1, 9):
                    split_lo(U_WOA + s + AHEAD)
                    residual(s - 1, U_WOA + s - 1, G[WOA_BANK[(s - 1) % 3]][:])
                    norm_tile(3, C_FFN + KT, s - 1)

            def final_norm():
                inverse(4, A(3))
                dve.wait_ge(rstd_ready, 5)
                dve.wait_ge(yh_ready, 5 * KT)
                for n in range(KT):
                    tile = slice(n * S, (n + 1) * S)
                    V.tensor_tensor(y_fin[:, tile], y_fin[:, tile], rstd[:], ALU.mult).then_inc(out_ready, 1)

            prologue()
            mixer()
            ffn_in(0)
            ffn_out(0)
            attention()
            ffn_in(1)
            ffn_out(1)
            final_norm()

        @block.tensor
        def _(pe):
            def mm3(out, stat, mov, first, last):
                pe.matmul(out, stat[0], mov[0], start=first, stop=False)
                pe.matmul(out, stat[0], mov[1], start=False, stop=False)
                return pe.matmul(out, stat[1], mov[0], start=False, stop=last)

            def weight(u, tile, n=P):
                at = (u % RING) * UNIT + tile * P
                return w_hi[:, at:at + n], w_lo[:, at:at + n]

            def tile_of(hi_t, lo_t, k, c0=0, n=S):
                return hi_t[:, k * S + c0:k * S + c0 + n], lo_t[:, k * S + c0:k * S + c0 + n]

            def begin(u):
                pe.wait_ge(lo_ready, u + 1)

            def y_tile(m, k, first):
                if first:
                    pe.wait_ge(y_ready, 8 * m + k + 1)
                return tile_of(y_hi, y_lo, k)

            def mean_square(m, bank, tok_bank=None):
                if m == 0:
                    pe.wait_ge(ones_set, 2)
                pe.wait_ge(sq_added, 8 * (m + 1))
                if tok_bank is not None:
                    for t in range(TT):
                        pe.matmul(tok_bank[:, t:t + 1], sq_sum[:, t * P:(t + 1) * P], ones_d[:, 0:1],
                                  start=True, stop=True)
                pe.matmul(bank, ones_d[:], sq_sum[:], start=True, stop=True).then_inc(ms_ready, 1)

            def whole_tile(u, bank, m, first):
                for k in range(KT):
                    ins = mm3(bank, weight(u, k), y_tile(m, k, first), k == 0, k == KT - 1)
                ins.then_inc(unit_done, 1)

            def token_major(u0, bank_of, m, first):
                for j in range(4):
                    begin(u0 + j)
                    for kk in range(2):
                        k = 2 * j + kk
                        if first:
                            pe.wait_ge(y_ready, 8 * m + k + 1)
                        for t in range(TT):
                            ins = mm3(bank_of(t), tile_of(y_hi, y_lo, k, t * P, P), weight(u0 + j, kk * 4, S),
                                      k == 0, k == KT - 1)
                    ins.then_inc(unit_done, 1)
                    if j == 0 and first:
                        mean_square(m, *MS_BANKS[m])

            MS_BANKS = {0: (G[3][:], G[2]), 2: (G[3][:], G[2])}

            def score_event(ev):
                a = ev % 2
                wait(pe, merged, ev - 1)
                if ev < 2:
                    if ev == 0:
                        pe.wait_ge(v_ready, TT)
                        pe.wait_ge(evacuated, E_REC + 2 * HG)
                        pe.wait_ge(logf_ready, 1)
                        pe.wait_ge(hk_ready, HG)
                else:
                    L = (ev - 2) // 2
                    done = sum(1 if (x_ - 2) // 2 == 0 else 2 for x_ in range(2, ev + 1))
                    pe.wait_ge(hat_ready, done)
                for m in range(8):
                    c0 = a * 2 * S + m * P
                    if ev < 2:
                        ins = pe.matmul(aux[:, c0:c0 + P], hk[:, c0:c0 + P], hq[:, c0:c0 + P], start=True, stop=True)
                    else:
                        right = lambda t: t[:, c0:c0 + P].rearrange("p (n two h) -> p n two h", two=2, h=1 << L)[:, :, 1, :]
                        ins = pe.matmul(right(aux), hat[:, c0:c0 + P], right(hat), start=True, stop=True)
                ins.then_inc(raw_scored, 1)

            def tail(unit):
                hc = lambda t, h, c: t[:, h * S + c * P:h * S + (c + 1) * P]
                if unit == TAIL + 1:
                    pe.wait_ge(khat_ready, 1)
                    pe.wait_ge(merged, 2 + 2 * LEVELS)
                    for c in range(3):
                        for h in range(HG):
                            ins = pe.transpose(A(c, h * P, P), hc(hat, h, c), ident[:])
                    ins.then_inc(khat_turned, 1)
                if unit == TAIL + 2:
                    pe.wait_ge(khat_copied, 3)
                    for c, bank in enumerate((3, 0, 1)):
                        for h in range(HG):
                            ins = pe.matmul(A(bank, h * P, P), khat_t[:, c * S + h * P:c * S + (h + 1) * P],
                                            hv[:, c * S + h * P:c * S + (h + 1) * P], start=True, stop=True)
                        ins.then_inc(kv_ready, 1)
                if unit == TAIL + 3:
                    pe.wait_ge(state_ready, 1)
                    for h in range(HG):
                        for c in range(TT):
                            ins = pe.matmul(A(h, c * P, P), hv[:, c * S + h * P:c * S + (h + 1) * P],
                                            hc(hsc, h, c), start=True, stop=c == 0)
                            if c:
                                ins = pe.matmul(A(h, c * P, P), state[:, (c - 1) * S + h * P:(c - 1) * S + (h + 1) * P],
                                                hc(hq, h, c), start=False, stop=True)
                        ins.then_inc(o_ready, 1)
                if unit == TAIL + 4:
                    pe.wait_ge(o_taken, 2 * HG)
                    for h in range(HG):
                        ins = pe.matmul(A(h), ones_h[:], ho_sq[:, h * S:(h + 1) * S], start=True, stop=True)
                    ins.then_inc(oms_ready, 1)

            def mixer():
                token_major(U_REC, A, 0, True)
                for u in range(4, 28):
                    begin(u)
                    wait(pe, evacuated, E_REC + u - 4 - 4 + 1)
                    if u == 6:
                        pe.wait_ge(inv_ready, 1)
                    whole_tile(u, G[u % 4][:], 0, False)
                    for ev in events(u):
                        score_event(ev)
                    tail(u)
                for u in range(U_WOR, U_WOR + 8):
                    begin(u)
                    half = (u - U_WOR) // 4
                    for e in range(2):
                        n = 2 * (u - U_WOR) + e
                        pe.wait_ge(evacuated, E_WOR + n - 4 + 1)
                        for k in range(4):
                            pe.wait_ge(mix_ready, 4 * half + k + 1)
                            ins = mm3(G[n % 4][:], weight(u, 4 * e + k), tile_of(mix_hi, mix_lo, 4 * half + k),
                                      k == 0, k == 3)
                    ins.then_inc(unit_done, 1)
                    tail(u)

            def ffn_in(l, bank_free):
                m = 1 + 2 * l

                def body(i, first):
                    for s in range(4):
                        begin(U_FI[l] + 4 * i + s)
                        pe.wait_ge(evacuated, bank_free[s] if first else E_FI[l] + 4 * i + s - 3)
                        whole_tile(U_FI[l] + s, G[s][:], m, first and s == 0)
                        if first and s == 0:
                            mean_square(m, A(3))

                body(0, True)
                with pe.Fori(1, FT // 2) as i:
                    body(i, False)

            def ffn_out(l):
                def body(i, first):
                    for e in range(2):
                        pe.wait_ge(evacuated, E_FO[l] if first else E_FO[l] + 2 * i + e - 1)
                        k = 0
                        for s in range(4):
                            begin(U_FO[l] + 8 * i + 4 * e + s)
                            for tile in range(FO_TILES[s]):
                                if first and e == 0:
                                    pe.wait_ge(act_ready, FT * l + k + 1)
                                ins = mm3(G[e][:], weight(U_FO[l] + s, tile), tile_of(act_hi, act_lo, k),
                                          k == 0, k == FT - 1)
                                k += 1
                            ins.then_inc(unit_done, 1)

                body(0, True)
                with pe.Fori(1, KT // 2) as i:
                    body(i, False)

            def attend(q, par, pos, tab):
                for n in range(8):
                    e, t = divmod(n, 4)
                    if pos == tab.qk[n]:
                        pe.wait_ge(evacuated, 2 * q + (E_QKV + 2))
                        wait(pe, biased, 8 * q + n - 1)
                        rows = slice(e * HD, (e + 1) * HD)
                        pe.matmul(A(n % 2, 0, (t + 1) * P), q_t[par][rows, t * P:(t + 1) * P],
                                  k_t[par][rows, 0:(t + 1) * P], start=True, stop=True).then_inc(scored, 1)
                    if pos == tab.turn[n]:
                        pe.wait_ge(normed, 8 * q + n + 1)
                        wait(pe, pt_ready, 8 * q + n - 1)
                        for j in range(t + 1):
                            ins = pe.transpose(A(2 + n % 2, j * P, P), prob[t][:, j * P:(j + 1) * P], ident[:])
                        ins.then_inc(turned, 1)
                if pos == tab.pv:
                    pe.wait_ge(pt_ready, 8 * q + 8)
                    pe.wait_ge(vp_ready, q + 1)
                    wait(pe, o_split, q)
                    for j in range(TT):
                        for e in range(2):
                            ins = pe.matmul(G[2][e * HD:(e + 1) * HD, j * P:],
                                            v_pair[par][:, j * P + e * HD:j * P + (e + 1) * HD],
                                            pt[e][:, j * S + j * P:(j + 1) * S], start=j == 0, stop=j == TT - 1,
                                            skip_group_check=True)
                    ins.then_inc(pv_done, 1)

            def pair(p, ps):
                for s in range(16):
                    k, j = s % 8, s // 8
                    if k == 0:
                        begin(U_QKV + 8 + 2 * p + j)
                        if ps == 0:
                            pe.wait_ge(v_ready, 2 * TT + j + 1)
                        else:
                            pe.wait_ge(evacuated, E_QKV + 2 * p - 1 + j)
                    ins = mm3(G[j][:], weight(U_QKV + 8 + 2 * ps + j, k), tile_of(y_hi, y_lo, k), k == 0, k == KT - 1)
                    if k == KT - 1:
                        ins.then_inc(unit_done, 1)
                    if s == 0 and ps == 1:
                        pe.wait_ge(v_ready, 3 * TT)
                    if ps > 1:
                        attend(p - 2, ps % 2, s + 16, ATT)
                    if ps > 0:
                        attend(p - 1, (ps + 1) % 2, s, ATT)

            def attention():
                token_major(U_QKV, A, 2, True)
                pe.wait_ge(evacuated, E_QKV)
                pe.wait_ge(inv_ready, 3)
                token_major(U_QKV + 4, lambda t: G[t][:], 2, False)
                pair(0, 0)
                pair(1, 1)
                with pe.Fori(1, PAIRS // 2) as i:
                    for r in range(2):
                        pair(2 * i + r, 2 + r)
                for n in range(3):
                    begin(U_WOA + n)
                pe.wait_ge(evacuated, E_QKV + 2 * PAIRS - 1)
                for s, (k, n) in enumerate(WOA_SLOTS):
                    if n == 0:
                        pe.wait_ge(o_split, k + 1)
                    if (k, n) == (0, 2):
                        pe.wait_ge(evacuated, E_QKV + 2 * PAIRS)
                    ins = mm3(G[WOA_BANK[n]][:], weight(U_WOA + n, k), tile_of(o_hi, o_lo, k), k == 0, k == KT - 1)
                    if k == KT - 1:
                        ins.then_inc(unit_done, 1)
                    attend(PAIRS - 2, 0, s + 16, ATT)
                    attend(PAIRS - 1, 1, s, LAST_ATT)
                for n in range(3, KT):
                    begin(U_WOA + n)
                    pe.wait_ge(evacuated, E_WOA + n - 2)
                    for k in range(KT):
                        ins = mm3(G[WOA_BANK[n % 3]][:], weight(U_WOA + n, k), tile_of(o_hi, o_lo, k), k == 0, k == KT - 1)
                    ins.then_inc(unit_done, 1)

            mixer()
            ffn_in(0, [E_FI[0] - 3 + b for b in range(4)])
            ffn_out(0)
            attention()
            pe.wait_ge(o_split, PAIRS)
            ffn_in(1, [E_FI[1] - 1, E_FI[1] - 2, E_FI[1] - 2, E_FI[1]])
            ffn_out(1)
            mean_square(4, A(3))


def blocks(w):
    k, n = w.shape
    return w.reshape(k // P, P, n // P, P).transpose(2, 1, 0, 3).reshape(n // P, P, k)


def token_major_units(w):
    k, n = w.shape
    return (w.reshape(k // (2 * P), 2, P, n // S, S).transpose(3, 0, 2, 1, 4)
            .reshape(n // S * (k // (2 * P)), P, 2 * S))


def constants():
    tq, ks = np.arange(P)[:, None], np.arange(P)[None, :]
    bias = np.empty((P, TT, P), np.float32)
    for col in range(TT):
        rel = (TT - 1 - col) * P + tq - ks
        count = ((rel >= 0) & (rel <= P)).astype(int) + ((rel >= 0) & (rel % 4 == 0)) + ((rel >= 0) & (rel % 16 == 0))
        bias[:, col] = np.where(count > 0, -np.log(np.maximum(count, 1)), 1e30)
    masks = np.zeros((P, LEVELS + 1, P), np.float32)
    s, t = np.arange(P)[:, None], np.arange(P)[None, :]
    for L in range(LEVELS):
        masks[:, L] = (s >> (L + 1) == t >> (L + 1)) & ((s >> L) % 2 == 0) & ((t >> L) % 2 == 1)
    masks[:, LEVELS] = s == t
    half = HD // 2
    freq = (np.float32(10000.0) ** (-np.arange(half, dtype=np.float32) / np.float32(half))).astype(np.float32)
    ang = np.arange(S, dtype=np.float32)[None, :] * freq[np.arange(P) % half][:, None]
    sign = np.where(np.arange(P) % HD < half, -1.0, 1.0)[:, None]
    trig = np.stack([np.cos(ang), np.sin(ang) * sign]).astype(np.float32)
    return bias.reshape(P, TT * P), masks.reshape(P, -1), trig


def kernel(x, mix_norm, ffn_norm, w_in_rec, conv_w, hgrn_lb, hgrn_norm, w_out_rec, w_qkv_attn, w_o_attn,
           w_ffn_in, w_ffn_out, final_norm):
    import concourse.bacc as bacc
    from concourse.bass_utils import run_bass_kernel_spmd

    x, mix_norm, ffn_norm, w_in_rec, conv_w, hgrn_lb, hgrn_norm, w_out_rec, w_qkv_attn, w_o_attn, w_ffn_in, \
        w_ffn_out, final_norm = (np.asarray(a) for a in (
            x, mix_norm, ffn_norm, w_in_rec, conv_w, hgrn_lb, hgrn_norm, w_out_rec, w_qkv_attn, w_o_attn,
            w_ffn_in, w_ffn_out, final_norm))
    bias, masks, trig = constants()
    cols = lambda a: a.reshape(-1, P).T
    params = np.concatenate([cols(mix_norm), cols(ffn_norm), cols(final_norm), cols(conv_w[0]), cols(hgrn_lb),
                             cols(hgrn_norm[0])], axis=1)
    b_, c_, v_, q_, f_, i_, g_ = (w_in_rec[0][:, n * S:(n + 1) * S] for n in range(7))
    b_, c_, v_ = (blocks(w) for w in (b_, c_, v_))
    conv = np.stack([c_, v_, b_], axis=1).reshape(3 * HG, P, UNIT)
    w_rec = np.concatenate([token_major_units(i_), blocks(f_), blocks(q_), blocks(g_), conv])
    w_or = np.concatenate([blocks(w_out_rec[0][h * S:(h + 1) * S]).reshape(4, 2, P, S).transpose(0, 2, 1, 3)
                           .reshape(4, P, UNIT) for h in range(2)])
    q_, k_, v_ = (w_qkv_attn[0][:, n * D:(n + 1) * D] for n in range(3))
    w_qkv = np.concatenate([token_major_units(v_), np.stack([blocks(q_), blocks(k_)], axis=1).reshape(2 * KT, P, UNIT)])
    w_oa = blocks(w_o_attn[0])
    w_fi = [np.stack([blocks(w[:, :FF]), blocks(w[:, FF:])], axis=1).reshape(2 * FT, P, UNIT) for w in w_ffn_in]
    w_fo = []
    for w in w_ffn_out:
        padded = np.zeros((KT, 4, P, max(FO_TILES) * P), w.dtype)
        whole, k0 = blocks(w), 0
        for s, tiles in enumerate(FO_TILES):
            padded[:, s, :, :tiles * P] = whole[:, :, k0 * P:(k0 + tiles) * P]
            k0 += tiles
        w_fo.append(padded.reshape(4 * KT, P, -1))

    arrays = {
        "x_in": x[0].T.reshape(KT, P, S).transpose(1, 0, 2), "params": params, "ident": np.eye(P, dtype=np.float32),
        "score_bias": bias, "level_masks": masks, "trig": trig, "w_rec": w_rec, "w_or": w_or, "w_fi0": w_fi[0],
        "w_fi1": w_fi[1], "w_fo0": w_fo[0], "w_fo1": w_fo[1], "w_qkv": w_qkv, "w_oa": w_oa,
    }
    arrays = {name: np.ascontiguousarray(a) for name, a in arrays.items()}
    nc = bacc.Bacc("TRN2", target_bir_lowering=False, num_devices=1)
    t = {name: nc.dram_tensor(name, a.shape, mybir.dt.from_np(a.dtype), kind="ExternalInput").ap()
         for name, a in arrays.items()}
    out = nc.dram_tensor("out", (KT, P, S), F32, kind="ExternalOutput").ap()
    trunk(nc, t["x_in"], t["params"], t["ident"], t["score_bias"], t["level_masks"], t["trig"], t["w_rec"],
          t["w_or"], [t["w_fi0"], t["w_fi1"]], [t["w_fo0"], t["w_fo1"]], t["w_qkv"], t["w_oa"], out)
    r = run_bass_kernel_spmd(nc, [arrays], core_ids=[0])
    return r.results[0]["out"].reshape(D, S).T[None]
```

```python
from contextlib import ExitStack

import numpy as np

import concourse.bass as bass
from concourse import mybir
from concourse.bass import ds

ALU = mybir.AluOpType
ACT = mybir.ActivationFunctionType
F32 = mybir.dt.float32
F32R = mybir.dt.float32r
U8 = mybir.dt.uint8

P = 128
S = 512
D = 1024
KT = D // P
TT = S // P
HG = 4
HEADS, HD = 16, 64
PAIRS = HEADS // 2
FF = 2816
FT = FF // P
EPS = 1e-6
CONV_W = 3
LEVELS = 7
QSCALE = -(HD ** -0.5)

RING, AHEAD = 4, 3
UNIT = 1024
FO_TILES = (6, 6, 5, 5)
assert sum(FO_TILES) == FT

U_REC = 0
U_WOR = U_REC + 28
U_FI = [U_WOR + 8, 0]
U_FO = [U_FI[0] + 2 * FT, 0]
U_QKV = U_FO[0] + 4 * KT
U_WOA = U_QKV + 24
U_FI[1] = U_WOA + 8
U_FO[1] = U_FI[1] + 2 * FT
U_END = U_FO[1] + 4 * KT
assert all(u % RING == 0 for u in (U_WOR, *U_FI, *U_FO, U_QKV, U_WOA, U_END))

E_REC = 0
E_WOR = E_REC + 24
E_FI = [E_WOR + 16, 0]
E_FO = [E_FI[0] + 2 * FT, 0]
E_QKV = E_FO[0] + KT
E_WOA = E_QKV + 2 * PAIRS
E_FI[1] = E_WOA + KT
E_FO[1] = E_FI[1] + 2 * FT

C_MIX, C_FFN, C_FIN, C_CONV, C_LB, C_HN = 0, 16, 32, 40, 52, 64
N_PARAMS = 65

DIAG_STEP = 12
LEVEL_STEP = [13, 13, 14, 14, 15, 15, 16, 17, 18, 19, 20, 21, 22, 23]
TAIL = 24

class Positions:
    def __init__(self, qk, bias, exp, norm, turn, probs, pv):
        self.qk = qk
        self.bias = [q + bias for q in qk]
        self.exp = [q + exp for q in qk]
        self.norm = [q + norm for q in qk]
        self.turn = [q + turn for q in qk]
        self.probs = [q + probs for q in qk]
        self.values, self.pv, self.out = 3, pv, pv + 1


ATT = Positions([6, 8, 9, 11, 12, 14, 15, 17], 1, 3, 6, 8, 9, 28)
LAST_ATT = Positions([6 + n for n in range(8)], 1, 2, 3, 4, 5, 19)
PEELED = 4
SWAP, ROPE = 0, 4
WOA_BANK = (0, 3, 1)
WOA_SLOTS = ([(k, n) for k in range(3) for n in range(2)] + [(k, 2) for k in range(3)]
             + [(k, n) for k in range(3, KT) for n in range(3)])


def unit_cols(u):
    for base in U_FO:
        if base <= u < base + 4 * KT:
            return FO_TILES[u % 4] * P
    return UNIT


class Chain:

    def __init__(self, eng, sem):
        self.eng, self.sem, self.n, self.shift = eng, sem, 0, 0

    def mark(self, ins):
        ins.then_inc(self.sem, 1)
        self.n += 1

    def fence(self):
        self.eng.wait_ge(self.sem, self.shift + self.n)

    def loop(self, i, first, per_round):
        self.shift, self.start, self.per = (i - first) * per_round, self.n, per_round

    def done(self, rounds):
        assert self.n - self.start == self.per, (self.n - self.start, self.per)
        self.shift, self.n = 0, self.start + rounds * self.per


def wait(eng, sem, value):
    if not isinstance(value, int) or value > 0:
        eng.wait_ge(sem, value)


def trunk(nc, x_in, params_in, ident_in, bias_in, masks_in, trig_in, w_rec, w_or, w_fi, w_fo, w_qkv,
          w_oa, out):
    with ExitStack() as ctx:
        def sem(name):
            return ctx.enter_context(nc.semaphore(name))

        base, sbuf_end = {"at": -(-nc.sbuf_base // 32) * 32}, nc.sbuf_top
        ctx.enter_context(nc.sbuf_tensor("arena", [P, (nc.sbuf_top - base["at"]) // 4], F32))

        def sb(name, cols, dt=F32, at=None):
            size = cols * (1 if dt == U8 else 4)
            if at is None:
                at = base["at"]
                base["at"] += -(-size // 32) * 32
            return nc.alloc_sbuf_tensor_at(name, [P, cols], dt, offset=at), at

        x, _ = sb("x", KT * S)
        w_raw, _ = sb("w_raw", RING * UNIT)
        w_hi, _ = sb("w_hi", RING * UNIT, F32R)
        w_lo, _ = sb("w_lo", RING * UNIT, F32R)
        y_hi, at_y = sb("y_hi", KT * S, F32R)
        y_lo, _ = sb("y_lo", KT * S, F32R)
        act_hi, at_b = sb("act_hi", FT * S, F32R)
        act_lo, _ = sb("act_lo", FT * S, F32R)
        rstd, _ = sb("rstd", S)
        sq, _ = sb("sq", 2 * S)
        sq_sum, _ = sb("sq_sum", S)
        ident, _ = sb("ident", P)
        ones_d, _ = sb("ones_d", 1)
        ones_h, _ = sb("ones_h", 1)
        ones, _ = sb("ones", P)
        eps, _ = sb("eps", 1)
        masks, _ = sb("masks", (LEVELS + 1) * P, U8)
        params, _ = sb("params", N_PARAMS)
        lb_e, _ = sb("lb_e", 12)
        lb_s, _ = sb("lb_s", 4)
        lb, _ = sb("lb", 4)
        one_lb, _ = sb("one_lb", 4)
        rstd_tok, _ = sb("rstd_tok", TT)
        rstd_head, _ = sb("rstd_head", HG * TT)
        neg_max, _ = sb("neg_max", 8)
        denom, _ = sb("denom", 8)
        recip, _ = sb("recip", 8)
        wait_carrier, _ = sb("wait_carrier", 8)
        at_t = base["at"]
        t_slot = [at_t + n * 2080 for n in range(6)]
        gate_t = [sb(f"gate_t{n}", S, at=t_slot[n])[0] for n in range(2)]
        silu_t = [sb(f"silu_t{n}", S, at=t_slot[2 + n])[0] for n in range(2)]
        up_t = [sb(f"up_t{n}", S, at=t_slot[4 + n])[0] for n in range(2)]
        conv_u, _ = sb("conv_u", S + CONV_W - 1, at=t_slot[0])
        conv_c, _ = sb("conv_c", S, at=t_slot[1])
        conv_y, _ = sb("conv_y", S, at=t_slot[2])
        conv_b, _ = sb("conv_b", S, at=t_slot[3])
        cos_k, _ = sb("cos_k", S, at=t_slot[0])
        sin_k, _ = sb("sin_k", S, at=t_slot[1])
        cos_q, _ = sb("cos_q", S, at=t_slot[2])
        sin_q, _ = sb("sin_q", S, at=t_slot[3])
        bias, _ = sb("bias", S, at=t_slot[4])
        swapped, _ = sb("swapped", S, at=t_slot[5])
        assert t_slot[5] + 2080 <= sbuf_end, (t_slot, sbuf_end)

        big = HG * S
        hq, hp, hk, hsg, hv, hat, hsc = (sb(n, big, at=at_b + m * big * 4)[0] for m, n in enumerate(
            ("hg_q", "hg_logf", "hg_k", "hg_gate", "hg_v", "hg_hat", "hg_scores")))
        masks_f, _ = sb("masks_f", (LEVELS + 1) * P, at=at_b + 6 * big * 4)
        mix_hi, _ = sb("mix_hi", KT * S, F32R, at=at_b + 7 * big * 4)
        mix_lo, _ = sb("mix_lo", KT * S, F32R, at=at_b + 9 * big * 4)
        state, _ = sb("hg_state", 3 * S, at=at_b + 2 * big * 4)
        khat_t, _ = sb("hg_khat_t", 3 * S, at=at_b + 5 * big * 4)
        ho, ho_sq, ho_gated = (sb(n, big, at=at_y + m * big * 4)[0] for m, n in enumerate(
            ("hg_o", "hg_o_sq", "hg_o_gated")))
        ho_diag, _ = sb("hg_o_diag", big, at=at_b + big * 4)
        o_hi, _ = sb("o_hi", KT * S, F32R, at=at_b)
        o_lo, _ = sb("o_lo", KT * S, F32R, at=at_b + 16384)
        v_tok, _ = sb("v_tok", TT * D, at=at_b + 32768)
        pt = [sb(f"probs_t{e}", TT * S, at=at_b + 49152 + e * 8192)[0] for e in range(2)]
        q_t = [sb(f"q_t{n}", S, at=at_b + 65536 + n * 2048)[0] for n in range(2)]
        k_t = [sb(f"k_t{n}", S, at=at_b + 69632 + n * 2048)[0] for n in range(2)]
        v_pair = [sb(f"v_pair{n}", TT * P, at=at_b + 73728 + n * 2048)[0] for n in range(2)]
        s_sb = [sb(f"scores{n}", S, at=at_b + 77824 + n * 2048)[0] for n in range(2)]
        prob = [sb(f"probs{n}", S, at=at_b + 81920 + n * 2048)[0] for n in range(4)]
        y_fin, _ = sb("y_fin", KT * S, at=at_y)

        G = [ctx.enter_context(nc.psum_tensor(f"gemm{n}", [P, S], F32)) for n in range(4)]
        aux = ctx.enter_context(nc.psum_tensor("aux", [P, 4 * S], F32))

        def A(bank, c0=0, n=S):
            return aux[:, bank * S + c0:bank * S + c0 + n]


        w_loaded = [sem(f"w_loaded{n}") for n in range(RING)]
        hi_ready = sem("hi_ready")
        lo_ready = sem("lo_ready")
        unit_done = sem("unit_done")
        evacuated = sem("evacuated")
        x_loaded = [sem(f"x_loaded{n}") for n in range(KT // 2)]
        params_loaded, consts_loaded, trig_loaded = sem("params_loaded"), sem("consts_loaded"), sem("trig_loaded")
        ones_set = sem("ones_set")
        masks_ready = sem("masks_ready")
        yh_ready, y_ready = sem("yh_ready"), sem("y_ready")
        sq_ready, sq_added = sem("sq_ready"), sem("sq_added")
        ms_ready = sem("ms_ready")
        root_ready = sem("root_ready")
        diag_ready = sem("diag_ready")
        spread_ready = sem("spread_ready")
        rstd_ready = sem("rstd_ready")
        v_ready = sem("v_ready")
        dve_chain = sem("dve_chain")
        lb_shifted, lb_exp, lb_ready = sem("lb_shifted"), sem("lb_exp"), sem("lb_ready")
        sig_ready = sem("sig_ready")
        f_ready = sem("f_ready")
        hk_ready = sem("hk_ready")
        logf_ready = sem("logf_ready")
        diff_ready, exp_ready = sem("diff_ready"), sem("exp_ready")
        hat_ready = sem("hat_ready")
        raw_scored, merged = sem("raw_scored"), sem("merged")
        conv_ready, mixh_ready, mix_ready = sem("conv_ready"), sem("mixh_ready"), sem("mix_ready")
        tail_diff, tail_exp, khat_ready, qhat_ready = (
            sem("tail_diff"), sem("tail_exp"), sem("khat_ready"), sem("qhat_ready"))
        khat_turned, khat_copied = sem("khat_turned"), sem("khat_copied")
        kv_ready, state_ready, o_ready, o_taken = sem("kv_ready"), sem("state_ready"), sem("o_ready"), sem("o_taken")
        silu_g_ready = sem("silu_g_ready")
        gain_ready, gated_ready = sem("gain_ready"), sem("gated_ready")
        oms_ready, oroot_ready, odiag_ready, ospread_ready, onorm_ready = (
            sem("oms_ready"), sem("oroot_ready"), sem("odiag_ready"), sem("ospread_ready"), sem("onorm_ready"))
        silu_ready, prod_ready = sem("silu_ready"), sem("prod_ready")
        acth_ready, act_ready = sem("acth_ready"), sem("act_ready")
        swap_ready = sem("swap_ready")
        vp_ready = sem("vp_ready")
        scored, biased, expd = sem("scored"), sem("biased"), sem("expd")
        normed, turned, pt_ready = sem("normed"), sem("turned"), sem("pt_ready")
        pv_done, oh_ready, o_split = sem("pv_done"), sem("oh_ready"), sem("o_split")
        out_ready, out_ready_pool, out_stored = sem("out_ready"), sem("out_ready_pool"), sem("out_stored")

        OUT_POOL = (2, 5)
        OUT_DVE = [n for n in range(KT) if n not in OUT_POOL]

        block = ctx.enter_context(nc.Block())

        def wslot(t, u, c0=0, n=None):
            s0 = (u % RING) * UNIT + c0
            return t[:, s0:s0 + (unit_cols(u) if n is None else n)]

        @block.sync
        def _(sp):
            def load(src, unit, slot, cols):
                sp.dma_start(w_raw[:, slot * UNIT:slot * UNIT + cols], src[unit, :, 0:cols]).then_inc(w_loaded[slot], 16)

            def loads(src, base_u, count):
                first = RING if base_u == 0 else 0
                for u in range(first):
                    load(src, u, u % RING, unit_cols(base_u + u))
                with sp.Fori(first // RING, count // RING) as i:
                    for s in range(RING):
                        sp.wait_ge(lo_ready, i * RING + (base_u + s + 1 - RING))
                        cols = unit_cols(base_u + s)
                        sp.dma_start(w_raw[:, s * UNIT:s * UNIT + cols],
                                     src[ds(i * RING + s, 1), :, 0:cols].rearrange("o p c -> (o p) c")
                                     ).then_inc(w_loaded[s], 16)

            loads(w_rec, U_REC, 28)
            loads(w_or, U_WOR, 8)
            loads(w_fi[0], U_FI[0], 2 * FT)
            loads(w_fo[0], U_FO[0], 4 * KT)
            loads(w_qkv, U_QKV, 24)
            loads(w_oa, U_WOA, 8)
            loads(w_fi[1], U_FI[1], 2 * FT)
            loads(w_fo[1], U_FO[1], 4 * KT)
            for n in range(KT):
                if n in OUT_POOL:
                    sp.wait_ge(out_ready_pool, OUT_POOL.index(n) + 1)
                else:
                    sp.wait_ge(out_ready, OUT_DVE.index(n) + 1)
                sp.dma_start(out[n], y_fin[:, n * S:(n + 1) * S]).then_inc(out_stored, 16)
            sp.wait_ge(out_stored, 16 * KT)

        @block.gpsimd
        def _(pool):
            nc.gpsimd.memset(ones_d[:], 1.0 / D).then_inc(ones_set, 1)
            nc.gpsimd.memset(ones_h[:], 1.0 / P).then_inc(ones_set, 1)
            nc.gpsimd.memset(ones[:], 1.0).then_inc(ones_set, 1)
            nc.gpsimd.memset(eps[:], EPS).then_inc(ones_set, 1)

            def add_squares(m, first, n, buf):
                src = sq[:, buf * S:(buf + 1) * S]
                pool.wait_ge(sq_ready, 8 * m + n + 1)
                if first:
                    wait(pool, ms_ready, m)
                    nc.gpsimd.tensor_copy(sq_sum[:], src).then_inc(sq_added, 1)
                else:
                    pool.wait_ge(sq_added, 8 * m + n)
                    nc.gpsimd.tensor_tensor(sq_sum[:], sq_sum[:], src, ALU.add).then_inc(sq_added, 1)

            def sum_squares(m):
                add_squares(m, True, 0, 0)
                add_squares(m, False, 1, 1)
                with pool.Fori(1, KT // 2) as i:
                    for r in range(2):
                        add_squares(m, False, 2 * i + r, r)

            sum_squares(0)
            pool.wait_ge(consts_loaded, 32)
            nc.gpsimd.tensor_copy(masks[:], masks_f[:]).then_inc(masks_ready, 1)
            pool.wait_ge(silu_g_ready, 1)
            nc.gpsimd.tensor_scalar(hsg[:], hsg[:], params[:, C_HN:C_HN + 1], None, ALU.mult).then_inc(gain_ready, 1)
            pool.wait_ge(gain_ready, 1)
            for h in range(HG):
                blk = slice(h * S, (h + 1) * S)
                pool.wait_ge(o_taken, 2 * h + 1)
                nc.gpsimd.tensor_tensor(ho_gated[:, blk], ho[:, blk], hsg[:, blk], ALU.mult).then_inc(gated_ready, 1)
            for m in range(1, 5):
                sum_squares(m)
            pool.wait_ge(rstd_ready, 5)
            pool.wait_ge(yh_ready, 5 * KT)
            for n in OUT_POOL:
                tile = slice(n * S, (n + 1) * S)
                nc.gpsimd.tensor_tensor(y_fin[:, tile], y_fin[:, tile], rstd[:], ALU.mult).then_inc(out_ready_pool, 1)

        def halves(t, a, L):
            h = 1 << L
            v = t[:, a * 2 * S:(a + 1) * 2 * S].rearrange("p (n two h) -> p n two h", two=2, h=h)
            return v[:, :, 0, :], v[:, :, 1, :]

        def events(step):
            return ([0, 1] if step == DIAG_STEP else []) + [
                2 + e for e in range(2 * LEVELS) if LEVEL_STEP[e] == step]


        @block.scalar
        def _(act):
            def split_hi(u, shift=0):
                s = u % RING
                cols = unit_cols(u)
                act.wait_ge(w_loaded[s], shift * (16 // RING) + 16 * (u // RING + 1))
                wait(act, unit_done, shift + (u + 1 - RING))
                nc.scalar.copy(wslot(w_hi, u, 0, cols), wslot(w_raw, u, 0, cols)).then_inc(hi_ready, 1)

            def square(m, n, buf, waited=False):
                if not waited:
                    wait(act, sq_added, 8 * m + n - 1)
                nc.scalar.activation(sq[:, buf * S:(buf + 1) * S], x[:, ds(n * S, S)], ACT.Square
                                     ).then_inc(sq_ready, 1)

            def gain_tile(gain, n, out_t):
                nc.scalar.mul(out_t[:, ds(n * S, S)], x[:, ds(n * S, S)], params[:, ds(n + gain, 1)]
                              ).then_inc(yh_ready, 1)

            def norm_tile(m, gain, n, buf, out_t=y_hi):
                wait(act, sq_added, 8 * m + n - 1)
                gain_tile(gain, n, out_t)
                square(m, n, buf, waited=True)

            def rstd_root(m, bank):
                act.wait_ge(ms_ready, m + 1)
                nc.scalar.activation(rstd_tok[:], bank[:, 0:TT], ACT.Sqrt, bias=eps[:]).then_inc(root_ready, 1)

            def rstd_copy(m, bank):
                act.wait_ge(spread_ready, m + 1)
                nc.scalar.copy(rstd[:], bank).then_inc(rstd_ready, 1)

            def prologue():
                act.dma_start(params[:], params_in).then_inc(params_loaded, 16)
                for c in range(KT // 2):
                    act.dma_start(x[:, c * 2 * S:(c + 1) * 2 * S].rearrange("p (t s) -> p t s", t=2),
                                  x_in[:, 2 * c:2 * c + 2, :]).then_inc(x_loaded[c], 16)
                act.dma_start(ident[:], ident_in).then_inc(consts_loaded, 16)
                act.dma_start(masks_f[:], masks_in).then_inc(consts_loaded, 16)
                act.wait_ge(params_loaded, 16)
                act.wait_ge(x_loaded[0], 16)
                gain_tile(C_MIX, 0, y_hi)
                split_hi(0)
                for n in range(1, KT):
                    act.wait_ge(x_loaded[n // 2], 16)
                    gain_tile(C_MIX, n, y_hi)
                    if n in (1, 3):
                        split_hi(n // 2 + 1)
                act.wait_ge(ones_set, 4)
                for n in range(KT):
                    square(0, n, n % 2)
                act.wait_ge(lb_shifted, 3)
                nc.scalar.activation(lb_e[:], lb_e[:], ACT.Exp).then_inc(lb_exp, 1)

            def level_exps(e):
                L, a = divmod(e, 2)
                lo, hi = halves(hat, a, L)
                act.wait_ge(diff_ready, e + 1)
                if L:
                    nc.scalar.activation(lo, lo, ACT.Exp)
                nc.scalar.activation(hi, halves(hp, a, L)[1], ACT.Exp).then_inc(exp_ready, 1)

            def conv_hi(j):
                act.wait_ge(conv_ready, j + 1)
                nc.scalar.copy(mix_hi[:, j * S:(j + 1) * S], conv_y[:]).then_inc(mixh_ready, 1)

            def mixer():
                for step in range(0, 36 + 1):
                    if step == 4:
                        rstd_root(0, G[3])
                    split_hi(step + AHEAD)
                    if step == 4:
                        rstd_copy(0, G[2][:])
                        act.wait_ge(unit_done, 4)
                        act.wait_ge(diag_ready, 1)
                        for t in range(TT):
                            nc.scalar.activation(hv[:, t * S:(t + 1) * S], A(t), ACT.Silu,
                                                 scale=rstd_tok[:, t:t + 1]).then_inc(v_ready, 1)
                    if step == 8:
                        act.wait_ge(evacuated, E_REC + HG)
                        nc.scalar.activation(hp[:], hk[:], ACT.Sigmoid).then_inc(sig_ready, 1)
                        nc.scalar.activation(hk[:], hk[:], ACT.Sigmoid, scale=-1.0).then_inc(sig_ready, 1)
                    if step == 9:
                        act.wait_ge(f_ready, HG)
                        nc.scalar.activation(hp[:], hp[:], ACT.Ln).then_inc(logf_ready, 1)
                    for x_ in events(step):
                        if x_ >= 2:
                            level_exps(x_ - 2)
                    if step == 16:
                        act.wait_ge(evacuated, E_REC + 3 * HG)
                        nc.scalar.activation(hsg[:], hsg[:], ACT.Silu).then_inc(silu_g_ready, 1)
                    if step == TAIL:
                        act.wait_ge(tail_diff, 1)
                        nc.scalar.activation(hat[:], hat[:], ACT.Exp).then_inc(tail_exp, 1)
                        nc.scalar.activation(hp[:], hp[:], ACT.Exp).then_inc(tail_exp, 1)
                    if step == TAIL + 2:
                        act.wait_ge(khat_turned, 1)
                        for c in range(3):
                            nc.scalar.copy(khat_t[:, c * S:(c + 1) * S], A(c)).then_inc(khat_copied, 1)
                    for j in range(HG):
                        if step == 19 + 3 * j:
                            conv_hi(j)
                    if step == TAIL + 4:
                        for h in range(HG):
                            act.wait_ge(o_ready, h + 1)
                            nc.scalar.copy(ho[:, h * S:(h + 1) * S], A(h)).then_inc(o_taken, 1)
                            nc.scalar.activation(ho_sq[:, h * S:(h + 1) * S], A(h), ACT.Square).then_inc(o_taken, 1)
                    if step == TAIL + 5:
                        act.wait_ge(oms_ready, 1)
                        nc.scalar.activation(rstd_head[:], A(0, 0, HG * TT), ACT.Sqrt, bias=eps[:]).then_inc(oroot_ready, 1)
                    if step == TAIL + 6:
                        for h in range(HG):
                            act.wait_ge(onorm_ready, h + 1)
                            nc.scalar.copy(mix_hi[:, (HG + h) * S:(HG + h + 1) * S], ho[:, h * S:(h + 1) * S]
                                           ).then_inc(mixh_ready, 1)
                    if step > U_WOR + 4:
                        for n in (2 * (step - U_WOR - 5), 2 * (step - U_WOR - 5) + 1):
                            act.wait_ge(evacuated, E_WOR + 8 + n + 1)
                            norm_tile(1, C_FFN, n, n % 2)

            def ffn_in(l):
                rstd_root(1 + 2 * l, A(3))
                rstd_copy(1 + 2 * l, A(2))

                def body(i, last):
                    for s in range(1, 5):
                        u = U_FI[l] + s + AHEAD
                        split_hi(u + 4 * i if last else u, 0 if last else 4 * i)
                        j, k = (s - 1) // 2, FT * l + 2 * i + (s - 1) // 2
                        if s % 2:
                            act.wait_ge(evacuated, E_FI[l] + 4 * i + s)
                            nc.scalar.activation(silu_t[j][:], gate_t[j][:], ACT.Silu).then_inc(silu_ready, 1)
                        else:
                            act.wait_ge(prod_ready, k + 1)
                            nc.scalar.copy(act_hi[:, ds((2 * i + j) * S, S)], up_t[j][:]).then_inc(acth_ready, 1)

                with act.Fori(0, FT // 2 - 1) as i:
                    body(i, False)
                body(FT // 2 - 1, True)

            def ffn_out(l):
                def body(i, last):
                    for s in range(1, 9):
                        u = U_FO[l] + s + AHEAD
                        if not last:
                            split_hi(u, 8 * i)
                        elif u + 8 * i < U_END:
                            split_hi(u + 8 * i)
                        if s % 4 == 0:
                            n = 2 * i + (s // 4 - 1)
                            act.wait_ge(evacuated, E_FO[l] + n + 1)
                            if l == 0:
                                norm_tile(2, C_MIX + KT, n, s // 4 - 1)
                            elif not last:
                                norm_tile(4, C_FIN, n, s // 4 - 1, y_fin)
                            else:
                                square(4, n, s // 4 - 1)
                                gain_tile(C_FIN, n, y_fin)

                with act.Fori(0, KT // 2 - 1) as i:
                    body(i, False)
                body(KT // 2 - 1, True)

            def swap(k, bank, g):
                if g == 0:
                    act.wait_ge(unit_done, k + (U_QKV + 8 + 1))
                    wait(act, evacuated, k + E_QKV)
                nc.scalar.copy(swapped[32 * (g ^ 1):32 * (g ^ 1) + 32, :], G[bank][32 * g:32 * g + 32, :]
                               ).then_inc(swap_ready, 1)

            def attend(q, par, pos, tab):
                if pos == tab.values:
                    wait(act, pv_done, q - 1)
                    src = v_tok[:].rearrange("s (j c) -> s j c", j=TT)[:, :, ds(q * P, P)]
                    nc.scalar.copy(v_pair[par][:].rearrange("s (j c) -> s j c", j=TT), src).then_inc(vp_ready, 1)
                for n in range(8):
                    t = n % 4
                    w = (t + 1) * P
                    if pos == tab.probs[n]:
                        act.wait_ge(turned, 8 * q + n + 1)
                        if t == 0:
                            wait(act, pv_done, q)
                        dst = pt[n // 4][:].rearrange("s (j t) -> s j t", j=TT)[:, 0:t + 1, t * P:w]
                        nc.scalar.copy(dst, A(2 + n % 2, 0, w).rearrange("s (j t) -> s j t", j=t + 1)
                                       ).then_inc(pt_ready, 1)
                for n in range(8):
                    t = n % 4
                    w = (t + 1) * P
                    if pos == tab.exp[n]:
                        act.wait_ge(biased, 8 * q + n + 1)
                        wait(act, turned, 8 * q + n - 3)
                        nc.scalar.activation(prob[t][:, 0:w], s_sb[n % 2][:, 0:w], ACT.Exp,
                                             bias=neg_max[:, n:n + 1], scale=-1.0,
                                             accum_out=denom[:, n:n + 1]).then_inc(expd, 1)
                if pos == tab.out:
                    act.wait_ge(pv_done, q + 1)
                    nc.scalar.copy(o_hi[:, ds(q * S, S)], G[2][:]).then_inc(oh_ready, 1)

            def values(half):
                for t in range(TT):
                    src = A(t) if half == 0 else G[t][:]
                    nc.scalar.activation(v_tok[:, t * D + half * S:t * D + half * S + S], src, ACT.Copy,
                                         scale=rstd_tok[:, t:t + 1]).then_inc(v_ready, 1)

            def pair(p, ps, shift=0):
                for s in range(16):
                    if s % 8 == 0:
                        split_hi(U_QKV + 8 + ps * 2 + s // 8 + AHEAD, shift)
                    if s == 0 and ps == 0:
                        act.wait_ge(unit_done, U_QKV + 8)
                        values(1)
                    if SWAP <= s < SWAP + 4 and ps > 0:
                        swap(2 * p - 1, 1, s - SWAP)
                    if 8 + SWAP <= s < 8 + SWAP + 4:
                        swap(2 * p, 0, s - 8 - SWAP)
                    if ps > 1:
                        attend(p - 2, ps % 2, s + 16, ATT)
                    if ps > 0:
                        attend(p - 1, (ps + 1) % 2, s, ATT)

            def attention():
                act.wait_ge(act_ready, FT)
                act.dma_start(cos_k[:], trig_in[0]).then_inc(trig_loaded, 16)
                act.dma_start(sin_k[:], trig_in[1]).then_inc(trig_loaded, 16)
                act.dma_start(bias[:], bias_in).then_inc(trig_loaded, 16)
                rstd_root(2, G[3])
                for s in range(1, 8):
                    split_hi(U_QKV + s + AHEAD)
                    if s == 1:
                        rstd_copy(2, G[2][:])
                    if s == 4:
                        act.wait_ge(unit_done, U_QKV + 4)
                        act.wait_ge(diag_ready, 3)
                        values(0)
                for p in range(PEELED):
                    pair(p, p)
                with act.Fori(PEELED // 2, PAIRS // 2) as i:
                    for r in range(2):
                        pair(2 * i + r, PEELED + r, 4 * (i - PEELED // 2))
                split_hi(U_WOA + AHEAD)
                for s in range(24):
                    if SWAP <= s < SWAP + 4:
                        swap(2 * PAIRS - 1, 1, s - SWAP)
                    attend(PAIRS - 2, 0, s + 16, ATT)
                    attend(PAIRS - 1, 1, s, LAST_ATT)
                for s in range(1, 9):
                    split_hi(U_WOA + s + AHEAD)
                    act.wait_ge(evacuated, E_WOA + s)
                    norm_tile(3, C_FFN + KT, s - 1, (s - 1) % 2)

            prologue()
            mixer()
            ffn_in(0)
            ffn_out(0)
            attention()
            ffn_in(1)
            ffn_out(1)
            rstd_root(4, A(3))
            rstd_copy(4, A(2))

        @block.vector
        def _(dve):
            V = nc.vector
            chain = Chain(dve, dve_chain)

            def split_lo(u, shift=0):
                cols = unit_cols(u)
                dve.wait_ge(hi_ready, shift + (u + 1))
                V.tensor_tensor(wslot(w_lo, u, 0, cols), wslot(w_raw, u, 0, cols),
                                wslot(w_hi, u, 0, cols).bitcast(F32), ALU.subtract).then_inc(lo_ready, 1)

            def norm_tile(m, gain, n):
                dve.wait_ge(yh_ready, 8 * m + n + 1)
                V.scalar_tensor_tensor(out=y_lo[:, ds(n * S, S)], in0=x[:, ds(n * S, S)],
                                       scalar=params[:, ds(n + gain, 1)],
                                       in1=y_hi[:, ds(n * S, S)].bitcast(F32),
                                       op0=ALU.mult, op1=ALU.subtract).then_inc(y_ready, 1)

            def residual(n, unit, bank):
                dve.wait_ge(unit_done, unit + 1)
                xn = x[:, ds(n * S, S)]
                V.tensor_tensor(xn, xn, bank, ALU.add).then_inc(evacuated, 1)

            def diagonals(roots, diag, tiles):
                chain.mark(V.reciprocal(roots[:], roots[:]))
                chain.fence()
                shape = [P, tiles, P]
                return V.tensor_tensor(diag.rearrange("p (c t) -> p c t", t=P), ident[:].unsqueeze(1).broadcast_to(shape),
                                       roots[:].unsqueeze(2).broadcast_to(shape), ALU.mult)

            def inverse(m):
                dve.wait_ge(root_ready, m + 1)
                diagonals(rstd_tok, sq[:, 0:S], TT).then_inc(diag_ready, 1)

            def prologue():
                dve.wait_ge(params_loaded, 16)
                row = [params[:, C_LB + 4 * r:C_LB + 4 * r + 4] for r in range(3)]
                chain.mark(V.tensor_tensor(lb_s[:], row[0], row[1], ALU.max))
                chain.fence()
                chain.mark(V.tensor_tensor(lb_s[:], lb_s[:], row[2], ALU.max))
                chain.fence()
                for r in range(3):
                    V.tensor_tensor(lb_e[:, 4 * r:4 * r + 4], row[r], lb_s[:], ALU.subtract
                                    ).then_inc(lb_shifted, 1)
                split_lo(0)
                for n in range(KT):
                    if n % 2 == 0:
                        dve.wait_ge(x_loaded[n // 2], 16)
                    norm_tile(0, C_MIX, n)
                    if n in (1, 3):
                        split_lo(n // 2 + 1)
                dve.wait_ge(lb_exp, 1)
                chain.mark(V.tensor_tensor(one_lb[:], lb_e[:, 0:4], lb_e[:, 8:12], ALU.add))
                chain.fence()
                chain.mark(V.tensor_tensor(lb_s[:], one_lb[:], lb_e[:, 4:8], ALU.add))
                chain.fence()
                chain.mark(V.reciprocal(lb_s[:], lb_s[:]))
                chain.fence()
                V.tensor_tensor(lb[:], lb_e[:, 4:8], lb_s[:], ALU.mult).then_inc(lb_ready, 1)
                V.tensor_tensor(one_lb[:], one_lb[:], lb_s[:], ALU.mult).then_inc(lb_ready, 1)
                chain.mark(V.memset(conv_u[:, 0:CONV_W - 1], 0.0))

            def take(u, dst):
                dve.wait_ge(unit_done, u + 1)
                V.tensor_tensor(dst, G[u % 4][:], rstd[:], ALU.mult).then_inc(evacuated, 1)

            def level_diff(e):
                L, a = divmod(e, 2)
                h = 1 << L
                lo = halves(hat, a, L)[0]
                plo = halves(hp, a, L)[0]
                if L:
                    dve.wait_ge(raw_scored, 2 + e - 2 + 1)
                    chain.fence()
                    V.tensor_tensor(lo, plo[:, :, h - 1:h].broadcast_to(plo.shape), plo, ALU.subtract
                                    ).then_inc(diff_ready, 1)
                else:
                    V.tensor_copy(lo, halves(hk, a, L)[0]).then_inc(diff_ready, 1)

            def level_hat(e):
                L, a = divmod(e, 2)
                h = 1 << L
                lo, hi = halves(hat, a, L)
                plo, phi = halves(hp, a, L)
                dve.wait_ge(exp_ready, e + 1)
                if L:
                    V.tensor_tensor(lo, lo, halves(hk, a, L)[0], ALU.mult).then_inc(hat_ready, 1)
                V.tensor_tensor(hi, hi, halves(hq, a, L)[1], ALU.mult).then_inc(hat_ready, 1)
                chain.mark(V.tensor_tensor(phi, phi, plo[:, :, h - 1:h].broadcast_to(phi.shape), ALU.add))

            def merge(ev):
                dve.wait_ge(raw_scored, ev + 1)
                if ev < 2:
                    dst = hsc[:, ev * 2 * S:(ev + 1) * 2 * S].rearrange("p (m t) -> p m t", t=P)
                    src = aux[:, ev * 2 * S:(ev + 1) * 2 * S].rearrange("p (m t) -> p m t", t=P)
                    mask = masks[:, LEVELS * P:]
                    mask = mask.unsqueeze(1).broadcast_to(dst.shape)
                else:
                    L, a = divmod(ev - 2, 2)
                    dst = halves(hsc, a, L)[1].rearrange("p (m n) h -> p m n h", m=8)
                    src = halves(aux, a, L)[1].rearrange("p (m n) h -> p m n h", m=8)
                    mask = masks[:, L * P:(L + 1) * P].rearrange("p (n two h) -> p n two h", two=2, h=1 << L)
                    mask = mask[:, :, 1, :].unsqueeze(1).broadcast_to(dst.shape)
                    dve.wait_ge(merged, ev - 1)
                V.copy_predicated(dst, mask, src).then_inc(merged, 1)

            def conv(j, part, u):
                if part == 0:
                    take(u, conv_c[:])
                elif part == 1:
                    take(u, conv_u[:, 2:])
                    dve.wait_ge(evacuated, E_REC + 12 + 3 * j + 2)
                    chain.mark(V.tensor_tensor(conv_u[:, 2:], conv_u[:, 2:], conv_c[:], ALU.mult))
                    wait(dve, mixh_ready, j)
                    chain.fence()
                    for tap in range(CONV_W - 1, -1, -1):
                        w = params[:, C_CONV + 4 * tap + j:C_CONV + 4 * tap + j + 1]
                        src = conv_u[:, tap:tap + S]
                        if tap == CONV_W - 1:
                            chain.mark(V.tensor_scalar(conv_y[:], src, w, None, ALU.mult))
                        else:
                            chain.mark(V.scalar_tensor_tensor(out=conv_y[:], in0=src, scalar=w, in1=conv_y[:],
                                                              op0=ALU.mult, op1=ALU.add))
                        chain.fence()
                else:
                    take(u, conv_b[:])
                    dve.wait_ge(evacuated, E_REC + 12 + 3 * j + 3)
                    V.tensor_tensor(conv_y[:], conv_y[:], conv_b[:], ALU.mult).then_inc(conv_ready, 1)

            def mix_split(k, src):
                dve.wait_ge(mixh_ready, k + 1)
                V.tensor_tensor(mix_lo[:, k * S:(k + 1) * S], src, mix_hi[:, k * S:(k + 1) * S].bitcast(F32),
                                ALU.subtract).then_inc(mix_ready, 1)

            def mixer():
                for step in range(0, 36 + 1):
                    if step == 4:
                        dve.wait_ge(consts_loaded, 32)
                        inverse(0)
                    split_lo(step + AHEAD)
                    pu = step - 1
                    if step == 5:
                        dve.wait_ge(rstd_ready, 1)
                    if step == DIAG_STEP:
                        dve.wait_ge(masks_ready, 1)
                        chain.mark(V.memset(hsc[:], 0.0))
                        dve.wait_ge(logf_ready, 1)
                        chain.fence()
                    for ev in events(step - 1):
                        merge(ev)
                    for ev in events(step):
                        if ev >= 2:
                            level_diff(ev - 2)
                    if 4 <= pu < 8:
                        h = pu - 4
                        take(pu, hk[:, h * S:(h + 1) * S])
                    elif 8 <= pu < 12:
                        h = pu - 8
                        take(pu, hq[:, h * S:(h + 1) * S])
                    elif 12 <= pu < 16:
                        h = pu - 12
                        take(pu, hsg[:, h * S:(h + 1) * S])
                    elif 16 <= pu < 28:
                        conv((pu - 16) // 3, (pu - 16) % 3, pu)
                    if step == 9:
                        dve.wait_ge(sig_ready, 2)
                        dve.wait_ge(lb_ready, 2)
                        for h in range(HG):
                            blk = slice(h * S, (h + 1) * S)
                            V.tensor_scalar(hp[:, blk], hp[:, blk], one_lb[:, h:h + 1], lb[:, h:h + 1],
                                            ALU.mult, ALU.add).then_inc(f_ready, 1)
                        for h in range(HG):
                            blk = slice(h * S, (h + 1) * S)
                            V.tensor_scalar(hk[:, blk], hk[:, blk], one_lb[:, h:h + 1], None, ALU.mult
                                            ).then_inc(hk_ready, 1)
                    for ev in events(step):
                        if ev >= 2:
                            level_hat(ev - 2)
                    for j in range(HG):
                        if step == (20 + 3 * j if j < HG - 1 else 28):
                            mix_split(j, conv_y[:])
                    tail(step)
                    if step > U_WOR:
                        for n in (2 * (pu - U_WOR), 2 * (pu - U_WOR) + 1):
                            residual(n % KT, pu, G[n % 4][:])
                            if n >= KT:
                                norm_tile(1, C_FFN, n - KT)

            def tail(step):
                if step == TAIL:
                    dve.wait_ge(raw_scored, 2 + 2 * LEVELS)
                    chain.fence()
                    pv = hp[:].rearrange("p (m t) -> p m t", t=P)
                    V.tensor_tensor(hat[:].rearrange("p (m t) -> p m t", t=P),
                                    pv[:, :, P - 1:P].broadcast_to(pv.shape), pv, ALU.subtract
                                    ).then_inc(tail_diff, 1)
                if step == TAIL + 1:
                    dve.wait_ge(tail_exp, 2)
                    V.tensor_tensor(hat[:], hat[:], hk[:], ALU.mult).then_inc(khat_ready, 1)
                    V.tensor_tensor(hq[:], hq[:], hp[:], ALU.mult).then_inc(qhat_ready, 1)
                if step == TAIL + 3:
                    dve.wait_ge(kv_ready, 3)
                    chain.mark(V.tensor_copy(state[:, 0:S], A(3)))
                    for c in (1, 2):
                        prev, cur = state[:, (c - 1) * S:c * S], state[:, c * S:(c + 1) * S]
                        decay = hp[:].rearrange("p (h t) -> p h t", h=HG)[:, :, c * P + P - 1:c * P + P]
                        chain.fence()
                        chain.mark(V.tensor_tensor(cur.rearrange("p (h v) -> p h v", h=HG),
                                                   prev.rearrange("p (h v) -> p h v", h=HG),
                                                   decay.broadcast_to([P, HG, P]), ALU.mult))
                        chain.fence()
                        ins = V.tensor_tensor(cur, cur, A(c - 1), ALU.add)
                        if c == 1:
                            chain.mark(ins)
                        else:
                            ins.then_inc(state_ready, 1)
                if step == TAIL + 5:
                    dve.wait_ge(oroot_ready, 1)
                    diagonals(rstd_head, ho_diag[:], HG * TT).then_inc(odiag_ready, 1)
                if step == TAIL + 6:
                    dve.wait_ge(ospread_ready, 1)
                    for h in range(HG):
                        dve.wait_ge(gated_ready, h + 1)
                        V.tensor_tensor(ho[:, h * S:(h + 1) * S], ho_gated[:, h * S:(h + 1) * S], A(h), ALU.mult
                                        ).then_inc(onorm_ready, 1)
                    for h in range(HG):
                        mix_split(HG + h, ho[:, h * S:(h + 1) * S])

            def ffn_in(l):
                inverse(1 + 2 * l)
                dve.wait_ge(rstd_ready, 2 + 2 * l)

                def body(i, last):
                    for s in range(1, 5):
                        u = U_FI[l] + s + AHEAD
                        split_lo(u + 4 * i if last else u, 0 if last else 4 * i)
                        j, k = (s - 1) // 2, FT * l + 2 * i + (s - 1) // 2
                        dve.wait_ge(unit_done, U_FI[l] + 4 * i + s)
                        dst = (gate_t if s % 2 else up_t)[j]
                        V.tensor_tensor(dst[:], G[s - 1][:], rstd[:], ALU.mult).then_inc(evacuated, 1)
                        if s % 2 == 0:
                            dve.wait_ge(evacuated, E_FI[l] + 4 * i + s)
                            dve.wait_ge(silu_ready, k + 1)
                            V.tensor_tensor(dst[:], dst[:], silu_t[j][:], ALU.mult).then_inc(prod_ready, 1)
                            dve.wait_ge(acth_ready, k + 1)
                            tile = ds((2 * i + j) * S, S)
                            V.tensor_tensor(act_lo[:, tile], dst[:], act_hi[:, tile].bitcast(F32), ALU.subtract
                                            ).then_inc(act_ready, 1)

                with dve.Fori(0, FT // 2 - 1) as i:
                    body(i, False)
                body(FT // 2 - 1, True)

            def ffn_out(l):
                def body(i, last):
                    for s in range(1, 9):
                        u = U_FO[l] + s + AHEAD
                        if not last:
                            split_lo(u, 8 * i)
                        elif u + 8 * i < U_END:
                            split_lo(u + 8 * i)
                        if s % 4 == 0:
                            n = 2 * i + (s // 4 - 1)
                            residual(n, U_FO[l] + 8 * i + s - 1, G[s // 4 - 1][:])
                            if l == 0:
                                norm_tile(2, C_MIX + KT, n)

                with dve.Fori(0, KT // 2 - 1) as i:
                    body(i, False)
                body(KT // 2 - 1, True)

            def rope(k, bank, dst, cos, sin, free):
                wait(dve, scored, free)
                dve.wait_ge(swap_ready, 4 * (k + 1))
                chain.mark(V.tensor_tensor(dst[:], G[bank][:], cos[:], ALU.mult))
                chain.mark(V.tensor_tensor(swapped[:], swapped[:], sin[:], ALU.mult))
                chain.fence()
                V.tensor_tensor(dst[:], dst[:], swapped[:], ALU.add).then_inc(evacuated, 1)

            def attend(q, par, pos, tab):
                for n in range(8):
                    t = n % 4
                    w = (t + 1) * P
                    if pos == tab.norm[n]:
                        dve.wait_ge(expd, 8 * q + n + 1)
                        chain.mark(V.reciprocal(recip[:, n:n + 1], denom[:, n:n + 1]))
                        chain.fence()
                        V.tensor_scalar(prob[t][:, 0:w], prob[t][:, 0:w], recip[:, n:n + 1], None, ALU.mult
                                        ).then_inc(normed, 1)
                for n in range(8):
                    t = n % 4
                    w = (t + 1) * P
                    if pos == tab.bias[n]:
                        dve.wait_ge(scored, 8 * q + n + 1)
                        wait(dve, expd, 8 * q + n - 1)
                        V.memset(wait_carrier[:, n:n + 1], 0.0)
                        V.tensor_tensor_reduce(out=s_sb[n % 2][:, 0:w], in0=A(n % 2, 0, w),
                                               in1=bias[:, (TT - 1 - t) * P:], scale=1.0, scalar=3e38,
                                               op0=ALU.add, op1=ALU.min, accum_out=neg_max[:, n:n + 1]
                                               ).then_inc(biased, 1)
                if pos == tab.out:
                    dve.wait_ge(oh_ready, q + 1)
                    V.tensor_tensor(o_lo[:, ds(q * S, S)], G[2][:], o_hi[:, ds(q * S, S)].bitcast(F32),
                                    ALU.subtract).then_inc(o_split, 1)

            def pair(p, ps, shift=0):
                for s in range(16):
                    if s % 8 == 0:
                        split_lo(U_QKV + 8 + ps * 2 + s // 8 + AHEAD, shift)
                    if s == ROPE and ps > 0:
                        rope(2 * p - 1, 1, k_t[(ps + 1) % 2], cos_k, sin_k, 8 * (p - 2))
                    if s == 8 + ROPE:
                        rope(2 * p, 0, q_t[ps % 2], cos_q, sin_q, 8 * (p - 1))
                    if ps > 1:
                        attend(p - 2, ps % 2, s + 16, ATT)
                    if ps > 0:
                        attend(p - 1, (ps + 1) % 2, s, ATT)

            def attention():
                inverse(2)
                for s in range(1, 8):
                    split_lo(U_QKV + s + AHEAD)
                    if s == 3:
                        dve.wait_ge(trig_loaded, 48)
                        dve.wait_ge(rstd_ready, 3)
                        for tab in (cos_k, sin_k):
                            chain.mark(V.tensor_tensor(tab[:], tab[:], rstd[:], ALU.mult))
                        chain.fence()
                        for tab, src in ((cos_q, cos_k), (sin_q, sin_k)):
                            chain.mark(V.tensor_scalar(tab[:], src[:], QSCALE, None, ALU.mult))
                        chain.fence()
                for p in range(PEELED):
                    pair(p, p)
                with dve.Fori(PEELED // 2, PAIRS // 2) as i:
                    chain.loop(i, PEELED // 2, 24)
                    for r in range(2):
                        pair(2 * i + r, PEELED + r, 4 * (i - PEELED // 2))
                chain.done((PAIRS - PEELED) // 2)
                split_lo(U_WOA + AHEAD)
                for s in range(24):
                    if s == ROPE:
                        rope(2 * PAIRS - 1, 1, k_t[1], cos_k, sin_k, 8 * (PAIRS - 2))
                    attend(PAIRS - 2, 0, s + 16, ATT)
                    attend(PAIRS - 1, 1, s, LAST_ATT)
                for s in range(1, 9):
                    split_lo(U_WOA + s + AHEAD)
                    residual(s - 1, U_WOA + s - 1, G[WOA_BANK[(s - 1) % 3]][:])
                    norm_tile(3, C_FFN + KT, s - 1)

            def final_norm():
                inverse(4)
                dve.wait_ge(rstd_ready, 5)
                dve.wait_ge(yh_ready, 5 * KT)
                for n in OUT_DVE:
                    tile = slice(n * S, (n + 1) * S)
                    V.tensor_tensor(y_fin[:, tile], y_fin[:, tile], rstd[:], ALU.mult).then_inc(out_ready, 1)

            prologue()
            mixer()
            ffn_in(0)
            ffn_out(0)
            attention()
            ffn_in(1)
            ffn_out(1)
            final_norm()

        @block.tensor
        def _(pe):
            def mm3(out, stat, mov, first, last):
                pe.matmul(out, stat[0], mov[0], start=first, stop=False)
                pe.matmul(out, stat[0], mov[1], start=False, stop=False)
                return pe.matmul(out, stat[1], mov[0], start=False, stop=last)

            def weight(u, tile, n=P):
                at = (u % RING) * UNIT + tile * P
                return w_hi[:, at:at + n], w_lo[:, at:at + n]

            def tile_of(hi_t, lo_t, k, c0=0, n=S):
                return hi_t[:, k * S + c0:k * S + c0 + n], lo_t[:, k * S + c0:k * S + c0 + n]

            def begin(u):
                pe.wait_ge(lo_ready, u + 1)

            def y_tile(m, k, first):
                if first:
                    pe.wait_ge(y_ready, 8 * m + k + 1)
                return tile_of(y_hi, y_lo, k)

            def mean_square(m, bank):
                if m == 0:
                    pe.wait_ge(ones_set, 4)
                pe.wait_ge(sq_added, 8 * (m + 1))
                for t in range(TT):
                    ins = pe.matmul(bank[:, t:t + 1], sq_sum[:, t * P:(t + 1) * P], ones_d[:], start=True, stop=True)
                ins.then_inc(ms_ready, 1)

            def spread(m, bank):
                pe.wait_ge(diag_ready, m + 1)
                pe.matmul(bank, ones[:], sq[:, 0:S], start=True, stop=True).then_inc(spread_ready, 1)

            def whole_tile(u, bank, m, first, spread_bank=None):
                for k in range(KT):
                    if spread_bank is not None and k == 3:
                        spread(m, spread_bank)
                    ins = mm3(bank, weight(u, k), y_tile(m, k, first), k == 0, k == KT - 1)
                ins.then_inc(unit_done, 1)

            def token_major(u0, bank_of, m, first):
                for j in range(4):
                    begin(u0 + j)
                    for kk in range(2):
                        k = 2 * j + kk
                        if first:
                            pe.wait_ge(y_ready, 8 * m + k + 1)
                        for t in range(TT):
                            ins = mm3(bank_of(t), tile_of(y_hi, y_lo, k, t * P, P), weight(u0 + j, kk * 4, S),
                                      k == 0, k == KT - 1)
                        if m == 2 and first and k == 2:
                            spread(2, G[2][:])
                    ins.then_inc(unit_done, 1)
                    if m == 2 and first and j == 0:
                        mean_square(2, G[3])

            def score_event(ev):
                a = ev % 2
                wait(pe, merged, ev - 1)
                if ev < 2:
                    if ev == 0:
                        pe.wait_ge(v_ready, TT)
                        pe.wait_ge(evacuated, E_REC + 2 * HG)
                        pe.wait_ge(logf_ready, 1)
                        pe.wait_ge(hk_ready, HG)
                else:
                    L = (ev - 2) // 2
                    done = sum(1 if (x_ - 2) // 2 == 0 else 2 for x_ in range(2, ev + 1))
                    pe.wait_ge(hat_ready, done)
                for m in range(8):
                    c0 = a * 2 * S + m * P
                    if ev < 2:
                        ins = pe.matmul(aux[:, c0:c0 + P], hk[:, c0:c0 + P], hq[:, c0:c0 + P], start=True, stop=True)
                    else:
                        right = lambda t: t[:, c0:c0 + P].rearrange("p (n two h) -> p n two h", two=2, h=1 << L)[:, :, 1, :]
                        ins = pe.matmul(right(aux), hat[:, c0:c0 + P], right(hat), start=True, stop=True)
                ins.then_inc(raw_scored, 1)

            def tail(unit):
                hc = lambda t, h, c: t[:, h * S + c * P:h * S + (c + 1) * P]
                if unit == TAIL + 1:
                    pe.wait_ge(khat_ready, 1)
                    pe.wait_ge(merged, 2 + 2 * LEVELS)
                    for c in range(3):
                        for h in range(HG):
                            ins = pe.transpose(A(c, h * P, P), hc(hat, h, c), ident[:])
                    ins.then_inc(khat_turned, 1)
                if unit == TAIL + 2:
                    pe.wait_ge(khat_copied, 3)
                    for c, bank in enumerate((3, 0, 1)):
                        for h in range(HG):
                            ins = pe.matmul(A(bank, h * P, P), khat_t[:, c * S + h * P:c * S + (h + 1) * P],
                                            hv[:, c * S + h * P:c * S + (h + 1) * P], start=True, stop=True)
                        ins.then_inc(kv_ready, 1)
                if unit == TAIL + 3:
                    pe.wait_ge(state_ready, 1)
                    for h in range(HG):
                        for c in range(TT):
                            ins = pe.matmul(A(h, c * P, P), hv[:, c * S + h * P:c * S + (h + 1) * P],
                                            hc(hsc, h, c), start=True, stop=c == 0)
                            if c:
                                ins = pe.matmul(A(h, c * P, P), state[:, (c - 1) * S + h * P:(c - 1) * S + (h + 1) * P],
                                                hc(hq, h, c), start=False, stop=True)
                        ins.then_inc(o_ready, 1)
                if unit == TAIL + 4:
                    pe.wait_ge(o_taken, 2 * HG)
                    for n in range(HG * TT):
                        ins = pe.matmul(A(0, n, 1), ho_sq[:, n * P:(n + 1) * P], ones_h[:], start=True, stop=True)
                    ins.then_inc(oms_ready, 1)
                if unit == TAIL + 5:
                    pe.wait_ge(odiag_ready, 1)
                    for h in range(HG):
                        ins = pe.matmul(A(h), ones[:], ho_diag[:, h * S:(h + 1) * S], start=True, stop=True)
                    ins.then_inc(ospread_ready, 1)

            def mixer():
                token_major(U_REC, A, 0, True)
                mean_square(0, G[3])
                for u in range(4, 28):
                    begin(u)
                    wait(pe, evacuated, E_REC + u - 4 - 4 + 1)
                    if u == 6:
                        pe.wait_ge(rstd_ready, 1)
                    whole_tile(u, G[u % 4][:], 0, False, G[2][:] if u == 4 else None)
                    for ev in events(u):
                        score_event(ev)
                    tail(u)
                for u in range(U_WOR, U_WOR + 8):
                    begin(u)
                    half = (u - U_WOR) // 4
                    for e in range(2):
                        n = 2 * (u - U_WOR) + e
                        pe.wait_ge(evacuated, E_WOR + n - 4 + 1)
                        for k in range(4):
                            pe.wait_ge(mix_ready, 4 * half + k + 1)
                            ins = mm3(G[n % 4][:], weight(u, 4 * e + k), tile_of(mix_hi, mix_lo, 4 * half + k),
                                      k == 0, k == 3)
                    ins.then_inc(unit_done, 1)
                    tail(u)

            def ffn_in(l, bank_free):
                m = 1 + 2 * l

                def body(i, first):
                    for s in range(4):
                        begin(U_FI[l] + 4 * i + s)
                        pe.wait_ge(evacuated, bank_free[s] if first else E_FI[l] + 4 * i + s - 3)
                        whole_tile(U_FI[l] + s, G[s][:], m, first and s == 0, A(2) if first and s == 1 else None)
                        if first and s == 0:
                            mean_square(m, A(3))

                body(0, True)
                with pe.Fori(1, FT // 2) as i:
                    body(i, False)

            def ffn_out(l):
                def body(i, first):
                    for e in range(2):
                        pe.wait_ge(evacuated, E_FO[l] - 3 + e if first else E_FO[l] + 2 * i + e - 1)
                        k = 0
                        for s in range(4):
                            begin(U_FO[l] + 8 * i + 4 * e + s)
                            for tile in range(FO_TILES[s]):
                                if first and e == 0:
                                    pe.wait_ge(act_ready, FT * l + k + 1)
                                ins = mm3(G[e][:], weight(U_FO[l] + s, tile), tile_of(act_hi, act_lo, k),
                                          k == 0, k == FT - 1)
                                k += 1
                            ins.then_inc(unit_done, 1)

                body(0, True)
                with pe.Fori(1, KT // 2) as i:
                    body(i, False)

            def attend(q, par, pos, tab):
                for n in range(8):
                    e, t = divmod(n, 4)
                    if pos == tab.qk[n]:
                        pe.wait_ge(evacuated, 2 * q + (E_QKV + 2))
                        wait(pe, biased, 8 * q + n - 1)
                        rows = slice(e * HD, (e + 1) * HD)
                        pe.matmul(A(n % 2, 0, (t + 1) * P), q_t[par][rows, t * P:(t + 1) * P],
                                  k_t[par][rows, 0:(t + 1) * P], start=True, stop=True).then_inc(scored, 1)
                    if pos == tab.turn[n]:
                        pe.wait_ge(normed, 8 * q + n + 1)
                        wait(pe, pt_ready, 8 * q + n - 1)
                        for j in range(t + 1):
                            ins = pe.transpose(A(2 + n % 2, j * P, P), prob[t][:, j * P:(j + 1) * P], ident[:])
                        ins.then_inc(turned, 1)
                if pos == tab.pv:
                    pe.wait_ge(pt_ready, 8 * q + 8)
                    pe.wait_ge(vp_ready, q + 1)
                    wait(pe, o_split, q)
                    for j in range(TT):
                        for e in range(2):
                            ins = pe.matmul(G[2][e * HD:(e + 1) * HD, j * P:],
                                            v_pair[par][:, j * P + e * HD:j * P + (e + 1) * HD],
                                            pt[e][:, j * S + j * P:(j + 1) * S], start=j == 0, stop=j == TT - 1,
                                            skip_group_check=True)
                    ins.then_inc(pv_done, 1)

            def pair(p, ps):
                for s in range(16):
                    k, j = s % 8, s // 8
                    if k == 0:
                        begin(U_QKV + 8 + 2 * p + j)
                        if ps == 0:
                            pe.wait_ge(v_ready, 2 * TT + j + 1)
                        else:
                            pe.wait_ge(evacuated, E_QKV + 2 * p - 1 + j)
                    ins = mm3(G[j][:], weight(U_QKV + 8 + 2 * ps + j, k), tile_of(y_hi, y_lo, k), k == 0, k == KT - 1)
                    if k == KT - 1:
                        ins.then_inc(unit_done, 1)
                    if s == 0 and ps == 1:
                        pe.wait_ge(v_ready, 3 * TT)
                    if ps > 1:
                        attend(p - 2, ps % 2, s + 16, ATT)
                    if ps > 0:
                        attend(p - 1, (ps + 1) % 2, s, ATT)

            def attention():
                token_major(U_QKV, A, 2, True)
                pe.wait_ge(evacuated, E_QKV)
                pe.wait_ge(rstd_ready, 3)
                token_major(U_QKV + 4, lambda t: G[t][:], 2, False)
                for p in range(PEELED):
                    pair(p, p)
                with pe.Fori(PEELED // 2, PAIRS // 2) as i:
                    for r in range(2):
                        pair(2 * i + r, PEELED + r)
                for n in range(3):
                    begin(U_WOA + n)
                pe.wait_ge(evacuated, E_QKV + 2 * PAIRS - 1)
                for s, (k, n) in enumerate(WOA_SLOTS):
                    if n == 0:
                        pe.wait_ge(o_split, k + 1)
                    if (k, n) == (0, 2):
                        pe.wait_ge(evacuated, E_QKV + 2 * PAIRS)
                    ins = mm3(G[WOA_BANK[n]][:], weight(U_WOA + n, k), tile_of(o_hi, o_lo, k), k == 0, k == KT - 1)
                    if k == KT - 1:
                        ins.then_inc(unit_done, 1)
                    attend(PAIRS - 2, 0, s + 16, ATT)
                    attend(PAIRS - 1, 1, s, LAST_ATT)
                for n in range(3, KT):
                    begin(U_WOA + n)
                    pe.wait_ge(evacuated, E_WOA + n - 2)
                    for k in range(KT):
                        ins = mm3(G[WOA_BANK[n % 3]][:], weight(U_WOA + n, k), tile_of(o_hi, o_lo, k), k == 0, k == KT - 1)
                    ins.then_inc(unit_done, 1)

            mixer()
            ffn_in(0, [E_FI[0] - 3 + b for b in range(4)])
            ffn_out(0)
            attention()
            pe.wait_ge(o_split, PAIRS)
            ffn_in(1, [E_FI[1] - 1, E_FI[1] - 2, E_FI[1] - 2, E_FI[1]])
            ffn_out(1)
            mean_square(4, A(3))
            spread(4, A(2))


def blocks(w):
    k, n = w.shape
    return w.reshape(k // P, P, n // P, P).transpose(2, 1, 0, 3).reshape(n // P, P, k)


def token_major_units(w):
    k, n = w.shape
    return (w.reshape(k // (2 * P), 2, P, n // S, S).transpose(3, 0, 2, 1, 4)
            .reshape(n // S * (k // (2 * P)), P, 2 * S))


def constants():
    tq, ks = np.arange(P)[:, None], np.arange(P)[None, :]
    bias = np.empty((P, TT, P), np.float32)
    for col in range(TT):
        rel = (TT - 1 - col) * P + tq - ks
        count = ((rel >= 0) & (rel <= P)).astype(int) + ((rel >= 0) & (rel % 4 == 0)) + ((rel >= 0) & (rel % 16 == 0))
        bias[:, col] = np.where(count > 0, -np.log(np.maximum(count, 1)), 1e30)
    masks = np.zeros((P, LEVELS + 1, P), np.float32)
    s, t = np.arange(P)[:, None], np.arange(P)[None, :]
    for L in range(LEVELS):
        masks[:, L] = (s >> (L + 1) == t >> (L + 1)) & ((s >> L) % 2 == 0) & ((t >> L) % 2 == 1)
    masks[:, LEVELS] = s == t
    half = HD // 2
    freq = (np.float32(10000.0) ** (-np.arange(half, dtype=np.float32) / np.float32(half))).astype(np.float32)
    ang = np.arange(S, dtype=np.float32)[None, :] * freq[np.arange(P) % half][:, None]
    sign = np.where(np.arange(P) % HD < half, -1.0, 1.0)[:, None]
    trig = np.stack([np.cos(ang), np.sin(ang) * sign]).astype(np.float32)
    return bias.reshape(P, TT * P), masks.reshape(P, -1), trig


def kernel(x, mix_norm, ffn_norm, w_in_rec, conv_w, hgrn_lb, hgrn_norm, w_out_rec, w_qkv_attn, w_o_attn,
           w_ffn_in, w_ffn_out, final_norm):
    import concourse.bacc as bacc
    from concourse.bass_utils import run_bass_kernel_spmd

    x, mix_norm, ffn_norm, w_in_rec, conv_w, hgrn_lb, hgrn_norm, w_out_rec, w_qkv_attn, w_o_attn, w_ffn_in, \
        w_ffn_out, final_norm = (np.asarray(a) for a in (
            x, mix_norm, ffn_norm, w_in_rec, conv_w, hgrn_lb, hgrn_norm, w_out_rec, w_qkv_attn, w_o_attn,
            w_ffn_in, w_ffn_out, final_norm))
    bias, masks, trig = constants()
    cols = lambda a: a.reshape(-1, P).T
    params = np.concatenate([cols(mix_norm), cols(ffn_norm), cols(final_norm), cols(conv_w[0]), cols(hgrn_lb),
                             cols(hgrn_norm[0])], axis=1)
    b_, c_, v_, q_, f_, i_, g_ = (w_in_rec[0][:, n * S:(n + 1) * S] for n in range(7))
    b_, c_, v_ = (blocks(w) for w in (b_, c_, v_))
    conv = np.stack([c_, v_, b_], axis=1).reshape(3 * HG, P, UNIT)
    w_rec = np.concatenate([token_major_units(i_), blocks(f_), blocks(q_), blocks(g_), conv])
    w_or = np.concatenate([blocks(w_out_rec[0][h * S:(h + 1) * S]).reshape(4, 2, P, S).transpose(0, 2, 1, 3)
                           .reshape(4, P, UNIT) for h in range(2)])
    q_, k_, v_ = (w_qkv_attn[0][:, n * D:(n + 1) * D] for n in range(3))
    w_qkv = np.concatenate([token_major_units(v_), np.stack([blocks(q_), blocks(k_)], axis=1).reshape(2 * KT, P, UNIT)])
    w_oa = blocks(w_o_attn[0])
    w_fi = [np.stack([blocks(w[:, :FF]), blocks(w[:, FF:])], axis=1).reshape(2 * FT, P, UNIT) for w in w_ffn_in]
    w_fo = []
    for w in w_ffn_out:
        padded = np.zeros((KT, 4, P, max(FO_TILES) * P), w.dtype)
        whole, k0 = blocks(w), 0
        for s, tiles in enumerate(FO_TILES):
            padded[:, s, :, :tiles * P] = whole[:, :, k0 * P:(k0 + tiles) * P]
            k0 += tiles
        w_fo.append(padded.reshape(4 * KT, P, -1))

    arrays = {
        "x_in": x[0].T.reshape(KT, P, S).transpose(1, 0, 2), "params": params, "ident": np.eye(P, dtype=np.float32),
        "score_bias": bias, "level_masks": masks, "trig": trig, "w_rec": w_rec, "w_or": w_or, "w_fi0": w_fi[0],
        "w_fi1": w_fi[1], "w_fo0": w_fo[0], "w_fo1": w_fo[1], "w_qkv": w_qkv, "w_oa": w_oa,
    }
    arrays = {name: np.ascontiguousarray(a) for name, a in arrays.items()}
    nc = bacc.Bacc("TRN2", target_bir_lowering=False, num_devices=1)
    t = {name: nc.dram_tensor(name, a.shape, mybir.dt.from_np(a.dtype), kind="ExternalInput").ap()
         for name, a in arrays.items()}
    out = nc.dram_tensor("out", (KT, P, S), F32, kind="ExternalOutput").ap()
    trunk(nc, t["x_in"], t["params"], t["ident"], t["score_bias"], t["level_masks"], t["trig"], t["w_rec"],
          t["w_or"], [t["w_fi0"], t["w_fi1"]], [t["w_fo0"], t["w_fo1"]], t["w_qkv"], t["w_oa"], out)
    r = run_bass_kernel_spmd(nc, [arrays], core_ids=[0])
    return r.results[0]["out"].reshape(D, S).T[None]
```

```python
from contextlib import ExitStack

import numpy as np

import concourse.bass as bass
from concourse import mybir
from concourse.bass import ds

ALU = mybir.AluOpType
ACT = mybir.ActivationFunctionType
F32 = mybir.dt.float32
F32R = mybir.dt.float32r
U8 = mybir.dt.uint8

P = 128
S = 512
D = 1024
KT = D // P
TT = S // P
HG = 4
HEADS, HD = 16, 64
PAIRS = HEADS // 2
FF = 2816
FT = FF // P
EPS = 1e-6
CONV_W = 3
LEVELS = 7
QSCALE = -(HD ** -0.5)

RING, AHEAD = 4, 3
WARM_UP = 20
UNIT = 1024
FO_TILES = (6, 6, 5, 5)
assert sum(FO_TILES) == FT

U_REC = 0
U_WOR = U_REC + 28
U_FI = [U_WOR + 8, 0]
U_FO = [U_FI[0] + 2 * FT, 0]
U_QKV = U_FO[0] + 4 * KT
U_WOA = U_QKV + 24
U_FI[1] = U_WOA + 8
U_FO[1] = U_FI[1] + 2 * FT
U_END = U_FO[1] + 4 * KT
assert all(u % RING == 0 for u in (U_WOR, *U_FI, *U_FO, U_QKV, U_WOA, U_END))

E_REC = 0
E_WOR = E_REC + 24
E_FI = [E_WOR + 16, 0]
E_FO = [E_FI[0] + 2 * FT, 0]
E_QKV = E_FO[0] + KT
E_WOA = E_QKV + 2 * PAIRS
E_FI[1] = E_WOA + KT
E_FO[1] = E_FI[1] + 2 * FT

C_MIX, C_FFN, C_FIN, C_CONV, C_LB, C_HN = 0, 16, 32, 40, 52, 64
N_PARAMS = 65

DIAG_STEP = 12
LEVEL_STEP = [13, 13, 14, 14, 15, 15, 16, 17, 18, 19, 20, 21, 22, 23]
TAIL = 24

class Positions:
    def __init__(self, qk, bias, exp, norm, turn, probs, pv):
        self.qk = qk
        self.bias = [q + bias for q in qk]
        self.exp = [q + exp for q in qk]
        self.norm = [q + norm for q in qk]
        self.turn = [q + turn for q in qk]
        self.probs = [q + probs for q in qk]
        self.values, self.pv, self.out = 3, pv, pv + 1


ATT = Positions([7, 7, 10, 10, 13, 13, 17, 17], 1, 3, 4, 8, 9, 27)
LAST_ATT = Positions([6, 6, 8, 8, 10, 10, 12, 12], 1, 2, 4, 5, 7, 19)
PEELED = 4
SWAP, ROPE = (0, 1, 2, 3), 4
WOA_BANK = (0, 3, 1)
WOA_SLOTS = ([(k, n) for k in range(3) for n in range(2)] + [(k, 2) for k in range(3)]
             + [(k, n) for k in range(3, KT) for n in range(3)])


def unit_cols(u):
    for base in U_FO:
        if base <= u < base + 4 * KT:
            return FO_TILES[u % 4] * P
    return UNIT


class Chain:

    def __init__(self, eng, sem):
        self.eng, self.sem, self.n, self.shift = eng, sem, 0, 0

    def mark(self, ins):
        ins.then_inc(self.sem, 1)
        self.n += 1

    def fence(self):
        self.eng.wait_ge(self.sem, self.shift + self.n)

    def loop(self, i, first, per_round):
        self.shift, self.start, self.per = (i - first) * per_round, self.n, per_round

    def done(self, rounds):
        assert self.n - self.start == self.per, (self.n - self.start, self.per)
        self.shift, self.n = 0, self.start + rounds * self.per


def wait(eng, sem, value):
    if not isinstance(value, int) or value > 0:
        eng.wait_ge(sem, value)


def trunk(nc, x_in, params_in, ident_in, bias_in, masks_in, trig_in, w_rec, w_or, w_fi, w_fo, w_qkv,
          w_oa, out):
    with ExitStack() as ctx:
        def sem(name):
            return ctx.enter_context(nc.semaphore(name))

        base, sbuf_end = {"at": -(-nc.sbuf_base // 32) * 32}, nc.sbuf_top
        ctx.enter_context(nc.sbuf_tensor("arena", [P, (nc.sbuf_top - base["at"]) // 4], F32))

        def sb(name, cols, dt=F32, at=None):
            size = cols * (1 if dt == U8 else 4)
            if at is None:
                at = base["at"]
                base["at"] += -(-size // 32) * 32
            return nc.alloc_sbuf_tensor_at(name, [P, cols], dt, offset=at), at

        x, _ = sb("x", KT * S)
        w_raw, _ = sb("w_raw", RING * UNIT)
        w_hi, _ = sb("w_hi", RING * UNIT, F32R)
        w_lo, _ = sb("w_lo", RING * UNIT, F32R)
        y_hi, at_y = sb("y_hi", KT * S, F32R)
        y_lo, _ = sb("y_lo", KT * S, F32R)
        act_hi, at_b = sb("act_hi", FT * S, F32R)
        act_lo, _ = sb("act_lo", FT * S, F32R)
        rstd, _ = sb("rstd", S)
        sq, _ = sb("sq", 2 * S)
        sq_sum, _ = sb("sq_sum", S)
        ident, _ = sb("ident", P)
        ones_d, _ = sb("ones_d", 1)
        ones_h, _ = sb("ones_h", 1)
        ones, _ = sb("ones", P)
        eps, _ = sb("eps", 1)
        masks, _ = sb("masks", (LEVELS + 1) * P, U8)
        params, _ = sb("params", N_PARAMS)
        lb_e, _ = sb("lb_e", 12)
        lb_s, _ = sb("lb_s", 4)
        lb, _ = sb("lb", 4)
        one_lb, _ = sb("one_lb", 4)
        rstd_tok, _ = sb("rstd_tok", TT)
        rstd_head, _ = sb("rstd_head", HG * TT)
        neg_max, _ = sb("neg_max", 8)
        denom, _ = sb("denom", 8)
        recip, _ = sb("recip", 8)
        wait_carrier, _ = sb("wait_carrier", 8)
        at_t = base["at"]
        t_slot = [at_t + n * 2080 for n in range(6)]
        gate_t = [sb(f"gate_t{n}", S, at=t_slot[n])[0] for n in range(2)]
        silu_t = [sb(f"silu_t{n}", S, at=t_slot[2 + n])[0] for n in range(2)]
        up_t = [sb(f"up_t{n}", S, at=t_slot[4 + n])[0] for n in range(2)]
        conv_u, _ = sb("conv_u", S + CONV_W - 1, at=t_slot[0])
        conv_c, _ = sb("conv_c", S, at=t_slot[1])
        conv_y, _ = sb("conv_y", S, at=t_slot[2])
        conv_b, _ = sb("conv_b", S, at=t_slot[3])
        cos_k, _ = sb("cos_k", S, at=t_slot[0])
        sin_k, _ = sb("sin_k", S, at=t_slot[1])
        cos_q, _ = sb("cos_q", S, at=t_slot[2])
        sin_q, _ = sb("sin_q", S, at=t_slot[3])
        bias, _ = sb("bias", S, at=t_slot[4])
        swapped, _ = sb("swapped", S, at=t_slot[5])
        assert t_slot[5] + 2080 <= sbuf_end, (t_slot, sbuf_end)

        big = HG * S
        hq, hp, hk, hsg, hv, hat, hsc = (sb(n, big, at=at_b + m * big * 4)[0] for m, n in enumerate(
            ("hg_q", "hg_logf", "hg_k", "hg_gate", "hg_v", "hg_hat", "hg_scores")))
        masks_f, _ = sb("masks_f", (LEVELS + 1) * P, at=at_b + 6 * big * 4)
        mix_hi, _ = sb("mix_hi", KT * S, F32R, at=at_b + 7 * big * 4)
        mix_lo, _ = sb("mix_lo", KT * S, F32R, at=at_b + 9 * big * 4)
        state, _ = sb("hg_state", 3 * S, at=at_b + 2 * big * 4)
        khat_t, _ = sb("hg_khat_t", 3 * S, at=at_b + 5 * big * 4)
        ho, ho_sq, ho_gated = (sb(n, big, at=at_y + m * big * 4)[0] for m, n in enumerate(
            ("hg_o", "hg_o_sq", "hg_o_gated")))
        ho_diag, _ = sb("hg_o_diag", big, at=at_b + big * 4)
        o_hi, _ = sb("o_hi", KT * S, F32R, at=at_b)
        o_lo, _ = sb("o_lo", KT * S, F32R, at=at_b + 16384)
        v_tok, _ = sb("v_tok", TT * D, at=at_b + 32768)
        pt = [sb(f"probs_t{e}", TT * S, at=at_b + 49152 + e * 8192)[0] for e in range(2)]
        q_t = [sb(f"q_t{n}", S, at=at_b + 65536 + n * 2048)[0] for n in range(2)]
        k_t = [sb(f"k_t{n}", S, at=at_b + 69632 + n * 2048)[0] for n in range(2)]
        v_pair = [sb(f"v_pair{n}", TT * P, at=at_b + 73728 + n * 2048)[0] for n in range(2)]
        s_sb = [sb(f"scores{n}", S, at=at_b + 77824 + n * 2048)[0] for n in range(2)]
        prob = [sb(f"probs{n}", S, at=at_b + 81920 + n * 2048)[0] for n in range(4)]
        y_fin, _ = sb("y_fin", KT * S, at=at_y)

        G = [ctx.enter_context(nc.psum_tensor(f"gemm{n}", [P, S], F32)) for n in range(4)]
        aux = ctx.enter_context(nc.psum_tensor("aux", [P, 4 * S], F32))

        def A(bank, c0=0, n=S):
            return aux[:, bank * S + c0:bank * S + c0 + n]


        w_loaded = [sem(f"w_loaded{n}") for n in range(RING)]
        half_loaded, half_hi, half_lo = sem("half_loaded"), sem("half_hi"), sem("half_lo")
        hi_ready = sem("hi_ready")
        lo_ready = sem("lo_ready")
        unit_done = sem("unit_done")
        evacuated = sem("evacuated")
        x_loaded = [sem(f"x_loaded{n}") for n in range(KT // 2 + 1)]
        params_loaded, consts_loaded, trig_loaded = sem("params_loaded"), sem("consts_loaded"), sem("trig_loaded")
        ones_set = sem("ones_set")
        masks_ready = sem("masks_ready")
        yh_ready, y_ready = sem("yh_ready"), sem("y_ready")
        sq_ready, sq_added = sem("sq_ready"), sem("sq_added")
        ms_ready = sem("ms_ready")
        root_ready = sem("root_ready")
        diag_ready = sem("diag_ready")
        spread_ready = sem("spread_ready")
        rstd_ready = sem("rstd_ready")
        v_ready = sem("v_ready")
        dve_chain = sem("dve_chain")
        lb_shifted, lb_exp, lb_ready = sem("lb_shifted"), sem("lb_exp"), sem("lb_ready")
        sig_ready = sem("sig_ready")
        f_ready = sem("f_ready")
        hk_ready = sem("hk_ready")
        logf_ready = sem("logf_ready")
        diff_ready, exp_ready = sem("diff_ready"), sem("exp_ready")
        hat_ready = sem("hat_ready")
        raw_scored, merged = sem("raw_scored"), sem("merged")
        conv_ready, mixh_ready, mix_ready = sem("conv_ready"), sem("mixh_ready"), sem("mix_ready")
        tail_diff, tail_exp, khat_ready, qhat_ready = (
            sem("tail_diff"), sem("tail_exp"), sem("khat_ready"), sem("qhat_ready"))
        khat_turned, khat_copied = sem("khat_turned"), sem("khat_copied")
        kv_ready, state0_ready, state_ready = sem("kv_ready"), sem("state0_ready"), sem("state_ready")
        o_ready, o_taken = sem("o_ready"), sem("o_taken")
        silu_g_ready = sem("silu_g_ready")
        gain_ready, gated_ready = sem("gain_ready"), sem("gated_ready")
        oms_ready, oroot_ready, odiag_ready, ospread_ready, onorm_ready = (
            sem("oms_ready"), sem("oroot_ready"), sem("odiag_ready"), sem("ospread_ready"), sem("onorm_ready"))
        silu_ready, prod_ready = sem("silu_ready"), sem("prod_ready")
        acth_ready, act_ready = sem("acth_ready"), sem("act_ready")
        swap_ready = sem("swap_ready")
        vp_ready = sem("vp_ready")
        scored, biased, expd = sem("scored"), sem("biased"), sem("expd")
        normed, turned, pt_ready = sem("normed"), sem("turned"), sem("pt_ready")
        pv_done, oh_ready, o_split = sem("pv_done"), sem("oh_ready"), sem("o_split")
        out_ready, out_ready_pool = sem("out_ready"), sem("out_ready_pool")
        out_stored, out_stored_act = sem("out_stored"), sem("out_stored_act")

        OUT_POOL = (2, 5)
        OUT_DVE = [n for n in range(KT) if n not in OUT_POOL]
        OUT_SP, OUT_ACT = (0, 3, 5, 7), (1, 2, 4, 6)

        block = ctx.enter_context(nc.Block())

        def wslot(t, u, c0=0, n=None):
            s0 = (u % RING) * UNIT + c0
            return t[:, s0:s0 + (unit_cols(u) if n is None else n)]

        def store(eng, tiles, stored):
            for n in tiles:
                if n in OUT_POOL:
                    eng.wait_ge(out_ready_pool, OUT_POOL.index(n) + 1)
                else:
                    eng.wait_ge(out_ready, OUT_DVE.index(n) + 1)
                eng.dma_start(out[n], y_fin[:, n * S:(n + 1) * S]).then_inc(stored, 16)
            eng.wait_ge(stored, 16 * len(tiles))

        @block.sync
        def _(sp):
            def load(src, unit, slot, c0, c1, loaded):
                sp.dma_start(w_raw[:, slot * UNIT + c0:slot * UNIT + c1], src[unit, :, c0:c1]).then_inc(loaded, 16)

            def loads(src, base_u, count):
                first = RING if base_u == 0 else 0
                for u in range(first):
                    load(src, u, u % RING, UNIT // 2 if u == 0 else 0, UNIT, w_loaded[u])
                with sp.Fori(first // RING, count // RING) as i:
                    for s in range(RING):
                        sp.wait_ge(lo_ready, i * RING + (base_u + s + 1 - RING))
                        cols = unit_cols(base_u + s)
                        sp.dma_start(w_raw[:, s * UNIT:s * UNIT + cols],
                                     src[ds(i * RING + s, 1), :, 0:cols].rearrange("o p c -> (o p) c")
                                     ).then_inc(w_loaded[s], 16)

            sp.dma_start(x[:, 0:S], x_in[:, 0, :]).then_inc(x_loaded[0], 16)
            load(w_rec, 0, 0, 0, UNIT // 2, half_loaded)
            loads(w_rec, U_REC, 28)
            loads(w_or, U_WOR, 8)
            loads(w_fi[0], U_FI[0], 2 * FT)
            loads(w_fo[0], U_FO[0], 4 * KT)
            loads(w_qkv, U_QKV, 24)
            loads(w_oa, U_WOA, 8)
            loads(w_fi[1], U_FI[1], 2 * FT)
            loads(w_fo[1], U_FO[1], 4 * KT)
            store(sp, OUT_SP, out_stored)

        @block.gpsimd
        def _(pool):
            nc.gpsimd.memset(ones_d[:], 1.0 / D).then_inc(ones_set, 1)
            nc.gpsimd.memset(ones_h[:], 1.0 / P).then_inc(ones_set, 1)
            nc.gpsimd.memset(ones[:], 1.0).then_inc(ones_set, 1)
            nc.gpsimd.memset(eps[:], EPS).then_inc(ones_set, 1)

            def add_squares(m, first, n, buf):
                src = sq[:, buf * S:(buf + 1) * S]
                pool.wait_ge(sq_ready, 8 * m + n + 1)
                if first:
                    wait(pool, ms_ready, m)
                    nc.gpsimd.tensor_copy(sq_sum[:], src).then_inc(sq_added, 1)
                else:
                    pool.wait_ge(sq_added, 8 * m + n)
                    nc.gpsimd.tensor_tensor(sq_sum[:], sq_sum[:], src, ALU.add).then_inc(sq_added, 1)

            def sum_squares(m):
                add_squares(m, True, 0, 0)
                with pool.Fori(0, KT // 2 - 1) as i:
                    for r in range(2):
                        add_squares(m, False, 2 * i + r + 1, 1 - r)
                if m < 4:
                    add_squares(m, False, KT - 1, 1)

            sum_squares(0)
            pool.wait_ge(consts_loaded, 32)
            nc.gpsimd.tensor_copy(masks[:], masks_f[:]).then_inc(masks_ready, 1)
            pool.wait_ge(silu_g_ready, 1)
            nc.gpsimd.tensor_scalar(hsg[:], hsg[:], params[:, C_HN:C_HN + 1], None, ALU.mult).then_inc(gain_ready, 1)
            pool.wait_ge(gain_ready, 1)
            for h in range(HG):
                blk = slice(h * S, (h + 1) * S)
                pool.wait_ge(o_taken, 2 * h + 1)
                nc.gpsimd.tensor_tensor(ho_gated[:, blk], ho[:, blk], hsg[:, blk], ALU.mult).then_inc(gated_ready, 1)
            for m in range(1, 5):
                sum_squares(m)
            pool.wait_ge(rstd_ready, 5)
            pool.wait_ge(yh_ready, 5 * KT)
            for n in OUT_POOL:
                tile = slice(n * S, (n + 1) * S)
                nc.gpsimd.tensor_tensor(y_fin[:, tile], y_fin[:, tile], rstd[:], ALU.mult).then_inc(out_ready_pool, 1)

        def halves(t, a, L):
            h = 1 << L
            v = t[:, a * 2 * S:(a + 1) * 2 * S].rearrange("p (n two h) -> p n two h", two=2, h=h)
            return v[:, :, 0, :], v[:, :, 1, :]

        def events(step):
            return ([0, 1] if step == DIAG_STEP else []) + [
                2 + e for e in range(2 * LEVELS) if LEVEL_STEP[e] == step]


        @block.scalar
        def _(act):
            def split_hi(u, shift=0):
                s = u % RING
                cols = unit_cols(u)
                act.wait_ge(w_loaded[s], shift * (16 // RING) + 16 * (u // RING + 1))
                wait(act, unit_done, shift + (u + 1 - RING))
                nc.scalar.copy(wslot(w_hi, u, 0, cols), wslot(w_raw, u, 0, cols)).then_inc(hi_ready, 1)

            def square(m, n, buf, waited=False):
                if not waited:
                    wait(act, sq_added, 8 * m + n - 1)
                nc.scalar.activation(sq[:, buf * S:(buf + 1) * S], x[:, ds(n * S, S)], ACT.Square
                                     ).then_inc(sq_ready, 1)

            def gain_tile(gain, n, out_t):
                nc.scalar.mul(out_t[:, ds(n * S, S)], x[:, ds(n * S, S)], params[:, ds(n + gain, 1)]
                              ).then_inc(yh_ready, 1)

            def norm_tile(m, gain, n, buf, out_t, unit, shift=0):
                wait(act, sq_added, 8 * m + n - 1)
                gain_tile(gain, n, out_t)
                if unit < U_END:
                    split_hi(unit, shift)
                square(m, n, buf, waited=True)

            def rstd_root(m, bank):
                act.wait_ge(ms_ready, m + 1)
                nc.scalar.activation(rstd_tok[:], bank[:, 0:TT], ACT.Sqrt, bias=eps[:]).then_inc(root_ready, 1)

            def rstd_copy(m, bank):
                act.wait_ge(spread_ready, m + 1)
                nc.scalar.copy(rstd[:], bank).then_inc(rstd_ready, 1)

            def prologue():
                act.dma_start(params[:], params_in).then_inc(params_loaded, 16)
                for c in range(1, KT // 2 + 1):
                    n0, n1 = 2 * c - 1, min(2 * c + 1, KT)
                    act.dma_start(x[:, n0 * S:n1 * S].rearrange("p (t s) -> p t s", s=S),
                                  x_in[:, n0:n1, :]).then_inc(x_loaded[c], 16)
                act.dma_start(ident[:], ident_in).then_inc(consts_loaded, 16)
                act.dma_start(masks_f[:], masks_in).then_inc(consts_loaded, 16)
                act.wait_ge(params_loaded, 16)
                for n in range(KT):
                    act.wait_ge(x_loaded[(n + 1) // 2], 16)
                    gain_tile(C_MIX, n, y_hi)
                    if n == 0:
                        act.wait_ge(half_loaded, 16)
                        nc.scalar.copy(wslot(w_hi, 0, 0, UNIT // 2), wslot(w_raw, 0, 0, UNIT // 2)).then_inc(half_hi, 1)
                        act.wait_ge(w_loaded[0], 16)
                        nc.scalar.copy(wslot(w_hi, 0, UNIT // 2, UNIT // 2), wslot(w_raw, 0, UNIT // 2, UNIT // 2)
                                       ).then_inc(hi_ready, 1)
                    if n in (1, 3, 5):
                        split_hi(n // 2 + 1)
                act.wait_ge(ones_set, 4)
                for n in range(KT):
                    square(0, n, n % 2)
                act.wait_ge(lb_shifted, 3)
                nc.scalar.activation(lb_e[:], lb_e[:], ACT.Exp).then_inc(lb_exp, 1)

            def level_exps(e):
                L, a = divmod(e, 2)
                lo, hi = halves(hat, a, L)
                act.wait_ge(diff_ready, e + 1)
                if L:
                    nc.scalar.activation(lo, lo, ACT.Exp)
                nc.scalar.activation(hi, halves(hp, a, L)[1], ACT.Exp).then_inc(exp_ready, 1)

            def conv_hi(j):
                act.wait_ge(conv_ready, j + 1)
                nc.scalar.copy(mix_hi[:, j * S:(j + 1) * S], conv_y[:]).then_inc(mixh_ready, 1)

            def mixer():
                for step in range(1, 36 + 1):
                    if step == 4:
                        rstd_root(0, G[3])
                    if step == U_WOR:
                        conv_hi(HG - 1)
                        act.wait_ge(kv_ready, 1)
                        nc.scalar.copy(state[:, 0:S], A(3)).then_inc(state0_ready, 1)
                    if step <= U_WOR + 4:
                        split_hi(step + AHEAD)
                    if step == 4:
                        rstd_copy(0, G[2][:])
                        act.wait_ge(unit_done, 4)
                        act.wait_ge(diag_ready, 1)
                        for t in range(TT):
                            nc.scalar.activation(hv[:, t * S:(t + 1) * S], A(t), ACT.Silu,
                                                 scale=rstd_tok[:, t:t + 1]).then_inc(v_ready, 1)
                    if step == 8:
                        act.wait_ge(evacuated, E_REC + HG)
                        nc.scalar.activation(hp[:], hk[:], ACT.Sigmoid).then_inc(sig_ready, 1)
                        nc.scalar.activation(hk[:], hk[:], ACT.Sigmoid, scale=-1.0).then_inc(sig_ready, 1)
                    if step == 9:
                        act.wait_ge(f_ready, HG)
                        nc.scalar.activation(hp[:], hp[:], ACT.Ln).then_inc(logf_ready, 1)
                    for x_ in events(step):
                        if x_ >= 2:
                            level_exps(x_ - 2)
                    if step == 16:
                        act.wait_ge(evacuated, E_REC + 3 * HG)
                        nc.scalar.activation(hsg[:], hsg[:], ACT.Silu).then_inc(silu_g_ready, 1)
                    if step == TAIL:
                        act.wait_ge(tail_diff, 1)
                        nc.scalar.activation(hat[:], hat[:], ACT.Exp).then_inc(tail_exp, 1)
                        nc.scalar.activation(hp[:], hp[:], ACT.Exp).then_inc(tail_exp, 1)
                    if step == TAIL + 3:
                        act.wait_ge(khat_turned, 1)
                        for c in range(3):
                            nc.scalar.copy(khat_t[:, c * S:(c + 1) * S], A(c)).then_inc(khat_copied, 1)
                    for j in range(HG):
                        if step == 20 + 3 * j and j < HG - 1:
                            conv_hi(j)
                    if step == TAIL + 5:
                        for h in range(HG):
                            act.wait_ge(o_ready, h + 1)
                            nc.scalar.copy(ho[:, h * S:(h + 1) * S], A(h)).then_inc(o_taken, 1)
                            nc.scalar.activation(ho_sq[:, h * S:(h + 1) * S], A(h), ACT.Square).then_inc(o_taken, 1)
                    if step == TAIL + 6:
                        act.wait_ge(oms_ready, 1)
                        nc.scalar.activation(rstd_head[:], A(0, 0, HG * TT), ACT.Sqrt, bias=eps[:]).then_inc(oroot_ready, 1)
                    if step == TAIL + 7:
                        for h in range(HG):
                            act.wait_ge(onorm_ready, h + 1)
                            nc.scalar.copy(mix_hi[:, (HG + h) * S:(HG + h + 1) * S], ho[:, h * S:(h + 1) * S]
                                           ).then_inc(mixh_ready, 1)
                    if step > U_WOR + 4:
                        tiles = (2 * (step - U_WOR - 5), 2 * (step - U_WOR - 5) + 1)
                        for n in tiles:
                            act.wait_ge(evacuated, E_WOR + 8 + n + 1)
                            gain_tile(C_FFN, n, y_hi)
                        split_hi(step + AHEAD)
                        for n in tiles:
                            square(1, n, n % 2)

            def ffn_in(l):
                rstd_root(1 + 2 * l, A(3))
                rstd_copy(1 + 2 * l, A(2))

                def body(i, last):
                    for s in range(1, 5):
                        u = U_FI[l] + s + AHEAD
                        split_hi(u + 4 * i if last else u, 0 if last else 4 * i)
                        j, k = (s - 1) // 2, FT * l + 2 * i + (s - 1) // 2
                        if s % 2:
                            act.wait_ge(evacuated, E_FI[l] + 4 * i + s)
                            nc.scalar.activation(silu_t[j][:], gate_t[j][:], ACT.Silu).then_inc(silu_ready, 1)
                        else:
                            act.wait_ge(prod_ready, k + 1)
                            nc.scalar.copy(act_hi[:, ds((2 * i + j) * S, S)], up_t[j][:]).then_inc(acth_ready, 1)

                with act.Fori(0, FT // 2 - 1) as i:
                    body(i, False)
                body(FT // 2 - 1, True)

            def ffn_out(l):
                def body(i, last):
                    for s in range(1, 9):
                        u, shift = U_FO[l] + s + AHEAD, 8 * i
                        if last:
                            u, shift = u + shift, 0
                        if s % 4:
                            if u < U_END:
                                split_hi(u, shift)
                            continue
                        n = 2 * i + (s // 4 - 1)
                        act.wait_ge(evacuated, E_FO[l] + n + 1)
                        if l == 0:
                            norm_tile(2, C_MIX + KT, n, s // 4 - 1, y_hi, u, shift)
                        elif not last:
                            norm_tile(4, C_FIN, n, s // 4 - 1, y_fin, u, shift)
                        else:
                            square(4, n, s // 4 - 1)
                            if u < U_END:
                                split_hi(u)
                            gain_tile(C_FIN, n, y_fin)

                with act.Fori(0, KT // 2 - 1) as i:
                    body(i, False)
                body(KT // 2 - 1, True)

            def swap(k, bank, g):
                if g == 0:
                    act.wait_ge(unit_done, k + (U_QKV + 8 + 1))
                    wait(act, evacuated, k + E_QKV)
                nc.scalar.copy(swapped[32 * (g ^ 1):32 * (g ^ 1) + 32, :], G[bank][32 * g:32 * g + 32, :]
                               ).then_inc(swap_ready, 1)

            def attend(q, par, pos, tab):
                if pos == tab.values:
                    wait(act, pv_done, q - 1)
                    src = v_tok[:].rearrange("s (j c) -> s j c", j=TT)[:, :, ds(q * P, P)]
                    nc.scalar.copy(v_pair[par][:].rearrange("s (j c) -> s j c", j=TT), src).then_inc(vp_ready, 1)
                for n in range(8):
                    t = n // 2
                    w = (t + 1) * P
                    if pos == tab.probs[n]:
                        act.wait_ge(turned, 8 * q + n + 1)
                        if t == 0:
                            wait(act, pv_done, q)
                        dst = pt[n % 2][:].rearrange("s (j t) -> s j t", j=TT)[:, 0:t + 1, t * P:w]
                        nc.scalar.copy(dst, A(2 + n % 2, 0, w).rearrange("s (j t) -> s j t", j=t + 1)
                                       ).then_inc(pt_ready, 1)
                for n in range(8):
                    t = n // 2
                    w = (t + 1) * P
                    if pos == tab.exp[n]:
                        act.wait_ge(biased, 8 * q + n + 1)
                        wait(act, turned, 8 * q + n - 3)
                        nc.scalar.activation(prob[n % 4][:, 0:w], s_sb[n % 2][:, 0:w], ACT.Exp,
                                             bias=neg_max[:, n:n + 1], scale=-1.0,
                                             accum_out=denom[:, n:n + 1]).then_inc(expd, 1)
                if pos == tab.out:
                    act.wait_ge(pv_done, q + 1)
                    nc.scalar.copy(o_hi[:, ds(q * S, S)], G[2][:]).then_inc(oh_ready, 1)

            def values(half):
                for t in range(TT):
                    src = A(t) if half == 0 else G[t][:]
                    nc.scalar.activation(v_tok[:, t * D + half * S:t * D + half * S + S], src, ACT.Copy,
                                         scale=rstd_tok[:, t:t + 1]).then_inc(v_ready, 1)

            def pair(p, ps, shift=0):
                for s in range(16):
                    if s == 0 and ps == 0:
                        act.wait_ge(unit_done, U_QKV + 8)
                        values(1)
                    if s % 8 == 0:
                        split_hi(U_QKV + 8 + ps * 2 + s // 8 + AHEAD, shift)
                    for g in range(4):
                        if s == SWAP[g] and ps > 0:
                            swap(2 * p - 1, 1, g)
                        if s == 8 + SWAP[g]:
                            swap(2 * p, 0, g)
                    if ps > 1:
                        attend(p - 2, ps % 2, s + 16, ATT)
                    if ps > 0:
                        attend(p - 1, (ps + 1) % 2, s, ATT)

            def attention():
                act.wait_ge(act_ready, FT)
                act.dma_start(cos_k[:], trig_in[0]).then_inc(trig_loaded, 16)
                act.dma_start(sin_k[:], trig_in[1]).then_inc(trig_loaded, 16)
                act.dma_start(bias[:], bias_in).then_inc(trig_loaded, 16)
                rstd_root(2, G[3])
                for s in range(1, 8):
                    split_hi(U_QKV + s + AHEAD)
                    if s == 1:
                        rstd_copy(2, G[2][:])
                    if s == 4:
                        act.wait_ge(unit_done, U_QKV + 4)
                        act.wait_ge(diag_ready, 3)
                        values(0)
                for p in range(PEELED):
                    pair(p, p)
                with act.Fori(PEELED // 2, PAIRS // 2) as i:
                    for r in range(2):
                        pair(2 * i + r, PEELED + r, 4 * (i - PEELED // 2))
                split_hi(U_WOA + AHEAD)
                for s in range(24):
                    for g in range(4):
                        if s == SWAP[g]:
                            swap(2 * PAIRS - 1, 1, g)
                    attend(PAIRS - 2, 0, s + 16, ATT)
                    attend(PAIRS - 1, 1, s, LAST_ATT)
                for s in range(1, 9):
                    act.wait_ge(evacuated, E_WOA + s)
                    norm_tile(3, C_FFN + KT, s - 1, (s - 1) % 2, y_hi, U_WOA + s + AHEAD)

            prologue()
            mixer()
            ffn_in(0)
            ffn_out(0)
            attention()
            ffn_in(1)
            ffn_out(1)
            rstd_root(4, A(3))
            rstd_copy(4, A(2))
            store(act, OUT_ACT, out_stored_act)

        @block.vector
        def _(dve):
            V = nc.vector
            chain = Chain(dve, dve_chain)

            def split_lo(u, shift=0):
                cols = unit_cols(u)
                dve.wait_ge(hi_ready, shift + (u + 1))
                V.tensor_tensor(wslot(w_lo, u, 0, cols), wslot(w_raw, u, 0, cols),
                                wslot(w_hi, u, 0, cols).bitcast(F32), ALU.subtract).then_inc(lo_ready, 1)

            def norm_tile(m, gain, n):
                dve.wait_ge(yh_ready, 8 * m + n + 1)
                V.scalar_tensor_tensor(out=y_lo[:, ds(n * S, S)], in0=x[:, ds(n * S, S)],
                                       scalar=params[:, ds(n + gain, 1)],
                                       in1=y_hi[:, ds(n * S, S)].bitcast(F32),
                                       op0=ALU.mult, op1=ALU.subtract).then_inc(y_ready, 1)

            def residual(n, unit, bank):
                dve.wait_ge(unit_done, unit + 1)
                xn = x[:, ds(n * S, S)]
                V.tensor_tensor(xn, xn, bank, ALU.add).then_inc(evacuated, 1)

            def diagonals(roots, diag, tiles):
                chain.mark(V.reciprocal(roots[:], roots[:]))
                chain.fence()
                shape = [P, tiles, P]
                return V.tensor_tensor(diag.rearrange("p (c t) -> p c t", t=P), ident[:].unsqueeze(1).broadcast_to(shape),
                                       roots[:].unsqueeze(2).broadcast_to(shape), ALU.mult)

            def inverse(m):
                dve.wait_ge(root_ready, m + 1)
                diagonals(rstd_tok, sq[:, 0:S], TT).then_inc(diag_ready, 1)

            def prologue():
                dve.wait_ge(params_loaded, 16)
                row = [params[:, C_LB + 4 * r:C_LB + 4 * r + 4] for r in range(3)]
                chain.mark(V.tensor_tensor(lb_s[:], row[0], row[1], ALU.max))
                chain.fence()
                chain.mark(V.tensor_tensor(lb_s[:], lb_s[:], row[2], ALU.max))
                chain.fence()
                for r in range(3):
                    V.tensor_tensor(lb_e[:, 4 * r:4 * r + 4], row[r], lb_s[:], ALU.subtract
                                    ).then_inc(lb_shifted, 1)
                for n in range(KT):
                    dve.wait_ge(x_loaded[(n + 1) // 2], 16)
                    norm_tile(0, C_MIX, n)
                    if n == 0:
                        for c0, hi, lo in ((0, half_hi, half_lo), (UNIT // 2, hi_ready, lo_ready)):
                            dve.wait_ge(hi, 1)
                            V.tensor_tensor(wslot(w_lo, 0, c0, UNIT // 2), wslot(w_raw, 0, c0, UNIT // 2),
                                            wslot(w_hi, 0, c0, UNIT // 2).bitcast(F32), ALU.subtract).then_inc(lo, 1)
                    if n in (1, 3, 5):
                        split_lo(n // 2 + 1)
                dve.wait_ge(lb_exp, 1)
                chain.mark(V.tensor_tensor(one_lb[:], lb_e[:, 0:4], lb_e[:, 8:12], ALU.add))
                chain.fence()
                chain.mark(V.tensor_tensor(lb_s[:], one_lb[:], lb_e[:, 4:8], ALU.add))
                chain.fence()
                chain.mark(V.reciprocal(lb_s[:], lb_s[:]))
                chain.fence()
                V.tensor_tensor(lb[:], lb_e[:, 4:8], lb_s[:], ALU.mult).then_inc(lb_ready, 1)
                V.tensor_tensor(one_lb[:], one_lb[:], lb_s[:], ALU.mult).then_inc(lb_ready, 1)
                chain.mark(V.memset(conv_u[:, 0:CONV_W - 1], 0.0))

            def take(u, dst):
                dve.wait_ge(unit_done, u + 1)
                V.tensor_tensor(dst, G[u % 4][:], rstd[:], ALU.mult).then_inc(evacuated, 1)

            def level_diff(e):
                L, a = divmod(e, 2)
                h = 1 << L
                lo = halves(hat, a, L)[0]
                plo = halves(hp, a, L)[0]
                if L:
                    dve.wait_ge(raw_scored, 2 + e - 2 + 1)
                    chain.fence()
                    V.tensor_tensor(lo, plo[:, :, h - 1:h].broadcast_to(plo.shape), plo, ALU.subtract
                                    ).then_inc(diff_ready, 1)
                else:
                    V.tensor_copy(lo, halves(hk, a, L)[0]).then_inc(diff_ready, 1)

            def level_hat(e):
                L, a = divmod(e, 2)
                h = 1 << L
                lo, hi = halves(hat, a, L)
                plo, phi = halves(hp, a, L)
                dve.wait_ge(exp_ready, e + 1)
                if L:
                    V.tensor_tensor(lo, lo, halves(hk, a, L)[0], ALU.mult).then_inc(hat_ready, 1)
                V.tensor_tensor(hi, hi, halves(hq, a, L)[1], ALU.mult).then_inc(hat_ready, 1)
                chain.mark(V.tensor_tensor(phi, phi, plo[:, :, h - 1:h].broadcast_to(phi.shape), ALU.add))

            def merge(ev):
                dve.wait_ge(raw_scored, ev + 1)
                if ev < 2:
                    dst = hsc[:, ev * 2 * S:(ev + 1) * 2 * S].rearrange("p (m t) -> p m t", t=P)
                    src = aux[:, ev * 2 * S:(ev + 1) * 2 * S].rearrange("p (m t) -> p m t", t=P)
                    mask = masks[:, LEVELS * P:]
                    mask = mask.unsqueeze(1).broadcast_to(dst.shape)
                else:
                    L, a = divmod(ev - 2, 2)
                    dst = halves(hsc, a, L)[1].rearrange("p (m n) h -> p m n h", m=8)
                    src = halves(aux, a, L)[1].rearrange("p (m n) h -> p m n h", m=8)
                    mask = masks[:, L * P:(L + 1) * P].rearrange("p (n two h) -> p n two h", two=2, h=1 << L)
                    mask = mask[:, :, 1, :].unsqueeze(1).broadcast_to(dst.shape)
                    dve.wait_ge(merged, ev - 1)
                V.copy_predicated(dst, mask, src).then_inc(merged, 1)

            def conv_take(j, part, u):
                take(u, (conv_c[:], conv_u[:, CONV_W - 1:], conv_b[:])[part])

            def conv_taps(j, taps):
                for tap in taps:
                    w = params[:, C_CONV + 4 * tap + j:C_CONV + 4 * tap + j + 1]
                    src = conv_u[:, tap:tap + S]
                    chain.fence()
                    if tap == CONV_W - 1:
                        chain.mark(V.tensor_scalar(conv_y[:], src, w, None, ALU.mult))
                    else:
                        chain.mark(V.scalar_tensor_tensor(out=conv_y[:], in0=src, scalar=w, in1=conv_y[:],
                                                          op0=ALU.mult, op1=ALU.add))

            def conv(j, part):
                early = range(CONV_W - 1, -1, -1) if j == HG - 1 else (CONV_W - 1,)
                if part == 1:
                    dve.wait_ge(evacuated, E_REC + 12 + 3 * j + 2)
                    chain.mark(V.tensor_tensor(conv_u[:, 2:], conv_u[:, 2:], conv_c[:], ALU.mult))
                    wait(dve, mixh_ready, j)
                    conv_taps(j, early)
                elif part == 2:
                    conv_taps(j, [tap for tap in range(CONV_W - 1, -1, -1) if tap not in early])
                    dve.wait_ge(evacuated, E_REC + 12 + 3 * j + 3)
                    chain.fence()
                    V.tensor_tensor(conv_y[:], conv_y[:], conv_b[:], ALU.mult).then_inc(conv_ready, 1)

            def mix_split(k, src):
                dve.wait_ge(mixh_ready, k + 1)
                V.tensor_tensor(mix_lo[:, k * S:(k + 1) * S], src, mix_hi[:, k * S:(k + 1) * S].bitcast(F32),
                                ALU.subtract).then_inc(mix_ready, 1)

            def mixer():
                for step in range(1, 36 + 1):
                    if step == 4:
                        dve.wait_ge(consts_loaded, 32)
                        inverse(0)
                    if step < U_WOR:
                        split_lo(step + AHEAD)
                    pu = step - 1
                    if step == 5:
                        dve.wait_ge(rstd_ready, 1)
                    if step == DIAG_STEP:
                        dve.wait_ge(masks_ready, 1)
                        chain.mark(V.memset(hsc[:], 0.0))
                        dve.wait_ge(logf_ready, 1)
                        chain.fence()
                    for ev in events(step - 1):
                        merge(ev)
                    for ev in events(step):
                        if ev >= 2:
                            level_diff(ev - 2)
                    if 4 <= pu < 8:
                        h = pu - 4
                        take(pu, hk[:, h * S:(h + 1) * S])
                    elif 8 <= pu < 12:
                        h = pu - 8
                        take(pu, hq[:, h * S:(h + 1) * S])
                    elif 12 <= pu < 16:
                        h = pu - 12
                        take(pu, hsg[:, h * S:(h + 1) * S])
                    elif 16 <= pu < 28:
                        conv_take((pu - 16) // 3, (pu - 16) % 3, pu)
                    if step == 9:
                        dve.wait_ge(sig_ready, 2)
                        dve.wait_ge(lb_ready, 2)
                        for h in range(HG):
                            blk = slice(h * S, (h + 1) * S)
                            V.tensor_scalar(hp[:, blk], hp[:, blk], one_lb[:, h:h + 1], lb[:, h:h + 1],
                                            ALU.mult, ALU.add).then_inc(f_ready, 1)
                        for h in range(HG):
                            blk = slice(h * S, (h + 1) * S)
                            V.tensor_scalar(hk[:, blk], hk[:, blk], one_lb[:, h:h + 1], None, ALU.mult
                                            ).then_inc(hk_ready, 1)
                    for ev in events(step):
                        if ev >= 2:
                            level_hat(ev - 2)
                    if step < U_WOR:
                        tail(step)
                    if 16 <= pu < 28:
                        conv((pu - 16) // 3, (pu - 16) % 3)
                    for j in range(HG):
                        if step == (20 + 3 * j if j < HG - 1 else 28):
                            mix_split(j, conv_y[:])
                    if step == U_WOR:
                        tail(step)
                        split_lo(step + AHEAD)
                    if step > U_WOR:
                        tiles = (2 * (pu - U_WOR), 2 * (pu - U_WOR) + 1)
                        for n in tiles:
                            residual(n % KT, pu, G[n % 4][:])
                        if tiles[0] >= KT:
                            for n in tiles:
                                norm_tile(1, C_FFN, n - KT)
                        split_lo(step + AHEAD)
                        tail(step)

            def tail(step):
                if step == TAIL:
                    dve.wait_ge(raw_scored, 2 + 2 * LEVELS)
                    chain.fence()
                    pv = hp[:].rearrange("p (m t) -> p m t", t=P)
                    V.tensor_tensor(hat[:].rearrange("p (m t) -> p m t", t=P),
                                    pv[:, :, P - 1:P].broadcast_to(pv.shape), pv, ALU.subtract
                                    ).then_inc(tail_diff, 1)
                if step == TAIL + 1:
                    dve.wait_ge(tail_exp, 2)
                    V.tensor_tensor(hat[:], hat[:], hk[:], ALU.mult).then_inc(khat_ready, 1)
                    V.tensor_tensor(hq[:], hq[:], hp[:], ALU.mult).then_inc(qhat_ready, 1)
                if step == TAIL + 4:
                    dve.wait_ge(kv_ready, 3)
                    dve.wait_ge(state0_ready, 1)
                    for c in (1, 2):
                        if c > 1:
                            chain.fence()
                        for h in range(HG):
                            prev, cur = (c - 1) * S + h * P, c * S + h * P
                            ins = V.scalar_tensor_tensor(
                                out=state[:, cur:cur + P], in0=state[:, prev:prev + P],
                                scalar=hp[:, h * S + c * P + P - 1:h * S + c * P + P],
                                in1=A(c - 1, h * P, P), op0=ALU.mult, op1=ALU.add)
                            if c == 1:
                                chain.mark(ins)
                            else:
                                ins.then_inc(state_ready, 1)
                if step == TAIL + 6:
                    dve.wait_ge(oroot_ready, 1)
                    diagonals(rstd_head, ho_diag[:], HG * TT).then_inc(odiag_ready, 1)
                if step == TAIL + 7:
                    dve.wait_ge(ospread_ready, 1)
                    for h in range(HG):
                        dve.wait_ge(gated_ready, h + 1)
                        V.tensor_tensor(ho[:, h * S:(h + 1) * S], ho_gated[:, h * S:(h + 1) * S], A(h), ALU.mult
                                        ).then_inc(onorm_ready, 1)
                    for h in range(HG):
                        mix_split(HG + h, ho[:, h * S:(h + 1) * S])

            def ffn_in(l):
                inverse(1 + 2 * l)
                dve.wait_ge(rstd_ready, 2 + 2 * l)

                def body(i, last):
                    for s in range(1, 5):
                        u = U_FI[l] + s + AHEAD
                        split_lo(u + 4 * i if last else u, 0 if last else 4 * i)
                        j, k = (s - 1) // 2, FT * l + 2 * i + (s - 1) // 2
                        dve.wait_ge(unit_done, U_FI[l] + 4 * i + s)
                        dst = (gate_t if s % 2 else up_t)[j]
                        V.tensor_tensor(dst[:], G[s - 1][:], rstd[:], ALU.mult).then_inc(evacuated, 1)
                        if s % 2 == 0:
                            dve.wait_ge(evacuated, E_FI[l] + 4 * i + s)
                            dve.wait_ge(silu_ready, k + 1)
                            V.tensor_tensor(dst[:], dst[:], silu_t[j][:], ALU.mult).then_inc(prod_ready, 1)
                            dve.wait_ge(acth_ready, k + 1)
                            tile = ds((2 * i + j) * S, S)
                            V.tensor_tensor(act_lo[:, tile], dst[:], act_hi[:, tile].bitcast(F32), ALU.subtract
                                            ).then_inc(act_ready, 1)

                with dve.Fori(0, FT // 2 - 1) as i:
                    body(i, False)
                body(FT // 2 - 1, True)

            def ffn_out(l):
                def body(i, last):
                    for s in range(1, 9):
                        u = U_FO[l] + s + AHEAD
                        if s % 4 == 0:
                            n = 2 * i + (s // 4 - 1)
                            residual(n, U_FO[l] + 8 * i + s - 1, G[s // 4 - 1][:])
                            if l == 0:
                                norm_tile(2, C_MIX + KT, n)
                        if not last:
                            split_lo(u, 8 * i)
                        elif u + 8 * i < U_END:
                            split_lo(u + 8 * i)

                with dve.Fori(0, KT // 2 - 1) as i:
                    body(i, False)
                body(KT // 2 - 1, True)

            def rope(k, bank, dst, cos, sin, free):
                wait(dve, scored, free)
                dve.wait_ge(swap_ready, 4 * (k + 1))
                chain.mark(V.tensor_tensor(dst[:], G[bank][:], cos[:], ALU.mult))
                chain.mark(V.tensor_tensor(swapped[:], swapped[:], sin[:], ALU.mult))
                chain.fence()
                V.tensor_tensor(dst[:], dst[:], swapped[:], ALU.add).then_inc(evacuated, 1)

            def attend(q, par, pos, tab):
                for n in range(8):
                    t = n // 2
                    w = (t + 1) * P
                    if pos == tab.norm[n]:
                        dve.wait_ge(expd, 8 * q + n + 1)
                        chain.mark(V.reciprocal(recip[:, n:n + 1], denom[:, n:n + 1]))
                        chain.fence()
                        V.tensor_scalar(prob[n % 4][:, 0:w], prob[n % 4][:, 0:w], recip[:, n:n + 1], None, ALU.mult
                                        ).then_inc(normed, 1)
                for n in range(8):
                    t = n // 2
                    w = (t + 1) * P
                    if pos == tab.bias[n]:
                        dve.wait_ge(scored, 8 * q + n + 1)
                        wait(dve, expd, 8 * q + n - 1)
                        V.memset(wait_carrier[:, n:n + 1], 0.0)
                        V.tensor_tensor_reduce(out=s_sb[n % 2][:, 0:w], in0=A(n % 2, 0, w),
                                               in1=bias[:, (TT - 1 - t) * P:], scale=1.0, scalar=3e38,
                                               op0=ALU.add, op1=ALU.min, accum_out=neg_max[:, n:n + 1]
                                               ).then_inc(biased, 1)
                if pos == tab.out:
                    dve.wait_ge(oh_ready, q + 1)
                    V.tensor_tensor(o_lo[:, ds(q * S, S)], G[2][:], o_hi[:, ds(q * S, S)].bitcast(F32),
                                    ALU.subtract).then_inc(o_split, 1)

            def pair(p, ps, shift=0):
                for s in range(16):
                    if s % 8 == 0:
                        split_lo(U_QKV + 8 + ps * 2 + s // 8 + AHEAD, shift)
                    if s == ROPE and ps > 0:
                        rope(2 * p - 1, 1, k_t[(ps + 1) % 2], cos_k, sin_k, 8 * (p - 2))
                    if s == 8 + ROPE:
                        rope(2 * p, 0, q_t[ps % 2], cos_q, sin_q, 8 * (p - 1))
                    if ps > 1:
                        attend(p - 2, ps % 2, s + 16, ATT)
                    if ps > 0:
                        attend(p - 1, (ps + 1) % 2, s, ATT)

            def attention():
                inverse(2)
                for s in range(1, 8):
                    split_lo(U_QKV + s + AHEAD)
                    if s == 3:
                        dve.wait_ge(trig_loaded, 48)
                        dve.wait_ge(rstd_ready, 3)
                        for tab in (cos_k, sin_k):
                            chain.mark(V.tensor_tensor(tab[:], tab[:], rstd[:], ALU.mult))
                        chain.fence()
                        for tab, src in ((cos_q, cos_k), (sin_q, sin_k)):
                            chain.mark(V.tensor_scalar(tab[:], src[:], QSCALE, None, ALU.mult))
                        chain.fence()
                for p in range(PEELED):
                    pair(p, p)
                with dve.Fori(PEELED // 2, PAIRS // 2) as i:
                    chain.loop(i, PEELED // 2, 24)
                    for r in range(2):
                        pair(2 * i + r, PEELED + r, 4 * (i - PEELED // 2))
                chain.done((PAIRS - PEELED) // 2)
                split_lo(U_WOA + AHEAD)
                for s in range(24):
                    if s == ROPE:
                        rope(2 * PAIRS - 1, 1, k_t[1], cos_k, sin_k, 8 * (PAIRS - 2))
                    attend(PAIRS - 2, 0, s + 16, ATT)
                    attend(PAIRS - 1, 1, s, LAST_ATT)
                for s in range(1, 9):
                    residual(s - 1, U_WOA + s - 1, G[WOA_BANK[(s - 1) % 3]][:])
                    norm_tile(3, C_FFN + KT, s - 1)
                    split_lo(U_WOA + s + AHEAD)

            def final_norm():
                inverse(4)
                dve.wait_ge(rstd_ready, 5)
                dve.wait_ge(yh_ready, 5 * KT)
                for n in OUT_DVE:
                    tile = slice(n * S, (n + 1) * S)
                    V.tensor_tensor(y_fin[:, tile], y_fin[:, tile], rstd[:], ALU.mult).then_inc(out_ready, 1)

            prologue()
            mixer()
            ffn_in(0)
            ffn_out(0)
            attention()
            ffn_in(1)
            ffn_out(1)
            final_norm()

        @block.tensor
        def _(pe):
            def mm3(out, stat, mov, first, last):
                pe.matmul(out, stat[0], mov[0], start=first, stop=False)
                pe.matmul(out, stat[0], mov[1], start=False, stop=False)
                return pe.matmul(out, stat[1], mov[0], start=False, stop=last)

            def weight(u, tile, n=P):
                at = (u % RING) * UNIT + tile * P
                return w_hi[:, at:at + n], w_lo[:, at:at + n]

            def tile_of(hi_t, lo_t, k, c0=0, n=S):
                return hi_t[:, k * S + c0:k * S + c0 + n], lo_t[:, k * S + c0:k * S + c0 + n]

            def begin(u):
                pe.wait_ge(lo_ready, u + 1)

            def y_tile(m, k, first):
                if first:
                    pe.wait_ge(y_ready, 8 * m + k + 1)
                return tile_of(y_hi, y_lo, k)

            def mean_square(m, bank):
                last = m == 4
                pe.wait_ge(sq_added, 8 * (m + 1) - last)
                for t in range(TT):
                    ins = pe.matmul(bank[:, t:t + 1], sq_sum[:, t * P:(t + 1) * P], ones_d[:],
                                    start=t == 0 or not last, stop=not last, skip_group_check=True)
                if last:
                    pe.wait_ge(sq_ready, 8 * (m + 1))
                    for t in range(TT):
                        ins = pe.matmul(bank[:, t:t + 1], sq[:, S + t * P:S + (t + 1) * P], ones_d[:], start=False,
                                        stop=t == TT - 1, skip_group_check=True)
                ins.then_inc(ms_ready, 1)

            def spread(m, bank):
                pe.wait_ge(diag_ready, m + 1)
                pe.matmul(bank, ones[:], sq[:, 0:S], start=True, stop=True).then_inc(spread_ready, 1)

            def whole_tile(u, bank, m, first, spread_bank=None):
                for k in range(KT):
                    if spread_bank is not None and k == 3:
                        spread(m, spread_bank)
                    ins = mm3(bank, weight(u, k), y_tile(m, k, first), k == 0, k == KT - 1)
                ins.then_inc(unit_done, 1)

            def token_major(u0, bank_of, m, first):
                for j in range(4):
                    if u0 + j == 0:
                        pe.wait_ge(half_lo, 1)
                    else:
                        begin(u0 + j)
                    for kk in range(2):
                        k = 2 * j + kk
                        if u0 + j == 0 and kk == 1:
                            begin(0)
                        if first:
                            pe.wait_ge(y_ready, 8 * m + k + 1)
                        for t in range(TT):
                            ins = mm3(bank_of(t), tile_of(y_hi, y_lo, k, t * P, P), weight(u0 + j, kk * 4, S),
                                      k == 0, k == KT - 1)
                        if m == 2 and first and k == 4:
                            spread(2, G[2][:])
                    ins.then_inc(unit_done, 1)
                    if m == 2 and first and j == 1:
                        mean_square(2, G[3])

            def score_event(ev):
                a = ev % 2
                wait(pe, merged, ev - 1)
                if ev < 2:
                    if ev == 0:
                        pe.wait_ge(v_ready, TT)
                        pe.wait_ge(evacuated, E_REC + 2 * HG)
                        pe.wait_ge(logf_ready, 1)
                        pe.wait_ge(hk_ready, HG)
                else:
                    L = (ev - 2) // 2
                    done = sum(1 if (x_ - 2) // 2 == 0 else 2 for x_ in range(2, ev + 1))
                    pe.wait_ge(hat_ready, done)
                for m in range(8):
                    c0 = a * 2 * S + m * P
                    if ev < 2:
                        ins = pe.matmul(aux[:, c0:c0 + P], hk[:, c0:c0 + P], hq[:, c0:c0 + P], start=True, stop=True)
                    else:
                        right = lambda t: t[:, c0:c0 + P].rearrange("p (n two h) -> p n two h", two=2, h=1 << L)[:, :, 1, :]
                        ins = pe.matmul(right(aux), hat[:, c0:c0 + P], right(hat), start=True, stop=True)
                ins.then_inc(raw_scored, 1)

            def tail(unit):
                hc = lambda t, h, c: t[:, h * S + c * P:h * S + (c + 1) * P]
                if unit == TAIL + 2:
                    pe.wait_ge(khat_ready, 1)
                    pe.wait_ge(merged, 2 + 2 * LEVELS)
                    for c in range(3):
                        for h in range(HG):
                            ins = pe.transpose(A(c, h * P, P), hc(hat, h, c), ident[:])
                    ins.then_inc(khat_turned, 1)
                if unit == TAIL + 3:
                    pe.wait_ge(khat_copied, 3)
                    for c, bank in enumerate((3, 0, 1)):
                        for h in range(HG):
                            ins = pe.matmul(A(bank, h * P, P), khat_t[:, c * S + h * P:c * S + (h + 1) * P],
                                            hv[:, c * S + h * P:c * S + (h + 1) * P], start=True, stop=True)
                        ins.then_inc(kv_ready, 1)
                if unit == TAIL + 4:
                    pe.wait_ge(state_ready, HG)
                    for h in range(HG):
                        for c in range(TT):
                            ins = pe.matmul(A(h, c * P, P), hv[:, c * S + h * P:c * S + (h + 1) * P],
                                            hc(hsc, h, c), start=True, stop=c == 0)
                            if c:
                                ins = pe.matmul(A(h, c * P, P), state[:, (c - 1) * S + h * P:(c - 1) * S + (h + 1) * P],
                                                hc(hq, h, c), start=False, stop=True)
                        ins.then_inc(o_ready, 1)
                if unit == TAIL + 5:
                    pe.wait_ge(o_taken, 2 * HG)
                    for n in range(HG * TT):
                        ins = pe.matmul(A(0, n, 1), ho_sq[:, n * P:(n + 1) * P], ones_h[:], start=True, stop=True)
                    ins.then_inc(oms_ready, 1)
                if unit == TAIL + 6:
                    pe.wait_ge(odiag_ready, 1)
                    for h in range(HG):
                        ins = pe.matmul(A(h), ones[:], ho_diag[:, h * S:(h + 1) * S], start=True, stop=True)
                    ins.then_inc(ospread_ready, 1)

            def warm_up():
                pe.wait_ge(ones_set, 4)
                for _ in range(WARM_UP):
                    pe.matmul(G[0][:, 0:P], ones[:], ones[:], start=True, stop=True)

            def mixer():
                warm_up()
                token_major(U_REC, A, 0, True)
                mean_square(0, G[3])
                for u in range(4, 28):
                    begin(u)
                    wait(pe, evacuated, E_REC + u - 4 - 4 + 1)
                    if u == 6:
                        pe.wait_ge(rstd_ready, 1)
                    whole_tile(u, G[u % 4][:], 0, False, G[2][:] if u == 4 else None)
                    for ev in events(u):
                        score_event(ev)
                    tail(u)
                for u in range(U_WOR, U_WOR + 8):
                    begin(u)
                    half = (u - U_WOR) // 4
                    for e, ks in ((0, range(3)), (1, range(3)), (0, (3,)), (1, (3,))):
                        n = 2 * (u - U_WOR) + e
                        if 0 in ks:
                            pe.wait_ge(evacuated, E_WOR + n - 4 + 1)
                        for k in ks:
                            pe.wait_ge(mix_ready, 4 * half + k + 1)
                            ins = mm3(G[n % 4][:], weight(u, 4 * e + k), tile_of(mix_hi, mix_lo, 4 * half + k),
                                      k == 0, k == 3)
                    ins.then_inc(unit_done, 1)
                    tail(u)

            def ffn_in(l, bank_free):
                m = 1 + 2 * l

                def body(i, first):
                    for s in range(4):
                        begin(U_FI[l] + 4 * i + s)
                        pe.wait_ge(evacuated, bank_free[s] if first else E_FI[l] + 4 * i + s - 3)
                        whole_tile(U_FI[l] + s, G[s][:], m, first and s == 0, A(2) if first and s == 2 else None)
                        if first and s == 1:
                            mean_square(m, A(3))

                body(0, True)
                with pe.Fori(1, FT // 2) as i:
                    body(i, False)

            def ffn_out(l):
                def body(i, first):
                    for e in range(2):
                        pe.wait_ge(evacuated, E_FO[l] - 3 + e if first else E_FO[l] + 2 * i + e - 1)
                        k = 0
                        for s in range(4):
                            begin(U_FO[l] + 8 * i + 4 * e + s)
                            for tile in range(FO_TILES[s]):
                                if first and e == 0:
                                    pe.wait_ge(act_ready, FT * l + k + 1)
                                ins = mm3(G[e][:], weight(U_FO[l] + s, tile), tile_of(act_hi, act_lo, k),
                                          k == 0, k == FT - 1)
                                k += 1
                            ins.then_inc(unit_done, 1)

                body(0, True)
                with pe.Fori(1, KT // 2) as i:
                    body(i, False)

            def attend(q, par, pos, tab):
                for t in range(TT):
                    if pos == tab.qk[2 * t]:
                        pe.wait_ge(evacuated, 2 * q + (E_QKV + 2))
                        wait(pe, biased, 8 * q + 2 * t)
                        for e in range(2):
                            rows = slice(e * HD, (e + 1) * HD)
                            pe.matmul(A(e, 0, (t + 1) * P), q_t[par][rows, t * P:(t + 1) * P],
                                      k_t[par][rows, 0:(t + 1) * P], start=True, stop=True).then_inc(scored, 1)
                for n in range(8):
                    t = n // 2
                    if pos == tab.turn[n]:
                        pe.wait_ge(normed, 8 * q + n + 1)
                        wait(pe, pt_ready, 8 * q + n - 1)
                        for j in range(t + 1):
                            ins = pe.transpose(A(2 + n % 2, j * P, P), prob[n % 4][:, j * P:(j + 1) * P], ident[:])
                        ins.then_inc(turned, 1)
                if pos == tab.pv:
                    pe.wait_ge(pt_ready, 8 * q + 8)
                    pe.wait_ge(vp_ready, q + 1)
                    wait(pe, o_split, q)
                    for j in range(TT):
                        for e in range(2):
                            ins = pe.matmul(G[2][e * HD:(e + 1) * HD, j * P:],
                                            v_pair[par][:, j * P + e * HD:j * P + (e + 1) * HD],
                                            pt[e][:, j * S + j * P:(j + 1) * S], start=j == 0, stop=j == TT - 1,
                                            skip_group_check=True)
                    ins.then_inc(pv_done, 1)

            def pair(p, ps):
                for s in range(16):
                    k, j = s % 8, s // 8
                    if k == 0:
                        begin(U_QKV + 8 + 2 * p + j)
                        if ps == 0:
                            pe.wait_ge(v_ready, 2 * TT + j + 1)
                        else:
                            pe.wait_ge(evacuated, E_QKV + 2 * p - 1 + j)
                    ins = mm3(G[j][:], weight(U_QKV + 8 + 2 * ps + j, k), tile_of(y_hi, y_lo, k), k == 0, k == KT - 1)
                    if k == KT - 1:
                        ins.then_inc(unit_done, 1)
                    if s == 0 and ps == 1:
                        pe.wait_ge(v_ready, 3 * TT)
                    if ps > 1:
                        attend(p - 2, ps % 2, s + 16, ATT)
                    if ps > 0:
                        attend(p - 1, (ps + 1) % 2, s, ATT)

            def attention():
                token_major(U_QKV, A, 2, True)
                pe.wait_ge(evacuated, E_QKV)
                pe.wait_ge(rstd_ready, 3)
                token_major(U_QKV + 4, lambda t: G[t][:], 2, False)
                for p in range(PEELED):
                    pair(p, p)
                with pe.Fori(PEELED // 2, PAIRS // 2) as i:
                    for r in range(2):
                        pair(2 * i + r, PEELED + r)
                for n in range(3):
                    begin(U_WOA + n)
                pe.wait_ge(evacuated, E_QKV + 2 * PAIRS - 1)
                for s, (k, n) in enumerate(WOA_SLOTS):
                    if n == 0:
                        pe.wait_ge(o_split, k + 1)
                    if (k, n) == (0, 2):
                        pe.wait_ge(evacuated, E_QKV + 2 * PAIRS)
                    ins = mm3(G[WOA_BANK[n]][:], weight(U_WOA + n, k), tile_of(o_hi, o_lo, k), k == 0, k == KT - 1)
                    if k == KT - 1:
                        ins.then_inc(unit_done, 1)
                    attend(PAIRS - 2, 0, s + 16, ATT)
                    attend(PAIRS - 1, 1, s, LAST_ATT)
                for n in range(3, KT):
                    begin(U_WOA + n)
                    pe.wait_ge(evacuated, E_WOA + n - 2)
                    for k in range(KT):
                        ins = mm3(G[WOA_BANK[n % 3]][:], weight(U_WOA + n, k), tile_of(o_hi, o_lo, k), k == 0, k == KT - 1)
                    ins.then_inc(unit_done, 1)

            mixer()
            ffn_in(0, [E_FI[0] - 3 + b for b in range(4)])
            ffn_out(0)
            attention()
            pe.wait_ge(o_split, PAIRS)
            ffn_in(1, [E_FI[1] - 1, E_FI[1] - 2, E_FI[1] - 2, E_FI[1]])
            ffn_out(1)
            mean_square(4, A(3))
            spread(4, A(2))


def blocks(w):
    k, n = w.shape
    return w.reshape(k // P, P, n // P, P).transpose(2, 1, 0, 3).reshape(n // P, P, k)


def token_major_units(w):
    k, n = w.shape
    return (w.reshape(k // (2 * P), 2, P, n // S, S).transpose(3, 0, 2, 1, 4)
            .reshape(n // S * (k // (2 * P)), P, 2 * S))


def constants():
    tq, ks = np.arange(P)[:, None], np.arange(P)[None, :]
    bias = np.empty((P, TT, P), np.float32)
    for col in range(TT):
        rel = (TT - 1 - col) * P + tq - ks
        count = ((rel >= 0) & (rel <= P)).astype(int) + ((rel >= 0) & (rel % 4 == 0)) + ((rel >= 0) & (rel % 16 == 0))
        bias[:, col] = np.where(count > 0, -np.log(np.maximum(count, 1)), 1e30)
    masks = np.zeros((P, LEVELS + 1, P), np.float32)
    s, t = np.arange(P)[:, None], np.arange(P)[None, :]
    for L in range(LEVELS):
        masks[:, L] = (s >> (L + 1) == t >> (L + 1)) & ((s >> L) % 2 == 0) & ((t >> L) % 2 == 1)
    masks[:, LEVELS] = s == t
    half = HD // 2
    freq = (np.float32(10000.0) ** (-np.arange(half, dtype=np.float32) / np.float32(half))).astype(np.float32)
    ang = np.arange(S, dtype=np.float32)[None, :] * freq[np.arange(P) % half][:, None]
    sign = np.where(np.arange(P) % HD < half, -1.0, 1.0)[:, None]
    trig = np.stack([np.cos(ang), np.sin(ang) * sign]).astype(np.float32)
    return bias.reshape(P, TT * P), masks.reshape(P, -1), trig


def kernel(x, mix_norm, ffn_norm, w_in_rec, conv_w, hgrn_lb, hgrn_norm, w_out_rec, w_qkv_attn, w_o_attn,
           w_ffn_in, w_ffn_out, final_norm):
    import concourse.bacc as bacc
    from concourse.bass_utils import run_bass_kernel_spmd

    x, mix_norm, ffn_norm, w_in_rec, conv_w, hgrn_lb, hgrn_norm, w_out_rec, w_qkv_attn, w_o_attn, w_ffn_in, \
        w_ffn_out, final_norm = (np.asarray(a) for a in (
            x, mix_norm, ffn_norm, w_in_rec, conv_w, hgrn_lb, hgrn_norm, w_out_rec, w_qkv_attn, w_o_attn,
            w_ffn_in, w_ffn_out, final_norm))
    bias, masks, trig = constants()
    cols = lambda a: a.reshape(-1, P).T
    params = np.concatenate([cols(mix_norm), cols(ffn_norm), cols(final_norm), cols(conv_w[0]), cols(hgrn_lb),
                             cols(hgrn_norm[0])], axis=1)
    b_, c_, v_, q_, f_, i_, g_ = (w_in_rec[0][:, n * S:(n + 1) * S] for n in range(7))
    b_, c_, v_ = (blocks(w) for w in (b_, c_, v_))
    conv = np.stack([c_, v_, b_], axis=1).reshape(3 * HG, P, UNIT)
    w_rec = np.concatenate([token_major_units(i_), blocks(f_), blocks(q_), blocks(g_), conv])
    w_or = np.concatenate([blocks(w_out_rec[0][h * S:(h + 1) * S]).reshape(4, 2, P, S).transpose(0, 2, 1, 3)
                           .reshape(4, P, UNIT) for h in range(2)])
    q_, k_, v_ = (w_qkv_attn[0][:, n * D:(n + 1) * D] for n in range(3))
    w_qkv = np.concatenate([token_major_units(v_), np.stack([blocks(q_), blocks(k_)], axis=1).reshape(2 * KT, P, UNIT)])
    w_oa = blocks(w_o_attn[0])
    w_fi = [np.stack([blocks(w[:, :FF]), blocks(w[:, FF:])], axis=1).reshape(2 * FT, P, UNIT) for w in w_ffn_in]
    w_fo = []
    for w in w_ffn_out:
        padded = np.zeros((KT, 4, P, max(FO_TILES) * P), w.dtype)
        whole, k0 = blocks(w), 0
        for s, tiles in enumerate(FO_TILES):
            padded[:, s, :, :tiles * P] = whole[:, :, k0 * P:(k0 + tiles) * P]
            k0 += tiles
        w_fo.append(padded.reshape(4 * KT, P, -1))

    arrays = {
        "x_in": x[0].T.reshape(KT, P, S).transpose(1, 0, 2), "params": params, "ident": np.eye(P, dtype=np.float32),
        "score_bias": bias, "level_masks": masks, "trig": trig, "w_rec": w_rec, "w_or": w_or, "w_fi0": w_fi[0],
        "w_fi1": w_fi[1], "w_fo0": w_fo[0], "w_fo1": w_fo[1], "w_qkv": w_qkv, "w_oa": w_oa,
    }
    arrays = {name: np.ascontiguousarray(a) for name, a in arrays.items()}
    nc = bacc.Bacc("TRN2", target_bir_lowering=False, num_devices=1)
    t = {name: nc.dram_tensor(name, a.shape, mybir.dt.from_np(a.dtype), kind="ExternalInput").ap()
         for name, a in arrays.items()}
    out = nc.dram_tensor("out", (KT, P, S), F32, kind="ExternalOutput").ap()
    trunk(nc, t["x_in"], t["params"], t["ident"], t["score_bias"], t["level_masks"], t["trig"], t["w_rec"],
          t["w_or"], [t["w_fi0"], t["w_fi1"]], [t["w_fo0"], t["w_fo1"]], t["w_qkv"], t["w_oa"], out)
    r = run_bass_kernel_spmd(nc, [arrays], core_ids=[0])
    return r.results[0]["out"].reshape(D, S).T[None]
```
